# Optimizing a Trainium2 kernel written in Bass

```python
import jax, jax.numpy as jnp
from jax import lax
import numpy as np

D_MODEL = 1024
BATCH = 1
SEQ = 512
DEPTH = 2

D_FF = 2816
N_SUB = 3
W_A = D_MODEL // 2
W_B = D_MODEL // 2
H_A = 8
DH_A = W_A // H_A
G_B = 8
DG_B = W_B // G_B
CONV_A = 4
CONV_B = 31
LRU_C = 8.0
W_C = D_MODEL
H_C = 8
DH_C = W_C // H_C
CHUNK = 128
EPS = 1e-6


def _rmsnorm(x, g):
    x32 = x.astype(jnp.float32)
    y = x32 * lax.rsqrt(jnp.mean(x32 * x32, axis=-1, keepdims=True) + EPS)
    return (y * g.astype(jnp.float32)).astype(x.dtype)

def _layernorm(x, g, b):
    x32 = x.astype(jnp.float32)
    mu = jnp.mean(x32, axis=-1, keepdims=True)
    var = jnp.mean(jnp.square(x32 - mu), axis=-1, keepdims=True)
    y = (x32 - mu) * lax.rsqrt(var + EPS)
    return (y * g.astype(jnp.float32) + b.astype(jnp.float32)).astype(x.dtype)

def _causal_dwconv(x, w, b):
    k = w.shape[0]
    y = lax.conv_general_dilated(
        x, w[:, None, :].astype(x.dtype), window_strides=(1,), padding=[(k - 1, 0)],
        dimension_numbers=("NWC", "WIO", "NWC"), feature_group_count=x.shape[-1])
    return y + b

def _swiglu(h, w13, w2):
    g, u = jnp.split(h @ w13, 2, axis=-1)
    return (jax.nn.silu(g) * u) @ w2

def _rg_lru(xr, gate_w, gate_b, lam):
    bsz, s, _ = xr.shape
    xh = xr.reshape(bsz, s, H_A, DH_A)
    gates = (jnp.einsum("bshd,hde->bshe", xh, gate_w) + gate_b).astype(jnp.float32)
    r, i = jnp.split(jax.nn.sigmoid(gates), 2, axis=-1)
    r = r.reshape(bsz, s, W_A)
    i = i.reshape(bsz, s, W_A)
    log_a = LRU_C * r * jax.nn.log_sigmoid(lam.astype(jnp.float32))
    a = jnp.exp(log_a)
    u = jnp.sqrt(-jnp.expm1(2.0 * log_a)) * (i * xr.astype(jnp.float32))

    def combine(left, right):
        a1, b1 = left
        a2, b2 = right
        return a1 * a2, a2 * b1 + b2

    _, h = lax.associative_scan(combine, (a, u), axis=1)
    return h.astype(xr.dtype)

def _mixer_ab(h, w_in, a_conv_w, a_conv_b, a_gate_w, a_gate_b, a_lam,
              b_conv_w, b_conv_b, b_norm_g, b_norm_b, w_out):
    z = h @ w_in
    a_gate, a_x, b_val, b_gate = jnp.split(z, [W_A, 2 * W_A, 2 * W_A + W_B], axis=-1)
    a_x = _causal_dwconv(a_x, a_conv_w, a_conv_b)
    y_a = _rg_lru(a_x, a_gate_w, a_gate_b, a_lam) * jax.nn.gelu(a_gate)
    v = b_val * jax.nn.sigmoid(b_gate)
    v = _causal_dwconv(v, b_conv_w, b_conv_b)
    bsz, s, _ = v.shape
    v = _layernorm(v.reshape(bsz, s, G_B, DG_B), b_norm_g.reshape(G_B, DG_B),
                   b_norm_b.reshape(G_B, DG_B)).reshape(bsz, s, W_B)
    y_b = jax.nn.silu(v)
    return jnp.concatenate([y_a, y_b], axis=-1) @ w_out

def _mixer_c(h, w_in, b_in, norm_g, norm_b, w_s, b_s, w_out):
    z = jax.nn.gelu(h @ w_in + b_in)
    u, v = jnp.split(z, 2, axis=-1)
    v = _layernorm(v, norm_g, norm_b)
    bsz, s, _ = v.shape
    vc = v.reshape(bsz, s // CHUNK, CHUNK, H_C, DH_C)
    mask = jnp.tril(jnp.ones((CHUNK, CHUNK), dtype=bool))
    ws = jnp.where(mask, w_s, jnp.zeros_like(w_s)).astype(v.dtype)
    mixed = jnp.einsum("hts,bnshd->bnthd", ws, vc) + jnp.transpose(b_s)[:, :, None]
    return (u * mixed.reshape(bsz, s, W_C)) @ w_out

def _sublayer(x, fn, pre_g, post_g, shift, scale, gate, res_w):
    h = _rmsnorm(x, pre_g) * (1.0 + scale[:, None, :]) + shift[:, None, :]
    y = _rmsnorm(fn(h), post_g)
    return x + res_w * (1.0 + gate[:, None, :]) * y

def first_inputs(seed: int = 0) -> dict:
    key = jax.random.key(seed)
    ks = jax.random.split(key, 32)
    ne = (DEPTH + 1) // 2
    no = DEPTH // 2
    f32 = jnp.float32

    def nrm(k, shape, scale):
        return jax.random.normal(k, shape, f32) * scale

    u_lam = jax.random.uniform(ks[14], (ne, W_A), f32, minval=0.9, maxval=0.999)
    sa = u_lam ** (1.0 / LRU_C)
    a_lam = jnp.log(sa) - jnp.log1p(-sa)
    return {
        "x": nrm(ks[0], (BATCH, SEQ, D_MODEL), 1.0),
        "c": nrm(ks[1], (BATCH, D_MODEL), 1.0),
        "ada_w": nrm(ks[2], (DEPTH, D_MODEL, N_SUB * 3 * D_MODEL), 0.1 * D_MODEL ** -0.5),
        "ada_b": nrm(ks[3], (DEPTH, N_SUB * 3 * D_MODEL), 0.01),
        "norm_pre": 1.0 + nrm(ks[4], (DEPTH, N_SUB, D_MODEL), 0.02),
        "norm_post": 1.0 + nrm(ks[5], (DEPTH, N_SUB, D_MODEL), 0.02),
        "ffn_w13": nrm(ks[6], (DEPTH, 2, D_MODEL, 2 * D_FF), D_MODEL ** -0.5),
        "ffn_w2": nrm(ks[7], (DEPTH, 2, D_FF, D_MODEL), D_FF ** -0.5),
        "ab_w_in": nrm(ks[8], (ne, D_MODEL, 2 * W_A + 2 * W_B), D_MODEL ** -0.5),
        "a_conv_w": nrm(ks[9], (ne, CONV_A, W_A), CONV_A ** -0.5),
        "a_conv_b": nrm(ks[10], (ne, W_A), 0.01),
        "a_gate_w": nrm(ks[11], (ne, H_A, DH_A, 2 * DH_A), DH_A ** -0.5),
        "a_gate_b": nrm(ks[12], (ne, H_A, 2 * DH_A), 0.01),
        "a_lam": a_lam,
        "b_conv_w": nrm(ks[15], (ne, CONV_B, W_B), CONV_B ** -0.5),
        "b_conv_b": nrm(ks[16], (ne, W_B), 0.01),
        "b_norm_g": 1.0 + nrm(ks[17], (ne, W_B), 0.02),
        "b_norm_b": nrm(ks[18], (ne, W_B), 0.01),
        "ab_w_out": nrm(ks[19], (ne, W_A + W_B, D_MODEL), (W_A + W_B) ** -0.5),
        "c_w_in": nrm(ks[20], (no, D_MODEL, 2 * W_C), D_MODEL ** -0.5),
        "c_b_in": nrm(ks[21], (no, 2 * W_C), 0.01),
        "c_norm_g": 1.0 + nrm(ks[22], (no, W_C), 0.02),
        "c_norm_b": nrm(ks[23], (no, W_C), 0.01),
        "c_w_s": nrm(ks[24], (no, H_C, CHUNK, CHUNK), 0.5 * CHUNK ** -0.5),
        "c_b_s": 1.0 + nrm(ks[25], (no, H_C, CHUNK), 0.01),
        "c_w_out": nrm(ks[26], (no, W_C, D_MODEL), W_C ** -0.5),
    }

def first_block(x, c, ada_w, ada_b, norm_pre, norm_post, ffn_w13, ffn_w2,
              ab_w_in, a_conv_w, a_conv_b, a_gate_w, a_gate_b, a_lam,
              b_conv_w, b_conv_b, b_norm_g, b_norm_b, ab_w_out,
              c_w_in, c_b_in, c_norm_g, c_norm_b, c_w_s, c_b_s, c_w_out):
    bsz = x.shape[0]
    c_act = jax.nn.silu(c)
    for l in range(DEPTH):
        mod = (c_act @ ada_w[l] + ada_b[l]).reshape(bsz, N_SUB, 3, D_MODEL)

        def ffn_pre(h, l=l):
            return _swiglu(h, ffn_w13[l, 0], ffn_w2[l, 0])

        def ffn_post(h, l=l):
            return _swiglu(h, ffn_w13[l, 1], ffn_w2[l, 1])

        if l % 2 == 0:
            k = l // 2

            def mixer(h, k=k):
                return _mixer_ab(h, ab_w_in[k], a_conv_w[k], a_conv_b[k], a_gate_w[k],
                                 a_gate_b[k], a_lam[k], b_conv_w[k], b_conv_b[k],
                                 b_norm_g[k], b_norm_b[k], ab_w_out[k])
        else:
            k = l // 2

            def mixer(h, k=k):
                return _mixer_c(h, c_w_in[k], c_b_in[k], c_norm_g[k], c_norm_b[k],
                                c_w_s[k], c_b_s[k], c_w_out[k])

        x = _sublayer(x, ffn_pre, norm_pre[l, 0], norm_post[l, 0],
                      mod[:, 0, 0], mod[:, 0, 1], mod[:, 0, 2], 0.5)
        x = _sublayer(x, mixer, norm_pre[l, 1], norm_post[l, 1],
                      mod[:, 1, 0], mod[:, 1, 1], mod[:, 1, 2], 1.0)
        x = _sublayer(x, ffn_post, norm_pre[l, 2], norm_post[l, 2],
                      mod[:, 2, 0], mod[:, 2, 1], mod[:, 2, 2], 0.5)
    return x


_first_inputs = first_inputs


def first_inputs(seed=0):
    import zlib

    import numpy as np

    out = dict(_first_inputs(seed))
    spreads = {}
    factors = {'a_gate_b': 8.0,
     'b_conv_b': 4.167,
     'b_norm_g': 3.912,
     'b_norm_b': 8.0,
     'c_b_in': 8.0,
     'c_norm_g': 8.0,
     'c_norm_b': 8.0,
     'c_b_s': 8.0}
    for name, (base, spread) in spreads.items():
        noise = np.random.default_rng([zlib.crc32(name.encode()), seed]).standard_normal(out[name].shape)
        drawn = base * np.exp(spread * noise) if base else spread * noise
        out[name] = __import__('jax').numpy.asarray(drawn.astype(out[name].dtype))
    for name, factor in factors.items():
        out[name] = (out[name] * factor).astype(out[name].dtype)
    return out


_narrow_inputs = first_inputs


def first_inputs(seed=0):

    out = dict(_narrow_inputs(seed))
    wider = {'a_conv_b': 7.28,
     'a_gate_b': 12.0,
     'b_norm_g': 4.16,
     'b_norm_b': 4.18,
     'c_norm_g': 12.0,
     'c_norm_b': 12.0,
     'c_b_s': 12.0}
    for name, times in wider.items():
        mean = out[name].mean()
        out[name] = (mean + times * (out[name] - mean)).astype(out[name].dtype)
    return out


GRID_W = 64
CTX_LEN = 256
N_EVEN = (DEPTH + 1) // 2
N_ODD = DEPTH // 2

RWKV_HEAD = 64
RWKV_HEADS = (3 * D_MODEL // 4) // RWKV_HEAD
RWKV_W = RWKV_HEADS * RWKV_HEAD
LORA_W = 64
LORA_A = 64
FOUR_GROUPS = 4
FOUR_W = D_MODEL - RWKV_W
FOUR_GROUP_W = FOUR_W // FOUR_GROUPS
MIX_W = RWKV_W + FOUR_W
N_SHIFT = 3 * RWKV_W + 2 * LORA_W + 2 * LORA_A
EVEN_IN = N_SHIFT + RWKV_W + 2 * FOUR_W
RWKV_GN_EPS = 64e-5

RET_HEADS = 8
RET_HEAD = D_MODEL // RET_HEADS
RET_W = RET_HEADS * RET_HEAD
ODD_IN = 4 * RET_W
RET_CHUNK = 128
ROPE_BASE = 10000.0


def rmsnorm(x, g):
    xf = x.astype(jnp.float32)
    y = xf * lax.rsqrt(jnp.mean(xf * xf, axis=-1, keepdims=True) + EPS)
    return (y * g.astype(jnp.float32)).astype(x.dtype)

def qshift(u, rows):
    b, l, ch = u.shape
    g = u.reshape(b, rows, GRID_W, ch // 4, 4)
    left = jnp.pad(g[:, :, :-1, :, 0], ((0, 0), (0, 0), (1, 0), (0, 0)))
    right = jnp.pad(g[:, :, 1:, :, 1], ((0, 0), (0, 0), (0, 1), (0, 0)))
    up = jnp.pad(g[:, :-1, :, :, 2], ((0, 0), (1, 0), (0, 0), (0, 0)))
    down = jnp.pad(g[:, 1:, :, :, 3], ((0, 0), (0, 1), (0, 0), (0, 0)))
    return jnp.stack([left, right, up, down], axis=-1).reshape(b, l, ch)

def bishift(u):
    b, l, ch = u.shape
    g = u.reshape(b, l, ch // 2, 2)
    prev = jnp.pad(g[:, :-1, :, 0], ((0, 0), (1, 0), (0, 0)))
    nxt = jnp.pad(g[:, 1:, :, 1], ((0, 0), (0, 1), (0, 0)))
    return jnp.stack([prev, nxt], axis=-1).reshape(b, l, ch)

def rwkv_dir_terms(r, k0, v, wl, al, w0, w2, a0, a2, k_k, k_a, r_k):
    b, l, _ = r.shape
    hs = lambda t: t.reshape(b, l, RWKV_HEADS, RWKV_HEAD)
    w_log = -jax.nn.softplus(-(w0 + jnp.tanh(wl) @ w2)) - 0.5
    decay = jnp.exp(-jnp.exp(w_log))
    a = jax.nn.sigmoid(a0 + al @ a2)
    kk = hs(k0 * k_k)
    kk = kk / jnp.maximum(jnp.sqrt(jnp.sum(kk * kk, axis=-1, keepdims=True)), 1e-12)
    k = hs(k0 * (1.0 + (a - 1.0) * k_a))
    rh, vh = hs(r), hs(v)
    bonus = jnp.sum(rh * k * r_k, axis=-1, keepdims=True) * vh
    return rh, hs(decay), k, vh, kk, kk * hs(a), bonus

def rwkv7_scan(r, w, k, v, kk, bb, s0, reverse):
    def step(s, inp):
        r_t, w_t, k_t, v_t, kk_t, b_t = inp
        sa = jnp.einsum('bhij,bhj->bhi', s, kk_t)
        s = s * w_t[:, :, None, :] - sa[..., None] * b_t[:, :, None, :] + v_t[..., None] * k_t[:, :, None, :]
        return s, jnp.einsum('bhij,bhj->bhi', s, r_t)
    xs = tuple(jnp.moveaxis(t, 1, 0) for t in (r, w, k, v, kk, bb))
    s, ys = lax.scan(step, s0, xs, reverse=reverse)
    return s, jnp.moveaxis(ys, 0, 1)

def fourier_mix(u):
    b, l, _ = u.shape
    g = u.astype(jnp.float32).reshape(b, l, FOUR_GROUPS, FOUR_GROUP_W)
    f = jnp.fft.fft2(g, axes=(1, 3), norm='ortho').real
    return f.reshape(b, l, FOUR_W).astype(u.dtype)

def even_mixer(hc, hl, rows, w_in, mu, w0, w2, a0, a2, k_k, k_a, r_k, lnx_g, lnx_b, w_out, need_ctx):
    cuts = np.cumsum([RWKV_W, RWKV_W, RWKV_W, LORA_W, LORA_W, LORA_A]).tolist()

    def proj(h, shift_fn):
        u = h @ w_in
        s, gate_r, four, gate_f = jnp.split(u, [N_SHIFT, N_SHIFT + RWKV_W, N_SHIFT + RWKV_W + FOUR_W], axis=-1)
        s = (s + (shift_fn(s) - s) * mu).astype(jnp.float32)
        r, k0, v, wl_f, wl_b, al_f, al_b = jnp.split(s, cuts, axis=-1)
        return r, k0, v, (wl_f, wl_b), (al_f, al_b), gate_r, four, gate_f

    pc = proj(hc, bishift)
    pl = proj(hl, lambda t: qshift(t, rows))
    bsz = hl.shape[0]
    zeros = jnp.zeros((bsz, RWKV_HEADS, RWKV_HEAD, RWKV_HEAD), jnp.float32)
    oc, ol = 0.0, 0.0
    for d in range(2):
        tc = rwkv_dir_terms(pc[0], pc[1], pc[2], pc[3][d], pc[4][d], w0[d], w2[d], a0[d], a2[d], k_k, k_a, r_k)
        tl = rwkv_dir_terms(pl[0], pl[1], pl[2], pl[3][d], pl[4][d], w0[d], w2[d], a0[d], a2[d], k_k, k_a, r_k)
        s_ctx, yc = rwkv7_scan(*tc[:6], zeros, d == 1)
        _, yl = rwkv7_scan(*tl[:6], s_ctx, d == 1)
        oc = oc + yc + tc[6]
        ol = ol + yl + tl[6]

    def finish(o, gate_r, four, gate_f):
        b, l = o.shape[:2]
        mean = jnp.mean(o, axis=-1, keepdims=True)
        var = jnp.mean(jnp.square(o - mean), axis=-1, keepdims=True)
        o = ((o - mean) * lax.rsqrt(var + RWKV_GN_EPS)).reshape(b, l, RWKV_W) * lnx_g + lnx_b
        yr = o.astype(gate_r.dtype) * jax.nn.silu(gate_r)
        yf = fourier_mix(four) * jax.nn.silu(gate_f)
        return jnp.concatenate([yr, yf], axis=-1) @ w_out

    out_l = finish(ol, pl[5], pl[6], pl[7])
    out_c = finish(oc, pc[5], pc[6], pc[7]) if need_ctx else None
    return out_c, out_l

def axial_rope(t):
    l = t.shape[1]
    pos = jnp.arange(l)
    rc = jnp.stack([pos // GRID_W, pos % GRID_W], axis=-1).astype(jnp.float32)
    half = RET_HEAD // 2
    inv = ROPE_BASE ** (-jnp.arange(0, half, 2, dtype=jnp.float32) / half)
    ang = (rc[:, :, None] * inv).reshape(l, half)[:, None, :]
    cos, sin = jnp.cos(ang), jnp.sin(ang)
    t1, t2 = t[..., :half], t[..., half:]
    return jnp.concatenate([t1 * cos - t2 * sin, t1 * sin + t2 * cos], axis=-1)

def retention_scan(q, k, v, log_gamma, r0, strict):
    bsz, l, h, dk = q.shape
    dv = v.shape[-1]
    n_chunks = l // RET_CHUNK
    pos = jnp.arange(RET_CHUNK, dtype=jnp.float32)
    diff = pos[:, None] - pos[None, :]
    mask = diff > 0 if strict else diff >= 0
    dmat = jnp.where(mask[None], jnp.exp(jnp.where(mask, diff, 0.0)[None] * log_gamma[:, None, None]), 0.0)
    xi = jnp.exp((pos[:, None] + 1.0) * log_gamma[None, :])
    zeta = jnp.exp((RET_CHUNK - 1.0 - pos[:, None]) * log_gamma[None, :])
    g_chunk = jnp.exp(RET_CHUNK * log_gamma)

    def chunk(r, inp):
        qc, kc, vc = inp
        sc = jnp.einsum('bihd,bjhd->bhij', qc, kc) * dmat
        inner = jnp.einsum('bhij,bjhe->bihe', sc, vc)
        cross = jnp.einsum('bihd,bhde->bihe', qc, r) * xi[None, :, :, None]
        r = r * g_chunk[None, :, None, None] + jnp.einsum('bjhd,bjhe->bhde', kc * zeta[None, :, :, None], vc)
        return r, inner + cross

    to_chunks = lambda t: jnp.moveaxis(t.reshape(bsz, n_chunks, RET_CHUNK, h, t.shape[-1]), 1, 0)
    r, o = lax.scan(chunk, r0, (to_chunks(q), to_chunks(k), to_chunks(v)))
    return r, jnp.moveaxis(o, 0, 1).reshape(bsz, l, h, dv)

def odd_mixer(hc, hl, w_in, decay_logit, w_out, need_ctx):
    bsz = hl.shape[0]

    def proj(h, rope):
        u = h @ w_in
        q, k, v, g = jnp.split(u, 4, axis=-1)
        l = h.shape[1]
        hs = lambda t: t.astype(jnp.float32).reshape(bsz, l, RET_HEADS, RET_HEAD)
        q, k, v = hs(q), hs(k) * (RET_HEAD ** -0.5), hs(v)
        if rope:
            q, k = axial_rope(q), axial_rope(k)
        return q, k, v, g

    qc, kc, vc, gc = proj(hc, False)
    ql, kl, vl, gl = proj(hl, True)
    lg = jax.nn.log_sigmoid(decay_logit.astype(jnp.float32))
    zeros = jnp.zeros((bsz, RET_HEADS, RET_HEAD, RET_HEAD), jnp.float32)
    flip = lambda t: jnp.flip(t, axis=1)
    rc_f, oc_f = retention_scan(qc, kc, vc, lg[0], zeros, False)
    _, ol_f = retention_scan(ql, kl, vl, lg[0], rc_f, False)
    rc_b, oc_b = retention_scan(flip(qc), flip(kc), flip(vc), lg[1], zeros, True)
    _, ol_b = retention_scan(flip(ql), flip(kl), flip(vl), lg[1], rc_b, True)

    def finish(of, ob, g):
        o = of + flip(ob)
        o = o * lax.rsqrt(jnp.mean(o * o, axis=-1, keepdims=True) + EPS)
        o = o.reshape(o.shape[0], o.shape[1], RET_W).astype(g.dtype)
        return (o * jax.nn.silu(g)) @ w_out

    out_l = finish(ol_f, ol_b, gl)
    out_c = finish(oc_f, oc_b, gc) if need_ctx else None
    return out_c, out_l

def second_inputs(seed: int = 0) -> dict:
    key = jax.random.key(seed)
    ks = jax.random.split(key, 24)
    f32 = jnp.float32
    nrm = lambda k, shape, s: jax.random.normal(k, shape, f32) * s
    D = D_MODEL
    gam = 1.0 - 2.0 ** (-5.0 - jnp.arange(RET_HEADS, dtype=f32))
    return {
        'x': nrm(ks[0], (BATCH, SEQ, D), 1.0),
        'c': nrm(ks[1], (BATCH, D), 1.0),
        'ctx': nrm(ks[2], (BATCH, CTX_LEN, D), 1.0),
        'c_ctx': nrm(ks[3], (D,), 1.0),
        'ada_w': nrm(ks[4], (DEPTH, D, 3 * D), D ** -0.5),
        'ada_b': nrm(ks[5], (DEPTH, 3 * D), 0.02),
        'norm_pre': 1.0 + nrm(ks[6], (DEPTH, D), 0.05),
        'norm_post': 1.0 + nrm(ks[7], (DEPTH, D), 0.05),
        'ev_w_in': nrm(ks[8], (N_EVEN, D, EVEN_IN), D ** -0.5),
        'ev_mu': jax.random.uniform(ks[9], (N_EVEN, N_SHIFT), f32),
        'ev_w0': jax.random.uniform(ks[10], (N_EVEN, 2, RWKV_W), f32, -4.0, 0.5),
        'ev_w2': nrm(ks[11], (N_EVEN, 2, LORA_W, RWKV_W), 0.1 * LORA_W ** -0.5),
        'ev_a0': nrm(ks[12], (N_EVEN, 2, RWKV_W), 0.5),
        'ev_a2': nrm(ks[13], (N_EVEN, 2, LORA_A, RWKV_W), 0.1 * LORA_A ** -0.5),
        'ev_k_k': 0.85 + nrm(ks[14], (N_EVEN, RWKV_W), 0.05),
        'ev_k_a': 1.0 + nrm(ks[15], (N_EVEN, RWKV_W), 0.05),
        'ev_r_k': nrm(ks[16], (N_EVEN, RWKV_HEADS, RWKV_HEAD), 0.1),
        'ev_lnx_g': 1.0 + nrm(ks[17], (N_EVEN, RWKV_W), 0.05),
        'ev_lnx_b': nrm(ks[18], (N_EVEN, RWKV_W), 0.02),
        'ev_w_out': nrm(ks[19], (N_EVEN, MIX_W, D), MIX_W ** -0.5),
        'od_w_in': nrm(ks[20], (N_ODD, D, ODD_IN), D ** -0.5),
        'od_decay_logit': (jnp.log(gam) - jnp.log1p(-gam)) + nrm(ks[21], (N_ODD, 2, RET_HEADS), 0.1),
        'od_w_out': nrm(ks[22], (N_ODD, RET_W, D), RET_W ** -0.5),
    }

def second_block(x, c, ctx, c_ctx, ada_w, ada_b, norm_pre, norm_post, ev_w_in, ev_mu, ev_w0, ev_w2, ev_a0, ev_a2,
              ev_k_k, ev_k_a, ev_r_k, ev_lnx_g, ev_lnx_b, ev_w_out, od_w_in, od_decay_logit, od_w_out):
    rows = x.shape[1] // GRID_W
    xl, xc = x, ctx
    sc, scc = jax.nn.silu(c), jax.nn.silu(c_ctx)
    for layer in range(DEPTH):
        need_ctx = layer < DEPTH - 1
        shift_l, scale_l, gate_l = jnp.split(sc @ ada_w[layer] + ada_b[layer], 3, axis=-1)
        shift_c, scale_c, gate_c = jnp.split(scc @ ada_w[layer] + ada_b[layer], 3, axis=-1)
        hl = rmsnorm(xl, norm_pre[layer]) * (1.0 + scale_l[:, None, :]) + shift_l[:, None, :]
        hc = rmsnorm(xc, norm_pre[layer]) * (1.0 + scale_c) + shift_c
        if layer % 2 == 0:
            i = layer // 2
            oc, ol = even_mixer(hc, hl, rows, ev_w_in[i], ev_mu[i], ev_w0[i], ev_w2[i], ev_a0[i], ev_a2[i],
                                ev_k_k[i], ev_k_a[i], ev_r_k[i], ev_lnx_g[i], ev_lnx_b[i], ev_w_out[i], need_ctx)
        else:
            i = layer // 2
            oc, ol = odd_mixer(hc, hl, od_w_in[i], od_decay_logit[i], od_w_out[i], need_ctx)
        xl = xl + gate_l[:, None, :] * rmsnorm(ol, norm_post[layer])
        if need_ctx:
            xc = xc + gate_c * rmsnorm(oc, norm_post[layer])
    return xl


def setup_inputs(seed=0):
    out = dict(first_inputs(seed))
    for name, value in second_inputs(seed + 1).items():
        if name != "x":
            out[name + "_2"] = value
    return out


def reference(
    x, c, ada_w, ada_b, norm_pre, norm_post, ffn_w13, ffn_w2, ab_w_in, a_conv_w, a_conv_b,
    a_gate_w, a_gate_b, a_lam, b_conv_w, b_conv_b, b_norm_g, b_norm_b, ab_w_out, c_w_in, c_b_in,
    c_norm_g, c_norm_b, c_w_s, c_b_s, c_w_out, c_2, ctx_2, c_ctx_2, ada_w_2, ada_b_2,
    norm_pre_2, norm_post_2, ev_w_in_2, ev_mu_2, ev_w0_2, ev_w2_2, ev_a0_2, ev_a2_2, ev_k_k_2,
    ev_k_a_2, ev_r_k_2, ev_lnx_g_2, ev_lnx_b_2, ev_w_out_2, od_w_in_2, od_decay_logit_2,
    od_w_out_2,
):
    x = first_block(
        x, c, ada_w, ada_b, norm_pre, norm_post, ffn_w13, ffn_w2, ab_w_in, a_conv_w, a_conv_b,
        a_gate_w, a_gate_b, a_lam, b_conv_w, b_conv_b, b_norm_g, b_norm_b, ab_w_out, c_w_in,
        c_b_in, c_norm_g, c_norm_b, c_w_s, c_b_s, c_w_out,
    )
    return second_block(
        x, c_2, ctx_2, c_ctx_2, ada_w_2, ada_b_2, norm_pre_2, norm_post_2, ev_w_in_2, ev_mu_2,
        ev_w0_2, ev_w2_2, ev_a0_2, ev_a2_2, ev_k_k_2, ev_k_a_2, ev_r_k_2, ev_lnx_g_2,
        ev_lnx_b_2, ev_w_out_2, od_w_in_2, od_decay_logit_2, od_w_out_2,
    )


_drawn_inputs = setup_inputs


def setup_inputs(seed=0):
    import zlib

    import numpy as np

    out = dict(_drawn_inputs(seed))
    spreads = {}
    factors = {'ev_w2_2': 7.648,
     'ev_a2_2': 4.03,
     'ev_r_k_2': 3.781,
     'ev_lnx_g_2': 11.574,
     'ev_lnx_b_2': 28.88,
     'norm_post_2': 2.675}
    for name, (base, spread) in spreads.items():
        noise = np.random.default_rng([zlib.crc32(name.encode()), seed]).standard_normal(out[name].shape)
        drawn = base * np.exp(spread * noise) if base else spread * noise
        out[name] = __import__('jax').numpy.asarray(drawn.astype(out[name].dtype))
    for name, factor in factors.items():
        out[name] = (out[name] * factor).astype(out[name].dtype)
    return out
```

```python
from contextlib import ExitStack, contextmanager

import numpy as np

import concourse.bass as bass
from concourse import mybir

F32 = mybir.dt.float32
F32R = mybir.dt.float32r
ALU = mybir.AluOpType
ACT = mybir.ActivationFunctionType
AX = mybir.AxisListType

P = 128
D = 1024
DB = D // P
SEQ = 512
CTX = 256
TOK = SEQ + CTX
LAT, CON = slice(0, SEQ), slice(SEQ, TOK)
D_FF = 2816
FB = D_FF // P
EPS = 1e-6
GN_EPS = 64e-5
NS = 3
GRID = 64
RW = 768
RB = RW // P
DECAY = float(np.exp(-0.5))
CH = 128
RAW = 4
SPLIT = 2
ADA = 1
ADA_W = 256
FIRST_ADA = 10
HI, LO = 0, 1
PASSES = ((HI, HI), (HI, LO), (LO, HI))



class Names:

    def __init__(self, **values):
        self.values = values

    def __getattr__(self, name):
        return self.values[name]


def loop(eng, lo, hi, step, body):
    turns = (hi - lo) // step
    if turns >= 2:
        with eng.Fori(0, turns) as t:
            for u in range(step):
                body(t * step + (lo + u), lo + u)
        lo += turns * step
    for i in range(lo, hi):
        body(i, i)


def at(i, n):
    return bass.ds(i, n)


class Steps:

    def __init__(self, eng, sem, base=0):
        self.eng, self.sem, self.base, self.n = eng, sem, base, 0

    def __call__(self, ins):
        self.n += 1
        ins.then_inc(self.sem, 1)
        self.eng.wait_ge(self.sem, self.base + self.n)


PARAM_PAGES = [
    [("ada_b0", 72), ("norm_pre", 48), ("c", 8)],
    [("ada_b1", 72), ("norm_post", 48), ("c_2", 8)],
    [("b_conv_w", 124), ("a_lam", 4)],
    [("a_conv_b", 4), ("a_conv_w", 16), ("b_conv_b", 4), ("b_norm_g", 4), ("b_norm_b", 4),
     ("gate_br", 4), ("gate_bi", 4), ("c_b_in", 16), ("c_norm_g", 8), ("c_norm_b", 8), ("c_ctx", 8),
     ("norm_pre_2", 16), ("norm_post_2", 16), ("k_k", 6), ("k_a", 6)],
    [("ada_b_2", 48), ("mu", 20), ("w0", 12), ("a0", 12), ("r_k", 6), ("lnx_g", 6), ("lnx_b", 6)],
]
PARAM_AT = {}
for _page, _rows in enumerate(PARAM_PAGES):
    _r = 0
    for _name, _n in _rows:
        PARAM_AT[_name] = _page * P + _r
        _r += _n
    assert _r <= P

CONST_COLS = {"ident": (0, 128), "ones": (128, 128), "bd64": (256, 128), "shift4": (384, 4),
              "shift2": (388, 2), "pos": (390, 1), "rpos": (391, 1)}
CONST_W = 392


def constants():
    i = np.arange(P)
    c = np.zeros((P, CONST_W), np.float32)
    c[:, 0:128] = np.eye(P)
    c[:, 128:256] = 1.0
    c[:, 256:384] = (i[:, None] // 64) == (i[None, :] // 64)
    c[:, 384:388] = (i[:, None] % 4) == np.arange(4)[None, :]
    c[:, 388:390] = (i[:, None] % 2) == np.arange(2)[None, :]
    c[:, 390] = i
    c[:, 391] = P - 1 - i
    su = (i[:, None] < i[None, :]).astype(np.float32)
    iu = (i[:, None] <= i[None, :]).astype(np.float32)
    masks = np.stack([su, iu, su.T, iu.T]).astype(np.float32)
    levels = []
    for n in (1, 2, 4, 8, 16, 32, 64):
        same = (i[:, None] // (2 * n)) == (i[None, :] // (2 * n))
        m = same & ((i[:, None] // n) % 2 == 1) & ((i[None, :] // n) % 2 == 0)
        levels += [m, m.T]
    levels = np.stack(levels).astype(np.float32)
    dist = np.abs(i[:, None] - i[None, :]).astype(np.float32)
    def dft(n):
        a = 2 * np.pi * np.outer(np.arange(n), np.arange(n)) / n
        return np.cos(a), np.sin(a)
    c64, s64 = dft(64)
    feat = np.zeros((P, 256))
    for g in range(2):
        feat[64 * g:64 * g + 64, 64 * g:64 * g + 64] = c64
        feat[64 * g:64 * g + 64, 128 + 64 * g:128 + 64 * g + 64] = s64
    time = []
    for n in (CTX, SEQ):
        cn, sn = dft(n)
        time.append((np.stack([cn, -sn]) / np.sqrt(n * 64.0)).astype(np.float32))
    half = 64
    tok = np.arange(SEQ)
    rc = np.stack([tok // GRID, tok % GRID], -1).astype(np.float32)
    inv = (np.float32(10000.0) ** (-np.arange(0, half, 2, dtype=np.float32) / half)).astype(np.float32)
    ang = (rc[:, :, None] * inv).astype(np.float32).reshape(SEQ, half).T
    cos, sin = np.cos(ang), np.sin(ang)
    rope = np.stack([np.concatenate([cos, cos]), np.concatenate([sin, sin])]).astype(np.float32)
    rot = np.zeros((P, P), np.float32)
    for d in range(half):
        rot[half + d, d] = -1.0
        rot[d, half + d] = 1.0
    posrow = np.stack([np.broadcast_to(i + 1.0, (P, P)), np.broadcast_to(P - i + 0.0, (P, P))])
    goes = np.ones((2, P, TOK), np.float32)
    goes[0, :, ::CH] = 0
    goes[1, :, CH - 1::CH] = 0
    return {
        "const": c, "masks": masks, "levels": levels, "dist": dist,
        "dft_feat": feat.astype(np.float32), "dft_ctx": time[0], "dft_lat": time[1],
        "rope": rope, "rot": rot, "posrow": posrow.astype(np.float32), "goes": goes,
    }



class Weights:

    def __init__(self):
        self.phases, self.total = [], 0

    def add(self, *segments):
        phase, n = [], self.total
        ada_before = sum(s.n for p in self.phases for s in p if s.ada)
        for turns, sources, ada in segments:
            phase.append(Names(n=turns, sources=sources, per=len(sources), base=n,
                                         ada=ada, ada_base=FIRST_ADA + ada_before))
            n += turns * len(sources)
            ada_before += turns if ada else 0
        self.total = n
        self.phases.append(phase)
        return phase


def load_ada(sp, K, seg, i, s):
    m, slot = seg.ada_base + i, (seg.ada_base + s) % ADA
    sp.wait_ge(K.ada_used, m - (ADA - 1))
    sp.dma_start(K.ada_raw[:, slot], seg.ada(i)).then_inc(K.ada_landed[slot], 16)


def load_turn(sp, K, seg, i, s):
    for j, source in enumerate(seg.sources):
        n, first = seg.base + seg.per * i + j, seg.base + seg.per * s + j
        if first >= RAW:
            sp.wait_ge(K.lo_ready, n - (RAW - 1))
        src = source(i)
        sp.dma_start(K.raw[:, first % RAW, 0:src.shape[1], :], src).then_inc(K.landed[first % RAW], 16)


def load_ahead(sp, K, phase):
    seg = phase[0]
    for i in range(RAW // seg.per):
        load_turn(sp, K, seg, i, i)
    if seg.ada:
        load_ada(sp, K, seg, 0, 0)


def weights_sp(sp, K, index):
    for k, seg in enumerate(K.weights.phases[index]):
        out = RAW // seg.per if k == 0 else 0
        if seg.ada:
            for i in range(1, out):
                load_ada(sp, K, seg, i, i)

        def turn(i, s, seg=seg):
            load_turn(sp, K, seg, i, s)
            if seg.ada:
                load_ada(sp, K, seg, i, s)
        loop(sp, out, seg.n, RAW // int(np.gcd(RAW, seg.per)), turn)
    if index + 1 < len(K.weights.phases):
        load_ahead(sp, K, K.weights.phases[index + 1])


def landed_value(seg, i, s, j):
    first = (seg.base + seg.per * s + j) // RAW + 1
    if isinstance(i, int):
        return 16 * first
    return (seg.base + seg.per * i + j - (seg.base + seg.per * s + j) % RAW) * (16 // RAW) + 16


def split_hi(act, K, seg, i, s, j, tiles):
    n, first = seg.base + seg.per * i + j, seg.base + seg.per * s + j
    act.wait_ge(K.landed[first % RAW], landed_value(seg, i, s, j))
    if first >= SPLIT:
        act.wait_ge(K.chunks_done, n - (SPLIT - 1))
    act.activation(K.w_hi[:, first % SPLIT, 0:tiles, :], K.raw[:, first % RAW, 0:tiles, :],
                   ACT.Copy).then_inc(K.hi_ready, 1)


def split_lo(pool, K, seg, i, s, j, tiles):
    n, first = seg.base + seg.per * i + j, seg.base + seg.per * s + j
    pool.wait_ge(K.hi_ready, n + 1)
    pool.tensor_tensor(K.w_lo[:, first % SPLIT, 0:tiles, :], K.raw[:, first % RAW, 0:tiles, :],
                       K.w_hi[:, first % SPLIT, 0:tiles, :].bitcast(F32),
                       ALU.subtract).then_inc(K.lo_ready, 1)


def split_all(pool, K, phase, tiles):
    for seg, counts in zip(phase, tiles):
        step = RAW // int(np.gcd(RAW, seg.per))

        def body(i, s, seg=seg, counts=counts):
            for j in range(seg.per):
                split_lo(pool, K, seg, i, s, j, counts[j])
        loop(pool, 0, seg.n, step, body)


def multiply(pe, K, seg, i, s, j, tiles, outs, moving, first=True, last=True, before=None):
    n, slot = seg.base + seg.per * i + j, (seg.base + seg.per * s + j) % SPLIT
    pe.wait_ge(K.lo_ready, n + 1)
    for k in range(tiles):
        if before:
            before(k)
        for p, (wp, ap) in enumerate(PASSES):
            w = (K.w_hi, K.w_lo)[wp]
            for out, tokens in outs:
                mm = pe.matmul(out, w[:, slot, k, :], moving(ap, k, tokens),
                               start=first and k == 0 and p == 0,
                               stop=last and k == tiles - 1 and p == len(PASSES) - 1)
    mm.then_inc(K.chunks_done, 1)



NORM_SEMS = ("sq_ready", "ssq_added", "ssq_done", "var_ready", "std_ready", "rstd_ready")


def squares_act(act, N, K, b, parts):
    if b >= 2:
        act.wait_ge(N.ssq_added, b - 1)
    for src, sl in parts:
        ins = act.activation(K.sq[:, b % 2, sl], src, ACT.Square)
    ins.then_inc(N.sq_ready, 1)


def squares_dve(dve, N, K, b, width):
    if b == 0:
        return
    dve.wait_ge(N.sq_ready, b + 1)
    if b == 1:
        dve.tensor_tensor(K.ssq[:, 0:width], K.sq[:, 0, 0:width], K.sq[:, 1, 0:width],
                          ALU.add).then_inc(N.ssq_added, 2)
    else:
        dve.wait_ge(N.ssq_added, b)
        dve.tensor_tensor(K.ssq[:, 0:width], K.ssq[:, 0:width], K.sq[:, b % 2, 0:width],
                          ALU.add).then_inc(N.ssq_added, 1)


def norm_pe(pe, N, K, banks, width, blocks=DB):
    pe.wait_ge(N.ssq_added, blocks)
    for t0 in range(0, width, 512):
        w = min(512, width - t0)
        mm = pe.matmul(banks[t0 // 512][:, 0:w], K.ones, K.ssq[:, t0:t0 + w], start=True, stop=True)
        mm.then_inc(N.ssq_done, 1)


def norm_act(act, N, K, width):
    act.wait_ge(N.var_ready, (width + 511) // 512)
    act.activation(K.var[:, 0:width], K.var[:, 0:width], ACT.Sqrt).then_inc(N.std_ready, 1)


def norm_dve(dve, N, K, banks, width):
    for n, t0 in enumerate(range(0, width, 512)):
        w = min(512, width - t0)
        dve.wait_ge(N.ssq_done, n + 1)
        dve.tensor_scalar(K.var[:, t0:t0 + w], banks[n][:, 0:w], 1.0 / D, EPS, ALU.mult,
                          ALU.add).then_inc(N.var_ready, 1)
    dve.wait_ge(N.std_ready, 1)
    dve.reciprocal(K.var[:, 0:width], K.var[:, 0:width]).then_inc(N.rstd_ready, 1)
    dve.wait_ge(N.rstd_ready, 1)



def width_of(mods):
    return sum(m[0].stop - m[0].start for m in mods)


def pre_act(act, K, S, mods):
    for b in range(DB):
        squares_act(act, S.pre, K, b, [(x[:, b, :], sl) for sl, x, _, _ in mods])
    norm_act(act, S.pre, K, width_of(mods))
    for b in range(DB):
        act.wait_ge(S.scaled, b + 1)
        for sl, _, _, shift in mods:
            ins = act.activation(S.h[:, HI, b, sl], K.sq[:, b % 2, sl], ACT.Identity,
                                 bias=shift[:, b:b + 1])
        ins.then_inc(S.h_hi, 1)


def pre_dve(dve, K, S, mods, gain, banks):
    width = width_of(mods)
    for n, (_, _, scale, _) in enumerate(mods):
        ins = dve.scalar_tensor_tensor(K.fac[:, n], scale, 1.0, gain, ALU.add, ALU.mult)
        ins.then_inc(S.fac_ready, 1)
    for b in range(DB):
        squares_dve(dve, S.pre, K, b, width)
    norm_dve(dve, S.pre, K, banks, width)
    dve.wait_ge(S.fac_ready, len(mods))

    def low(b):
        dve.wait_ge(S.h_hi, b + 1)
        for sl, _, _, shift in mods:
            ins = dve.scalar_tensor_tensor(S.h[:, LO, b, sl], K.sq[:, b % 2, sl], shift[:, b:b + 1],
                                           S.h[:, HI, b, sl].bitcast(F32), ALU.add, ALU.subtract)
        ins.then_inc(S.h_ready, 1)

    for b in range(DB):
        if b >= 2:
            dve.wait_ge(S.h_ready, b - 1)
        for n, (sl, x, _, _) in enumerate(mods):
            ins = dve.scalar_tensor_tensor(K.sq[:, b % 2, sl], x[:, b, :], K.fac[:, n, b:b + 1], K.var[:, sl], ALU.mult, ALU.mult)
        ins.then_inc(S.scaled, 1)
        if b >= 1:
            low(b - 1)
    low(DB - 1)



def post_act_block(act, K, S, n, s, parts, width):
    for ps, sl in parts:
        ins = act.activation(S.y[:, at(n, 1), sl], ps, ACT.Copy)
    ins.then_inc(S.y_ready, 1)
    if s >= 2:
        act.wait_ge(S.post.ssq_added, n - 1)
    for ps, sl in parts:
        ins = act.activation(K.sq[:, s % 2, sl], ps, ACT.Square)
    ins.then_inc(S.post.sq_ready, 1)


def post_dve(dve, K, S, mods, gain, res, banks, after_pre=True):
    width = width_of(mods)
    for n, (_, _, gate) in enumerate(mods):
        dve.tensor_scalar(K.fac2[:, n], gate, 1.0 if res is not None else 0.0, res or 1.0, ALU.add,
                          ALU.mult).then_inc(S.fac_ready, 1)
    first, scaled = (len(mods), DB) if after_pre else (0, 0)
    dve.wait_ge(S.fac_ready, first + len(mods))
    for n, _ in enumerate(mods):
        dve.tensor_tensor(K.fac[:, n], K.fac2[:, n], gain, ALU.mult).then_inc(S.fac_ready, 1)
    for b in range(DB):
        squares_dve(dve, S.post, K, b, width)
    norm_dve(dve, S.post, K, banks, width)
    dve.wait_ge(S.fac_ready, first + 2 * len(mods))
    dve.wait_ge(S.y_ready, DB)

    def add(b):
        dve.wait_ge(S.scaled, scaled + b + 1)
        for sl, x, _ in mods:
            ins = dve.tensor_tensor(x[:, b, :], x[:, b, :], K.sq[:, b % 2, sl], ALU.add)
        ins.then_inc(S.x_ready, 1)

    for b in range(DB):
        if b >= 2:
            dve.wait_ge(S.x_ready, b - 1)
        for n, (sl, _, _) in enumerate(mods):
            ins = dve.scalar_tensor_tensor(K.sq[:, b % 2, sl], S.y[:, b, sl], K.fac[:, n, b:b + 1],
                                           K.var[:, sl], ALU.mult, ALU.mult)
        ins.then_inc(S.scaled, 1)
        if b >= 1:
            add(b - 1)
    add(DB - 1)


SUB_SEMS = ("scaled", "h_hi", "h_ready", "fac_ready", "y_ready", "x_ready")


@contextmanager
def phase(K, *names):
    nc = K.nc
    with ExitStack() as ctx:
        S = Names()
        assert len(names) <= K.local_n, len(names)
        for k, name in enumerate(names):
            K.serial += 1
            h = ctx.enter_context(nc.semaphore(f"{name.replace('.', '_')}_{K.serial}", num=K.local0 + k))
            if "." in name:
                group, field = name.split(".")
                S.values.setdefault(group, Names()).values[field] = h
            else:
                S.values[name] = h
        S.sb = lambda name, shape, dt=F32: K.sbuf(ctx, name, shape, dt)
        S.psum = lambda name, shape, dt=F32: K.psum(ctx, name, shape, dt)
        yield S
    nc.all_engine_barrier(sems_to_clear=range(K.local0, K.local0 + K.local_n))


def norm_names(group):
    return tuple(f"{group}.{n}" for n in NORM_SEMS)



def ada_sum(dve, K, steps, m, s, vecs):
    if isinstance(m, int):
        dve.wait_ge(K.ada_landed[0], 16 * (m + 1))
    else:
        dve.wait_ge(K.ada_landed[0], m * 16 + 16)
    for v, vec in enumerate(vecs):
        acc = K.ada_acc[:, v, :]
        for k in range(DB):
            col = K.cact[:, vec, k:k + 1]
            if k == 0:
                ins = dve.tensor_scalar(acc, K.ada_raw[:, 0, k, :], col, None, ALU.mult)
            else:
                ins = dve.scalar_tensor_tensor(acc, K.ada_raw[:, 0, k, :], col, acc, ALU.mult, ALU.add)
            if v == len(vecs) - 1 and k == DB - 1:
                ins.then_inc(K.ada_used, 1)
            else:
                steps(ins)


def ada_pe(pe, K, m, nv):
    pe.wait_ge(K.ada_used, m + 1)
    for v in range(nv):
        mm = pe.matmul(K.ada_ps[:, v, :], K.ones, K.ada_acc[:, v, :], start=True, stop=True)
    mm.then_inc(K.ada_total, 1)


def ada_columns(dve, K, steps, m, bias, out, nv):
    dve.wait_ge(K.ada_total, m + 1)
    ident = K.ident.rearrange("p (a c) -> p a c", a=1).broadcast_to([P, 2, P])
    for v in range(nv):
        dia = K.ada_dia[:, v]
        steps(dve.tensor_tensor(dia, K.ada_ps[:, v, :].rearrange("p (a c) -> p a c", a=2), ident, ALU.mult))
        steps(dve.tensor_reduce(K.ada_col[:, v, :], dia, AX.X, ALU.add))
    for v in range(nv):
        ins = dve.tensor_tensor(out(v), K.ada_col[:, v, :], bias, ALU.add)
    steps(ins)


def ada_ops(nv):
    return nv * DB - 1 + 2 * nv + 1


def start_phase(K):
    nc, A = K.nc, K.A
    with phase(K, "const_in", "x_in", "turned", "copied", "silu_ready", "steps", "stored") as S:
        S.rows_in = K.pool_sem("rows_in")
        xin = S.sb("x_in", [P, SEQ // P, D])
        rows = S.sb("param_rows", [P, len(PARAM_PAGES), P])
        ps = [S.psum(f"turn{i}", [P, 512]) for i in range(4)]
        pages = len(PARAM_PAGES)
        used = [sum(n for _, n in page) for page in PARAM_PAGES]
        with nc.Block() as block:

            @block.sync
            def _(sp):
                sp.dma_start(K.const[:], A["const"]).then_inc(S.const_in, 16)
                for m in range(FIRST_ADA):
                    if m >= ADA:
                        sp.wait_ge(K.ada_used, m - ADA + 1)
                    sp.dma_start(K.ada_raw[:, 0], K.ada_src(0, m)).then_inc(K.ada_landed[0], 16)
                load_ahead(sp, K, K.weights.phases[0])

            @block.scalar
            def _(act):
                act.dma_start(xin[:], A["x"].rearrange("a (t p) d -> p (a t) d", p=P)).then_inc(S.x_in, 16)
                act.wait_ge(S.copied, pages)
                for v, name in enumerate(("c", "c_2", "c_ctx")):
                    act.activation(K.cact[:, v, :], K.pcol(name, DB), ACT.Silu).then_inc(S.silu_ready, 1)

            @block.gpsimd
            def _(pool):
                for page, entries in enumerate(PARAM_PAGES):
                    r = 0
                    for name, n in entries:
                        for r0, nr, src in K.rows(name):
                            dst = rows[r + r0:r + r0 + nr, page, :]
                            if len(src.shape) == 3:
                                dst = dst.rearrange("p (a c) -> p a c", a=src.shape[1])
                            pool.dma_start(dst, src).then_inc(S.rows_in, 16)
                        r += n

            @block.tensor
            def _(pe):
                pe.wait_ge(S.const_in, 16)
                pe.wait_ge(S.rows_in, 16 * K.row_loads)
                for page in range(pages):
                    if page >= 4:
                        pe.wait_ge(S.copied, page - 3)
                    pe.transpose(ps[page % 4][:, 0:used[page]], rows[0:used[page], page, :],
                                 K.ident[0:used[page], 0:used[page]]).then_inc(S.turned, 1)
                pe.wait_ge(S.x_in, 16)
                for b in range(DB):
                    n = pages + b
                    pe.wait_ge(S.copied, n - 3)
                    for t in range(SEQ // P):
                        mm = pe.transpose(ps[n % 4][:, t * P:(t + 1) * P], xin[:, t, b * P:(b + 1) * P], K.ident)
                    mm.then_inc(S.turned, 1)
                for m in range(FIRST_ADA):
                    ada_pe(pe, K, m, 1)

            @block.vector
            def _(dve):
                for page in range(pages):
                    dve.wait_ge(S.turned, page + 1)
                    dve.tensor_copy(K.params[:, page * P:page * P + used[page]],
                                    ps[page % 4][:, 0:used[page]]).then_inc(S.copied, 1)
                for b in range(DB):
                    n = pages + b
                    dve.wait_ge(S.turned, n + 1)
                    dve.tensor_copy(K.x[:, b, :], ps[n % 4][:]).then_inc(S.copied, 1)
                dve.wait_ge(S.silu_ready, 3)
                dve.wait_ge(S.copied, pages + DB)
                steps = Steps(dve, S.steps)
                for m in range(FIRST_ADA):
                    ada_sum(dve, K, steps, m, m, (0,))
                    ada_columns(dve, K, steps, m, K.pcol("ada_b0", 72)[:, 2 * m:2 * m + 2],
                                lambda v, m=m: K.mods[:, 2 * m:2 * m + 2], 1)



def ffn_phase(K, index, layer, sub, which):
    nc, A = K.nc, K.A
    seg = K.weights.phases[index]
    up, down = seg[:-1], seg[-1]
    u0 = up[0]
    shift, scale, gate = (K.mod_cols(layer, sub, kind) for kind in range(3))
    pre_mods = [(LAT, K.x, scale, shift)]
    post_mods = [(LAT, K.x, gate)]
    tiles = (8, 8, FB - 16)
    with phase(K, *norm_names("pre"), *norm_names("post"), *SUB_SEMS, "silu_ready", "prod_ready",
               "hid_hi", "hid_ready", "steps") as S:
        hid = S.sb("hid", [P, 2, FB, SEQ], F32R)
        sil = S.sb("sil", [P, 2, SEQ])
        prod = S.sb("prod", [P, 2, SEQ])
        K.norm_buffers(S, SEQ)
        with ExitStack() as c:
            S.h = K.sbuf(c, "h", [P, 2, DB, SEQ], F32R)
        S.y = S.sb("y", [P, DB, SEQ])
        banks = [S.psum(f"acc{i}", [P, 512]) for i in range(4)]
        sums = [S.psum("sums", [P, 512])]
        with nc.Block() as block:

            @block.sync
            def _(sp):
                weights_sp(sp, K, index)

            @block.gpsimd
            def _(pool):
                split_all(pool, K, [Names(n=FB, per=2, base=u0.base), down], [(8, 8), tiles])

            @block.scalar
            def _(act):
                def split_up(i, s):
                    for j in range(2):
                        split_hi(act, K, u0, i, s, j, 8)

                def hidden(i, s):
                    act.wait_ge(K.chunks_done, u0.base + 2 * i + 1)
                    if s >= 2:
                        act.wait_ge(S.prod_ready, i - 1)
                    act.activation(sil[:, s % 2, :], banks[2 * (s % 2)][:], ACT.Silu).then_inc(S.silu_ready, 1)
                    act.wait_ge(S.prod_ready, i + 1)
                    act.activation(hid[:, HI, at(i, 1), :], prod[:, s % 2, :], ACT.Copy).then_inc(S.hid_hi, 1)

                split_up(0, 0)
                pre_act(act, K, S, pre_mods)

                def turn(i, s):
                    split_up(i + 1, s + 1)
                    hidden(i, s)
                turn(0, 0)
                turn(1, 1)
                loop(act, 2, FB - 1, 2, turn)
                split_hi(act, K, down, 0, 0, 0, tiles[0])
                hidden(FB - 1, FB - 1)
                for n in range(DB):
                    for j in range(3):
                        if n + j > 0:
                            split_hi(act, K, down, n, n, j, tiles[j])
                    if n:
                        act.wait_ge(K.chunks_done, down.base + 3 * n)
                        post_act_block(act, K, S, n - 1, n - 1, [(banks[(n - 1) % 4][:], LAT)], SEQ)
                act.wait_ge(K.chunks_done, down.base + 3 * DB)
                post_act_block(act, K, S, DB - 1, DB - 1, [(banks[(DB - 1) % 4][:], LAT)], SEQ)
                norm_act(act, S.post, K, SEQ)

            @block.tensor
            def _(pe):
                norm_pe(pe, S.pre, K, sums, SEQ)
                done = 0
                for part in up:
                    def turn(i, s, part=part, done=done):
                        i, s = i + done, s + done
                        if s >= 2:
                            pe.wait_ge(S.prod_ready, i - 1)
                        for j in range(2):
                            multiply(pe, K, u0, i, s, j, 8, [(banks[2 * (s % 2) + j][:], LAT)],
                                     lambda p, k, sl: S.h[:, p, k, sl],
                                     before=(lambda k: pe.wait_ge(S.h_ready, k + 1)) if s == 0 and j == 0 else None)
                        if part.ada:
                            ada_pe(pe, K, part.ada_base + i - done, part.ada.vecs)
                    lead = 2 if done == 0 else 0
                    for i in range(lead):
                        turn(i, i)
                    loop(pe, lead, part.n, 2, turn)
                    done += part.n

                pe.wait_ge(S.prod_ready, FB - 1)

                def block_turn(n, s):
                    if s >= 4:
                        pe.wait_ge(S.post.sq_ready, n - 3)
                    for j in range(3):
                        if s == 0:
                            pe.wait_ge(S.hid_ready, (8, 16, FB)[j])
                        multiply(pe, K, down, n, s, j, tiles[j], [(banks[s % 4][:], LAT)],
                                 lambda p, k, sl, j=j: hid[:, p, 8 * j + k, sl], first=j == 0, last=j == 2)
                for n in range(4):
                    block_turn(n, n)
                loop(pe, 4, DB, 4, block_turn)
                norm_pe(pe, S.post, K, sums, SEQ)

            @block.vector
            def _(dve):
                pre_dve(dve, K, S, pre_mods, K.pcol("norm_pre", 48)[:, (layer * NS + sub) * DB:][:, 0:DB], sums)
                done, base = 0, 0
                for part in up:
                    nv = part.ada.vecs if part.ada else 0
                    per = ada_ops(nv) if nv else 0

                    def turn(i, s, part=part, done=done, base=base, nv=nv, per=per):
                        steps = Steps(dve, S.steps, i * per + base)
                        if nv:
                            m = part.ada_base + i
                            ada_sum(dve, K, steps, m, s, part.ada.use)
                        i, s = i + done, s + done
                        dve.wait_ge(S.silu_ready, i + 1)
                        dve.wait_ge(K.chunks_done, u0.base + 2 * i + 2)
                        dve.tensor_tensor(prod[:, s % 2, :], sil[:, s % 2, :], banks[2 * (s % 2) + 1][:],
                                          ALU.mult).then_inc(S.prod_ready, 1)
                        dve.wait_ge(S.hid_hi, i + 1)
                        dve.tensor_tensor(hid[:, LO, at(i, 1), :], prod[:, s % 2, :],
                                          hid[:, HI, at(i, 1), :].bitcast(F32),
                                          ALU.subtract).then_inc(S.hid_ready, 1)
                        if nv:
                            ada_columns(dve, K, steps, m, part.ada.bias(i - done), part.ada.out(i - done), nv)
                            assert steps.n == per
                    loop(dve, 0, part.n, 2, turn)
                    done += part.n
                    base += part.n * per
                post_dve(dve, K, S, post_mods, K.pcol("norm_post", 48)[:, (layer * NS + sub) * DB:][:, 0:DB],
                         0.5, sums)

def split_operand_act(act, S, n, src, dst):
    act.wait_ge(S.m_full, n + 1)
    act.activation(dst, src, ACT.Copy).then_inc(S.m_hi, 1)


def split_operand_dve(dve, S, n, src, hi, lo):
    dve.wait_ge(S.m_hi, n + 1)
    dve.tensor_tensor(lo, src, hi.bitcast(F32), ALU.subtract).then_inc(S.m_ready, 1)


def out_pe(pe, K, S, seg, operand, banks_of, ready):
    for n in range(DB):
        if n >= 2:
            pe.wait_ge(S.post.sq_ready, n - 1)
        multiply(pe, K, seg, n, n, 0, DB, banks_of(n), lambda p, k, sl: operand[:, p, k, sl],
                 before=(lambda k: pe.wait_ge(ready, k + 1)) if n == 0 else None)


def out_act(act, K, S, seg, banks_of, width, first_split):
    for n in range(DB):
        if n + 1 >= first_split and n + 1 < DB:
            split_hi(act, K, seg, n + 1, n + 1, 0, DB)
        act.wait_ge(K.chunks_done, seg.base + n + 1)
        post_act_block(act, K, S, n, n, banks_of(n), width)
    norm_act(act, S.post, K, width)



CONV_A, CONV_B = 4, 31
LRU_C = 8.0


def lru_scale(dve, steps, lam, t, out):
    z, q, q2, acc = t[1], t[2], t[3], t[4]
    steps(dve.tensor_scalar(acc, z, 2.0, None, ALU.add))
    steps(dve.reciprocal(acc, acc))
    steps(dve.tensor_tensor(q, z, acc, ALU.mult))
    steps(dve.tensor_tensor(q2, q, q, ALU.mult))
    steps(dve.tensor_scalar(acc, q2, 1.0 / 19, 1.0 / 17, ALU.mult, ALU.add))
    for d in (15, 13, 11, 9, 7, 5, 3, 1):
        steps(dve.tensor_tensor(acc, acc, q2, ALU.mult))
        steps(dve.tensor_scalar(acc, acc, 1.0 / d, None, ALU.add))
    steps(dve.tensor_tensor(acc, acc, q, ALU.mult))
    steps(dve.tensor_scalar(q, lam, 0.0, None, ALU.min))
    steps(dve.scalar_tensor_tensor(out, acc, -2.0, q, ALU.mult, ALU.add))


LRU_SCALE_STEPS = 5 + 16 + 3


def mixer_ab_phase(K, index, layer, sub):
    nc, A = K.nc, K.A
    pairs, ax_seg, ag_seg, out_seg = K.weights.phases[index]
    shift, scale, gate = (K.mod_cols(layer, sub, kind) for kind in range(3))
    pre_mods, post_mods = [(LAT, K.x, scale, shift)], [(LAT, K.x, gate)]
    HB = 4
    with phase(K, *norm_names("pre"), *norm_names("post"), *SUB_SEMS, "gate_ready", "v_ready", "ax_ready",
               "pads", "conv_b", "conv_a", "lam_z", "steps", "w_in", "gates_ps", "ri_ready", "exp_ready",
               "sq_in", "root_ready", "ya_in", "stat_in", "stat_ps", "dev_ready", "dsq_ready", "gn_var",
               "gn_std", "gn_out", "m_full", "m_hi", "m_ready") as S:
        K.norm_buffers(S, SEQ)
        ga = S.sb("a_gate", [P, HB, SEQ])
        axp = S.sb("a_x_padded", [P, HB, CONV_A - 1 + SEQ])
        vp = S.sb("v_padded", [P, HB, CONV_B - 1 + SEQ])
        gsig = S.sb("b_gate", [P, 2, SEQ])
        conv = S.sb("conv", [P, 2, SEQ])
        vc = S.sb("v_conv", [P, HB, SEQ])
        xc = S.sb("x_conv", [P, HB, SEQ])
        wr = S.sb("gate_w", [P, 2, HB, P])
        lam = S.sb("lam", [P, 6, HB])
        mo = S.sb("m", [P, 2, DB, SEQ], F32R)
        with ExitStack() as c:
            S.h = K.sbuf(c, "h", [P, 2, DB, SEQ], F32R)
        with ExitStack() as c:
            ri = K.sbuf(c, "r_i", [P, 2, HB, SEQ])
            th = K.sbuf(c, "tanh", [P, HB, SEQ])
            mf = K.sbuf(c, "m_full", [P, HB, SEQ])
        with ExitStack() as c:
            S.y = K.sbuf(c, "y", [P, DB, SEQ])
        banks = [S.psum(f"acc{i}", [P, 512]) for i in range(4)]
        stat = [S.psum(f"stat{i}", [P, 512]) for i in range(2)]
        sums = [S.psum("sums", [P, 512])]
        wr4 = wr.rearrange("p g b (t e) -> p g b t e", t=2)
        out_banks = lambda n: [(banks[n % 2][:], LAT)]

        with nc.Block() as block:

            @block.sync
            def _(sp):
                weights_sp(sp, K, index)

            @block.gpsimd
            def _(pool):
                pool.memset(wr[:], 0.0).then_inc(S.pads, 1)
                pool.memset(axp[:, :, 0:CONV_A - 1], 0.0).then_inc(S.pads, 1)
                pool.memset(vp[:, :, 0:CONV_B - 1], 0.0).then_inc(S.pads, 1)
                split_all(pool, K, [pairs, ax_seg, ag_seg, out_seg], [(8, 8), (8,), (8,), (8,)])

            @block.scalar
            def _(act):
                act.wait_ge(S.pads, 1)
                for t in range(2):
                    for g in range(2):
                        src = A["a_gate_w"][0].rearrange("(b t) d e -> t d b e", t=2)[t]
                        act.dma_start(wr4[64 * t:64 * t + 64, g, :, t, :],
                                      src[:, :, 64 * g:64 * g + 64]).then_inc(S.w_in, 16)
                act.activation(lam[:, 0], K.pcol("a_lam", HB), ACT.Abs).then_inc(S.lam_z, 1)
                act.wait_ge(S.lam_z, 1)
                act.activation(lam[:, 1], lam[:, 0], ACT.Exp, scale=-1.0).then_inc(S.lam_z, 1)
                chunks = [(pairs, i, j) for i in range(HB) for j in range(2)] + \
                         [(ax_seg, i, 0) for i in range(HB)] + [(ag_seg, i, 0) for i in range(HB)]
                for n in range(SPLIT):
                    split_hi(act, K, chunks[n][0], chunks[n][1], chunks[n][1], chunks[n][2], 8)
                pre_act(act, K, S, pre_mods)
                for n, (seg, i, j) in enumerate(chunks):
                    act.wait_ge(K.chunks_done, pairs.base + n + 1)
                    bank = banks[n % 4]
                    if seg is pairs and j == 1:
                        if i >= 2:
                            act.wait_ge(S.v_ready, i - 1)
                        act.activation(gsig[:, i % 2, :], bank[:], ACT.Sigmoid).then_inc(S.gate_ready, 1)
                    elif seg is ax_seg:
                        if i == 0:
                            act.wait_ge(S.pads, 2)
                        act.activation(axp[:, i, CONV_A - 1:], bank[:], ACT.Copy).then_inc(S.ax_ready, 1)
                    elif seg is ag_seg:
                        act.activation(ga[:, i, :], bank[:], ACT.Gelu_apprx_tanh).then_inc(S.ax_ready, 1)
                    if n + SPLIT < len(chunks):
                        nxt, ni, nj = chunks[n + SPLIT]
                        split_hi(act, K, nxt, ni, ni, nj, 8)
                    else:
                        split_hi(act, K, out_seg, n + SPLIT - len(chunks), n + SPLIT - len(chunks), 0, 8)
                for b in range(HB):
                    for g, name in enumerate(("gate_br", "gate_bi")):
                        n = 2 * b + g
                        act.wait_ge(S.gates_ps, n + 1)
                        act.activation(ri[:, g, b, :], banks[n % 4][:], ACT.Sigmoid,
                                       bias=K.pcol(name, HB)[:, b:b + 1]).then_inc(S.ri_ready, 1)
                act.wait_ge(S.steps, LRU_SCALE_STEPS + 2)
                for b in range(HB):
                    act.wait_ge(S.ri_ready, 2 * b + 1)
                    act.activation(th[:, b, :], ri[:, 0, b, :], ACT.Tanh,
                                   scale=lam[:, 5, b:b + 1]).then_inc(S.exp_ready, 1)
                    act.wait_ge(S.exp_ready, 2 * b + 1)
                    act.activation(ri[:, 0, b, :], ri[:, 0, b, :], ACT.Exp,
                                   scale=lam[:, 0, b:b + 1]).then_inc(S.exp_ready, 1)
                for b in range(HB):
                    act.wait_ge(S.sq_in, b + 1)
                    act.activation(th[:, b, :], th[:, b, :], ACT.Sqrt).then_inc(S.root_ready, 1)
                for b in range(HB):
                    split_operand_act(act, S, b, mf[:, b, :], mo[:, HI, b, :])
                for b in range(HB):
                    act.wait_ge(S.dev_ready, b + 1)
                    act.activation(K.sq[:, b % 2, :], vc[:, b, :], ACT.Square).then_inc(S.dsq_ready, 1)
                    act.wait_ge(S.gn_var, b + 1)
                    act.activation(th[:, b, :], th[:, b, :], ACT.Sqrt).then_inc(S.gn_std, 1)
                for b in range(HB):
                    act.wait_ge(S.gn_out, b + 1)
                    act.activation(mf[:, b, :], vc[:, b, :], ACT.Silu, scale=K.pcol("b_norm_g", HB)[:, b:b + 1],
                                   bias=K.pcol("b_norm_b", HB)[:, b:b + 1]).then_inc(S.m_full, 1)
                    split_operand_act(act, S, HB + b, mf[:, b, :], mo[:, HI, HB + b, :])
                out_act(act, K, S, out_seg, out_banks, SEQ, SPLIT)

            @block.tensor
            def _(pe):
                norm_pe(pe, S.pre, K, sums, SEQ)
                hm = lambda p, k, sl: S.h[:, p, k, sl]
                n = 0
                for seg in (pairs, ax_seg, ag_seg):
                    for i in range(HB):
                        for j in range(seg.per):
                            if 4 <= n < 12:
                                pe.wait_ge(S.v_ready, (n - 4) // 2 + 1)
                            elif n >= 12:
                                pe.wait_ge(S.ax_ready, n - 11)
                            multiply(pe, K, seg, i, i, j, 8, [(banks[n % 4][:], LAT)], hm,
                                     before=(lambda k: pe.wait_ge(S.h_ready, k + 1)) if n == 0 else None)
                            n += 1
                pe.wait_ge(S.w_in, 16 * 4)
                for b in range(HB):
                    pe.wait_ge(S.conv_a, 3 * HB + b + 1)
                    for g in range(2):
                        n = 2 * b + g
                        pe.wait_ge(S.ax_ready, HB + n + 1) if n < 4 else pe.wait_ge(S.ri_ready, n - 3)
                        pe.matmul(banks[n % 4][:], wr[:, g, b, :], xc[:, b, :], start=True,
                                  stop=True).then_inc(S.gates_ps, 1)
                for b in range(HB):
                    pe.wait_ge(S.stat_in, b + 1)
                    pe.matmul(stat[0][:], K.bd64, vc[:, b, :], start=True, stop=True).then_inc(S.stat_ps, 1)
                    pe.wait_ge(S.dsq_ready, b + 1)
                    pe.matmul(stat[1][:], K.bd64, K.sq[:, b % 2, :], start=True, stop=True).then_inc(S.stat_ps, 1)
                pe.wait_ge(S.ri_ready, 2 * HB)
                out_pe(pe, K, S, out_seg, mo, out_banks, S.m_ready)
                norm_pe(pe, S.post, K, sums, SEQ)

            @block.vector
            def _(dve):
                steps = Steps(dve, S.steps)
                pre_dve(dve, K, S, pre_mods, K.pcol("norm_pre", 48)[:, (layer * NS + sub) * DB:][:, 0:DB], sums)
                dve.wait_ge(S.lam_z, 2)
                lru_scale(dve, steps, K.pcol("a_lam", HB), [lam[:, q] for q in range(5)], lam[:, 0])
                steps(dve.tensor_scalar(lam[:, 0], lam[:, 0], LRU_C, None, ALU.mult))
                steps(dve.tensor_scalar(lam[:, 5], lam[:, 0], -1.0, None, ALU.mult))
                dve.wait_ge(S.pads, 3)
                taps = K.pcol("b_conv_w", CONV_B * HB)
                done = 0
                for b in range(HB):
                    dve.wait_ge(S.gate_ready, b + 1)
                    dve.tensor_tensor(vp[:, b, CONV_B - 1:], banks[(2 * b) % 4][:], gsig[:, b % 2, :],
                                      ALU.mult).then_inc(S.v_ready, 1)
                    dve.wait_ge(S.v_ready, b + 1)
                    for k in range(CONV_B):
                        col = taps[:, HB * k + b:HB * k + b + 1]
                        src = vp[:, b, k:k + SEQ]
                        if k >= 2:
                            dve.wait_ge(S.conv_b, done - 1)
                            ins = dve.scalar_tensor_tensor(conv[:, k % 2, :], src, col, conv[:, k % 2, :],
                                                           ALU.mult, ALU.add)
                        else:
                            if b:
                                dve.wait_ge(S.conv_b, done)
                            ins = dve.tensor_scalar(conv[:, k % 2, :], src, col,
                                                    K.pcol("b_conv_b", HB)[:, b:b + 1] if k == 0 else 0.0,
                                                    ALU.mult, ALU.add)
                        ins.then_inc(S.conv_b, 1)
                        done += 1
                    dve.wait_ge(S.conv_b, done)
                    dve.tensor_tensor(vc[:, b, :], conv[:, 0, :], conv[:, 1, :], ALU.add).then_inc(S.conv_b, 1)
                    done += 1
                dve.wait_ge(S.ax_ready, HB)
                taps = K.pcol("a_conv_w", CONV_A * HB)
                for k in range(CONV_A):
                    for b in range(HB):
                        col = taps[:, HB * k + b:HB * k + b + 1]
                        src = axp[:, b, k:k + SEQ]
                        if k:
                            dve.wait_ge(S.conv_a, HB * (k - 1) + b + 1)
                            ins = dve.scalar_tensor_tensor(xc[:, b, :], src, col, xc[:, b, :], ALU.mult, ALU.add)
                        else:
                            ins = dve.tensor_scalar(xc[:, b, :], src, col, K.pcol("a_conv_b", HB)[:, b:b + 1],
                                                    ALU.mult, ALU.add)
                        ins.then_inc(S.conv_a, 1)
                for b in range(HB):
                    dve.wait_ge(S.exp_ready, 2 * b + 2)
                    steps(dve.tensor_tensor(mf[:, b, :], ri[:, 0, b, :], ri[:, 0, b, :], ALU.mult))
                    dve.scalar_tensor_tensor(th[:, b, :], mf[:, b, :], 1.0, th[:, b, :], ALU.add,
                                             ALU.mult).then_inc(S.sq_in, 1)
                    dve.wait_ge(S.ri_ready, 2 * HB)
                    steps(dve.tensor_tensor(xc[:, b, :], xc[:, b, :], ri[:, 1, b, :], ALU.mult))
                for b in range(HB):
                    dve.wait_ge(S.root_ready, b + 1)
                    steps(dve.tensor_tensor(xc[:, b, :], xc[:, b, :], th[:, b, :], ALU.mult))
                    steps(dve.tensor_tensor_scan(th[:, b, :], ri[:, 0, b, :], xc[:, b, :], 0.0, ALU.mult, ALU.add))
                    dve.wait_ge(S.ax_ready, 2 * HB)
                    dve.tensor_tensor(mf[:, b, :], th[:, b, :], ga[:, b, :], ALU.mult).then_inc(S.m_full, 1)
                for b in range(HB):
                    split_operand_dve(dve, S, b, mf[:, b, :], mo[:, HI, b, :], mo[:, LO, b, :])
                for b in range(HB):
                    if b == 0:
                        dve.wait_ge(S.conv_b, done)
                        dve.sem_inc(S.stat_in, HB)
                    dve.wait_ge(S.stat_ps, 2 * b + 1)
                    dve.scalar_tensor_tensor(vc[:, b, :], stat[0][:], -1.0 / 64, vc[:, b, :], ALU.mult,
                                             ALU.add).then_inc(S.dev_ready, 1)
                    dve.wait_ge(S.stat_ps, 2 * b + 2)
                    dve.tensor_scalar(th[:, b, :], stat[1][:], 1.0 / 64, EPS, ALU.mult, ALU.add).then_inc(S.gn_var, 1)
                    dve.wait_ge(S.gn_std, b + 1)
                    steps(dve.reciprocal(th[:, b, :], th[:, b, :]))
                    dve.tensor_tensor(vc[:, b, :], vc[:, b, :], th[:, b, :], ALU.mult).then_inc(S.gn_out, 1)
                for b in range(HB):
                    split_operand_dve(dve, S, HB + b, mf[:, b, :], mo[:, HI, HB + b, :], mo[:, LO, HB + b, :])
                post_dve(dve, K, S, post_mods, K.pcol("norm_post", 48)[:, (layer * NS + sub) * DB:][:, 0:DB],
                         1.0, sums)

C_HEADS = 8


def mixer_c_phase(K, index, layer, sub):
    nc, A = K.nc, K.A
    values, gates, out_seg = K.weights.phases[index]
    in_seg = Names(n=2 * DB, per=1, base=values.base)
    shift, scale, gate = (K.mod_cols(layer, sub, kind) for kind in range(3))
    pre_mods, post_mods = [(LAT, K.x, scale, shift)], [(LAT, K.x, gate)]
    NC = SEQ // CH
    with phase(K, *norm_names("pre"), *norm_names("post"), *norm_names("mid"), *SUB_SEMS, "z_ready", "mean_ps",
               "dev_ready", "vn_scaled", "vn_ready", "vt_ps", "vt_ready", "ws_ps", "ws_ready",
               "mix_ps", "m_full", "m_hi", "m_ready") as S:
        K.norm_buffers(S, SEQ)
        S.ws_in, S.mask_in = K.pool_sem("ws_in"), K.pool_sem("mask_in")
        z = S.sb("z", [P, 2, DB, SEQ])
        ws = S.sb("w_s", [P, C_HEADS, P])
        wst = S.sb("w_s_turned", [P, C_HEADS, P])
        mask = S.sb("mask", [P, P])
        bs = S.sb("b_s", [1, C_HEADS, P])
        vt = S.sb("v_turned", [P, 2, NC, P])
        mf = S.sb("m_full", [P, 2, SEQ])
        S.y = S.sb("y", [P, DB, SEQ])
        with ExitStack() as c:
            S.h = K.sbuf(c, "h", [P, 2, DB, SEQ], F32R)
        mo = S.sb("m", [P, 2, DB, SEQ], F32R)
        banks = [S.psum(f"acc{i}", [P, 512]) for i in range(4)]
        sums = [S.psum("sums", [P, 512])]
        tp = S.psum("turn", [P, 512])
        mixp = banks[2:4]
        out_banks = lambda n: [(banks[n % 2][:], LAT)]

        def turned_copy(act, b):
            act.wait_ge(S.vt_ps, b + 1)
            if b >= 2:
                act.wait_ge(S.mix_ps, b - 1)
            act.activation(vt[:, b % 2].rearrange("p n d -> p (n d)"), tp[:], ACT.Copy).then_inc(S.vt_ready, 1)

        def mix_pe(pe, b):
            pe.wait_ge(S.vt_ready, b + 1)
            if b >= 2:
                pe.wait_ge(S.m_full, b - 1)
            for n in range(NC):
                out = mixp[b % 2][:, n * P:(n + 1) * P]
                pe.matmul(out, vt[:, b % 2, n, :], wst[:, b, :], start=True, stop=False)
                mm = pe.matmul(out, K.ones[0:1, :], bs[:, b, :], start=False, stop=True)
            mm.then_inc(S.mix_ps, 1)

        with nc.Block() as block:

            @block.sync
            def _(sp):
                weights_sp(sp, K, index)

            @block.gpsimd
            def _(pool):
                pool.dma_start(ws[:], A["c_w_s"][0].rearrange("h t s -> t h s")).then_inc(S.ws_in, 16)
                pool.dma_start(mask[:], A["masks"][1]).then_inc(S.mask_in, 16)
                pool.dma_start(bs[:], A["c_b_s"]).then_inc(S.mask_in, 16)
                split_all(pool, K, [in_seg, out_seg], [(8,), (8,)])

            @block.scalar
            def _(act):
                for n in range(SPLIT):
                    split_hi(act, K, in_seg, n, n, 0, 8)
                pre_act(act, K, S, pre_mods)

                for n in range(2 * DB):
                    act.wait_ge(K.chunks_done, in_seg.base + n + 1)
                    half = (1 - n // DB) * DB + n % DB
                    act.activation(z[:, n // DB, n % DB, :], banks[n % 4][:], ACT.Gelu_apprx_tanh,
                                   bias=K.pcol("c_b_in", 2 * DB)[:, half:half + 1]).then_inc(S.z_ready, 1)
                    if n + SPLIT < 2 * DB:
                        split_hi(act, K, in_seg, n + SPLIT, n + SPLIT, 0, 8)
                    else:
                        m = n + SPLIT - 2 * DB
                        split_hi(act, K, out_seg, m, m, 0, 8)
                for b in range(DB):
                    act.wait_ge(S.dev_ready, b + 1)
                    squares_act(act, S.mid, K, b, [(z[:, 0, b, :], LAT)])
                norm_act(act, S.mid, K, SEQ)
                for b in range(DB):
                    act.wait_ge(S.vn_scaled, b + 1)
                    act.activation(z[:, 0, b, :], z[:, 0, b, :], ACT.Identity,
                                   bias=K.pcol("c_norm_b", DB)[:, b:b + 1]).then_inc(S.vn_ready, 1)
                    if b >= 1:
                        turned_copy(act, b - 1)
                    if b >= 3:
                        split_operand_act(act, S, b - 3, mf[:, (b - 3) % 2, :], mo[:, HI, b - 3, :])
                turned_copy(act, DB - 1)
                for b in range(DB - 3, DB):
                    split_operand_act(act, S, b, mf[:, b % 2, :], mo[:, HI, b, :])
                out_act(act, K, S, out_seg, out_banks, SEQ, SPLIT)

            @block.tensor
            def _(pe):
                norm_pe(pe, S.pre, K, sums, SEQ)
                hm = lambda p, k, sl: S.h[:, p, k, sl]
                for n in range(2 * DB):
                    if n >= 4:
                        pe.wait_ge(S.z_ready, n - 3)
                    multiply(pe, K, in_seg, n, n, 0, 8, [(banks[n % 4][:], LAT)], hm,
                             before=(lambda k: pe.wait_ge(S.h_ready, k + 1)) if n == 0 else None)
                pe.wait_ge(S.ws_in, 16)
                pe.wait_ge(S.z_ready, 2 * DB)
                for h in range(0, C_HEADS, 4):
                    for q in range(4):
                        mm = pe.transpose(mixp[h // 4][:, q * P:(q + 1) * P], ws[:, h + q, :], K.ident)
                    mm.then_inc(S.ws_ps, 1)
                pe.wait_ge(S.z_ready, DB)
                for b in range(DB):
                    mm = pe.matmul(tp[:], K.ones, z[:, 0, b, :], start=b == 0, stop=b == DB - 1)
                mm.then_inc(S.mean_ps, 1)
                norm_pe(pe, S.mid, K, sums, SEQ)
                pe.wait_ge(S.ws_ready, 2)
                pe.wait_ge(S.mask_in, 32)
                for b in range(DB):
                    pe.wait_ge(S.vn_ready, b + 1)
                    if b >= 1:
                        pe.wait_ge(S.vt_ready, b)
                    for n in range(NC):
                        mm = pe.transpose(tp[:, n * P:(n + 1) * P], z[:, 0, b, n * CH:(n + 1) * CH], K.ident)
                    mm.then_inc(S.vt_ps, 1)
                    if b >= 1:
                        mix_pe(pe, b - 1)
                mix_pe(pe, DB - 1)
                out_pe(pe, K, S, out_seg, mo, out_banks, S.m_ready)
                norm_pe(pe, S.post, K, sums, SEQ)

            @block.vector
            def _(dve):
                pre_dve(dve, K, S, pre_mods, K.pcol("norm_pre", 48)[:, (layer * NS + sub) * DB:][:, 0:DB], sums)
                dve.wait_ge(S.mask_in, 32)
                low = mask.rearrange("p (a c) -> p a c", a=1).broadcast_to([P, 4, P])
                for h in range(2):
                    dve.wait_ge(S.ws_ps, h + 1)
                    dve.tensor_tensor(wst[:, 4 * h:4 * h + 4, :],
                                      mixp[h].rearrange("p (a c) -> p a c", a=4), low,
                                      ALU.mult).then_inc(S.ws_ready, 1)
                dve.wait_ge(S.mean_ps, 1)
                for b in range(DB):
                    dve.scalar_tensor_tensor(z[:, 0, b, :], tp[:], -1.0 / D, z[:, 0, b, :], ALU.mult,
                                             ALU.add).then_inc(S.dev_ready, 1)
                for b in range(DB):
                    squares_dve(dve, S.mid, K, b, SEQ)
                norm_dve(dve, S.mid, K, sums, SEQ)
                for b in range(DB):
                    dve.scalar_tensor_tensor(z[:, 0, b, :], z[:, 0, b, :], K.pcol("c_norm_g", DB)[:, b:b + 1],
                                             K.var[:, 0:SEQ], ALU.mult, ALU.mult).then_inc(S.vn_scaled, 1)
                dve.wait_ge(S.z_ready, 2 * DB)
                for b in range(DB):
                    dve.wait_ge(S.mix_ps, b + 1)
                    if b >= 2:
                        dve.wait_ge(S.m_ready, b - 1)
                    dve.tensor_tensor(mf[:, b % 2, :], mixp[b % 2][:], z[:, 1, b, :], ALU.mult).then_inc(S.m_full, 1)
                    split_operand_dve(dve, S, b, mf[:, b % 2, :], mo[:, HI, b, :], mo[:, LO, b, :])
                post_dve(dve, K, S, post_mods, K.pcol("norm_post", 48)[:, (layer * NS + sub) * DB:][:, 0:DB],
                         1.0, sums)



def output_phase(K):
    nc = K.nc
    with phase(K, "turned", "copied", "stored") as S:
        rows = S.sb("out_rows", [P, SEQ // P, D])
        ps = [S.psum(f"turn{i}", [P, 512]) for i in range(4)]
        NT = SEQ // P
        with nc.Block() as block:

            @block.tensor
            def _(pe):
                for n in range(2 * NT):
                    t, half = n // 2, n % 2
                    if n >= 4:
                        pe.wait_ge(S.copied, n - 3)
                    for q in range(4):
                        mm = pe.transpose(ps[n % 4][:, q * P:(q + 1) * P],
                                          K.x[:, 4 * half + q, t * P:(t + 1) * P], K.ident)
                    mm.then_inc(S.turned, 1)

            @block.vector
            def _(dve):
                for n in range(2 * NT):
                    dve.wait_ge(S.turned, n + 1)
                    dve.tensor_copy(rows[:, n // 2, (n % 2) * 512:(n % 2) * 512 + 512],
                                    ps[n % 4][:]).then_inc(S.copied, 1)

            @block.sync
            def _(sp):
                for t in range(NT):
                    sp.wait_ge(S.copied, 2 * t + 2)
                    sp.dma_start(K.out.rearrange("a (t p) d -> p (a t) d", p=P)[:, t, :],
                                 rows[:, t, :]).then_inc(S.stored, 16)
                sp.wait_ge(S.stored, 16 * NT)



LORA_BLOCKS = 2
SHIFT_BLOCKS = 3 * RB + LORA_BLOCKS
GATE_R, FOUR, GATE_F = SHIFT_BLOCKS, SHIFT_BLOCKS + RB, SHIFT_BLOCKS + RB + 2
EVEN_BLOCKS = GATE_F + 2
PARTS = (LAT, CON)


def even_in_phase(K, index, layer):
    nc, A, u = K.nc, K.A, K.u
    seg, late = K.weights.phases[index]
    pre_mods = [(sl, x, K.mod2_cols(layer, v, 1), K.mod2_cols(layer, v, 0))
                for v, (sl, x) in enumerate(((LAT, K.x), (CON, K.xc)))]
    with phase(K, *norm_names("pre"), *SUB_SEMS, "ctx_in", "turned", "copied", "coef", "based", "shifted",
               "late_ready", "late_out0", "late_out1", "x_saved") as S:
        K.norm_buffers(S, TOK)
        stage = S.sb("late", [P, 2, TOK])
        with ExitStack() as c:
            rows = K.sbuf(c, "ctx_rows", [P, CTX // P, D])
        S.h = S.sb("h", [P, 2, DB, TOK], F32R)
        keep = S.sb("keep", [P, SHIFT_BLOCKS])
        move4 = S.sb("move4", [P, 4, SHIFT_BLOCKS])
        move2 = S.sb("move2", [P, 2, SHIFT_BLOCKS])
        lat = [S.psum(f"lat{i}", [P, 512]) for i in range(4)]
        con = [S.psum(f"con{i}", [P, 512]) for i in range(4)]
        sums = con[2:4]
        late_out = (S.late_out0, S.late_out1)
        outs = lambda s: [(lat[s % 4][:], LAT), (con[s % 4][:, 0:CTX], CON)]
        NT = CTX // P

        with nc.Block() as block:

            @block.sync
            def _(sp):
                sp.dma_start(rows[:], A["ctx_2"].rearrange("a (t p) d -> p (a t) d", p=P)).then_inc(S.ctx_in, 16)
                sp.dma_start(K.x_dram, K.x[:]).then_inc(S.x_saved, 16)
                weights_sp(sp, K, index)
                sp.wait_ge(S.x_saved, 16)

            @block.gpsimd
            def _(pool):
                split_all(pool, K, [seg, late], [(8,), (8,)])

            @block.scalar
            def _(act):
                for n in range(SPLIT):
                    split_hi(act, K, seg, n, n, 0, DB)
                act.wait_ge(S.copied, DB)
                pre_act(act, K, S, pre_mods)

                def base_turn(i, s):
                    act.wait_ge(K.chunks_done, seg.base + i + 1)
                    for ps, sl in outs(s):
                        ins = act.activation(u[:, at(i, 1), sl], ps, ACT.Copy, scale=keep[:, at(i, 1)])
                    ins.then_inc(S.based, 1)

                def turn(i, s):
                    base_turn(i, s)
                    split_hi(act, K, seg, i + SPLIT, s + SPLIT, 0, DB)
                act.wait_ge(S.coef, 1 + 4 + 2)
                loop(act, 0, SHIFT_BLOCKS - 4, 4, turn)
                for i in range(SHIFT_BLOCKS - 4, SHIFT_BLOCKS):
                    base_turn(i, i)
                    if i + SPLIT < SHIFT_BLOCKS:
                        split_hi(act, K, seg, i + SPLIT, i + SPLIT, 0, DB)
                    else:
                        split_hi(act, K, late, i + SPLIT - SHIFT_BLOCKS, i + SPLIT - SHIFT_BLOCKS, 0, DB)
                for i in range(late.n):
                    act.wait_ge(K.chunks_done, late.base + i + 1)
                    if i >= 2:
                        act.wait_ge(late_out[i % 2], 16 * (i // 2))
                    func = ACT.Copy if i in (RB, RB + 1) else ACT.Silu
                    for ps, sl in outs(SHIFT_BLOCKS + i):
                        ins = act.activation(stage[:, i % 2, sl], ps, func)
                    ins.then_inc(S.late_ready, 1)
                    if i + SPLIT < late.n:
                        split_hi(act, K, late, i + SPLIT, i + SPLIT, 0, DB)
                    act.wait_ge(S.late_ready, i + 1)
                    act.dma_start(K.late_dram[i], stage[:, i % 2, :]).then_inc(late_out[i % 2], 16)
                for o in late_out:
                    act.wait_ge(o, 16 * (late.n // 2))
                act.wait_ge(S.shifted, 6 * SHIFT_BLOCKS)
                act.activation(u[:, 3 * RB, :], u[:, 3 * RB, :], ACT.Tanh)

            @block.tensor
            def _(pe):
                pe.wait_ge(S.ctx_in, 16)
                for b in range(DB):
                    if b >= 4:
                        pe.wait_ge(S.copied, b - 3)
                    for t in range(NT):
                        mm = pe.transpose(lat[b % 4][:, t * P:(t + 1) * P], rows[:, t, b * P:(b + 1) * P], K.ident)
                    mm.then_inc(S.turned, 1)
                norm_pe(pe, S.pre, K, sums, TOK)

                def turn(i, s):
                    if s >= 4:
                        pe.wait_ge(S.based, i - 3)
                        pe.wait_ge(S.shifted, i * 6 - 18)
                    multiply(pe, K, seg, i, s, 0, DB, outs(s), lambda p, k, sl: S.h[:, p, k, sl],
                             before=(lambda k: pe.wait_ge(S.h_ready, k + 1)) if s == 0 else None)
                for i in range(4):
                    turn(i, i)
                loop(pe, 4, SHIFT_BLOCKS, 4, turn)
                for i in range(late.n):
                    if i < 4:
                        pe.wait_ge(S.based, SHIFT_BLOCKS - 3 + i)
                        pe.wait_ge(S.shifted, 6 * (SHIFT_BLOCKS - 3 + i))
                    else:
                        pe.wait_ge(S.late_ready, i - 3)
                    multiply(pe, K, late, i, i, 0, DB, outs(SHIFT_BLOCKS + i), lambda p, k, sl: S.h[:, p, k, sl])

            @block.vector
            def _(dve):
                for b in range(DB):
                    dve.wait_ge(S.turned, b + 1)
                    dve.tensor_copy(K.xc[:, b, :], lat[b % 4][:, 0:CTX]).then_inc(S.copied, 1)
                dve.wait_ge(S.copied, DB)
                mu = K.pcol("mu", SHIFT_BLOCKS)
                dve.tensor_scalar(keep[:], mu, -1.0, 1.0, ALU.mult, ALU.add).then_inc(S.coef, 1)
                for m in range(4):
                    dve.tensor_scalar(move4[:, m, :], mu, K.shift4[:, m:m + 1], None, ALU.mult).then_inc(S.coef, 1)
                for m in range(2):
                    dve.tensor_scalar(move2[:, m, :], mu, K.shift2[:, m:m + 1], None, ALU.mult).then_inc(S.coef, 1)
                pre_dve(dve, K, S, pre_mods, K.pcol("norm_pre_2", 16)[:, layer * DB:][:, 0:DB], sums)
                dve.wait_ge(S.coef, 7)

                def add(i, dst, src, col, before):
                    if before is not None:
                        dve.wait_ge(S.shifted, i * 6 + before)
                    dve.scalar_tensor_tensor(dst, src, col, dst, ALU.mult, ALU.add).then_inc(S.shifted, 1)

                def turn(i, s):
                    dve.wait_ge(S.based, i + 1)
                    (L, _), (C, _) = outs(s)
                    one = at(i, 1)
                    grid = lambda ap: ap.rearrange("p (r c) -> p r c", c=GRID)
                    ul = u[:, one, LAT].rearrange("p a t -> p (a t)")
                    uc = u[:, one, CON].rearrange("p a t -> p (a t)")
                    c4 = [move4[:, m, one] for m in range(4)]
                    c2 = [move2[:, m, one] for m in range(2)]
                    add(i, grid(ul)[:, :, 1:], grid(L)[:, :, :-1], c4[0], None)
                    add(i, uc[:, 1:], C[:, :-1], c2[0], None)
                    add(i, grid(ul)[:, :, :-1], grid(L)[:, :, 1:], c4[1], 1)
                    add(i, uc[:, :-1], C[:, 1:], c2[1], 2)
                    add(i, ul[:, GRID:], L[:, :-GRID], c4[2], 3)
                    add(i, ul[:, :-GRID], L[:, GRID:], c4[3], 5)
                loop(dve, 0, SHIFT_BLOCKS, 4, turn)


def even_scan_phase(K):
    nc, A, u = K.nc, K.A, K.u
    NCH = TOK // CH
    ORDER = ((4, 5, 0, 1, 2, 3), (5, 4, 3, 2, 1, 0))
    LEVELS = 6
    PE_U, EV_U, AC_U, PO_U = 4 + 2 * LEVELS + 4, 3 + 4 + 2 * LEVELS + 3, 7, 4
    PP, PA, PD = 6, 13, 4 + 4 + 2 + 2 * 7 + 3 + 2 + 2
    with phase(K, "tables", "zeros", "w_out", "pp", "pa", "pd", "omk", "lw",
               *(f"{n}{d}" for n in ("pe", "ev", "ac", "po") for d in range(2))) as S:
        masks = S.sb("masks", [P, 4, P])
        levels = S.sb("levels", [P, 7, 2, P])
        goes = S.sb("goes", [P, TOK])
        lw = S.sb("lora_w", [P, 4, P])
        omk = S.sb("one_minus_ka", [P, RB])
        kk = S.sb("kk", [P, TOK])
        vst = S.sb("v_block", [P, TOK])
        sgm = S.sb("sgm", [P, 4, TOK])
        cs = S.sb("cs", [P, 2, TOK])
        wi = S.sb("w_inv", [P, 2, TOK])
        wlast = S.sb("w_last", [P, 2, NCH])
        flat = K.x.rearrange("p b t -> p (b t)")
        kt = [flat[:, d * TOK:(d + 1) * TOK] for d in range(2)]
        ksum, tmp = flat[:, 2 * TOK:3 * TOK], flat[:, 3 * TOK:4 * TOK]
        U = []
        for d in range(2):
            U.append(Names(
                qp=S.sb("q_r_padded", [P, 2, 2, P]), bqr=S.sb("bqr", [P, 2, 2, P]), kqr=S.sb("kqr", [P, 2, 2, P]),
                low=S.sb("low", [P, 2, P]), tx=S.sb("t_x", [P, 2, 2, P]), y=S.sb("y", [P, 2, P]),
                vp=S.sb("v_padded", [P, 2, P]), tok=S.sb("tok", [P, 3, P]), rp=S.sb("rhs_padded", [P, 2, P]),
                sp=S.sb("sa_padded", [P, 2, P]), s=S.sb("state", [P, P]),
                b=[S.psum(f"u{d}_{i}", [P, 512]) for i in range(4)],
                pe=(S.pe0, S.pe1)[d], ev=(S.ev0, S.ev1)[d], ac=(S.ac0, S.ac1)[d], po=(S.po0, S.po1)[d]))
        pre_banks = [(U[p // 2].b[2 * (p % 2)], U[p // 2].b[2 * (p % 2) + 1]) for p in range(4)]

        def both(banks):
            return [(banks[0][:], LAT), (banks[1][:, 0:CTX], CON)]

        def heads(ap):
            return ap.rearrange("p (a c) -> p a c", a=1).broadcast_to([P, 2, P])

        cols = lambda d, k: slice(ORDER[d][k] * CH, (ORDER[d][k] + 1) * CH)

        with nc.Block() as block:

            @block.sync
            def _(sp):
                sp.dma_start(masks[:], A["masks"].rearrange("m s t -> s m t")).then_inc(S.tables, 16)
                sp.dma_start(levels[:], A["levels"].rearrange("(n d) t s -> t n d s", d=2)).then_inc(S.tables, 16)
                sp.dma_start(goes[:], A["goes"][0]).then_inc(S.tables, 16)
                sp.wait_ge(S.zeros, 1)

                def load(b):
                    for d in range(2):
                        for w, name in enumerate(("ev_w2_2", "ev_a2_2")):
                            sp.dma_start(lw[64 * d:64 * d + 64, 2 * d + w, :],
                                         A[name][0, d][:, at(b * P, P)]).then_inc(S.lw, 16)
                load(0)
                with sp.Fori(0, RB - 1) as b:
                    sp.wait_ge(S.pp, b * PP + 4)
                    load(b + 1)

            @block.gpsimd
            def _(pool):
                pool.memset(lw[:], 0.0).then_inc(S.zeros, 1)
                for d in range(2):
                    for t in (U[d].qp, U[d].vp, U[d].rp, U[d].sp):
                        pool.memset(t[:], 0.0).then_inc(S.zeros, 1)
                pool.wait_ge(S.zeros, 9)
                with pool.Fori(0, RB) as b:
                    pool.wait_ge(S.pd, b * PD + PD)
                    for k in range(NCH):
                        for d in range(2):
                            c, V = cols(d, k), U[d]
                            pool.wait_ge(V.pe, b * (NCH * PE_U) + (k * PE_U + 1))
                            for h in range(2):
                                hp = slice(64 * h, 64 * h + 64)
                                for w, src in enumerate((sgm[hp, 2 * d, c], cs[hp, d, c])):
                                    pool.tensor_tensor(V.qp[hp, h, w, :], src, K.ones[hp, :], ALU.mult).then_inc(V.po, 1)

            @block.tensor
            def _(pe):
                pe.wait_ge(S.zeros, 9)
                for d in range(2):
                    pe.sem_inc(U[d].pe, 1)
                with pe.Fori(0, RB) as b:
                    pe.wait_ge(S.lw, b * 64 + 64)
                    for d in range(2):
                        pe.wait_ge(U[d].ev, b * (NCH * EV_U) + 1)
                    for p in range(4):
                        for ps, sl in both(pre_banks[p]):
                            mm = pe.matmul(ps, lw[:, p, :], u[:, 3 * RB + p % 2, sl], start=True, stop=True)
                        mm.then_inc(S.pp, 1)
                    pe.wait_ge(S.pa, b * PA + 5)
                    for ps, sl in both(pre_banks[0]):
                        mm = pe.matmul(ps, K.bd64, tmp[:, sl], start=True, stop=True)
                    mm.then_inc(S.pp, 1)
                    pe.wait_ge(S.pd, b * PD + (PD - 4))
                    for ps, sl in both(pre_banks[1]):
                        mm = pe.matmul(ps, K.bd64, ksum[:, sl], start=True, stop=True)
                    mm.then_inc(S.pp, 1)
                    for k in range(NCH):
                        ticks = [Names(ev=b * (NCH * EV_U) + (k * EV_U + 1),
                                                 ac=b * (NCH * AC_U) + k * AC_U, po=b * (NCH * PO_U) + k * PO_U)
                                 for d in range(2)]
                        for d in range(2):
                            V, t, c = U[d], ticks[d], cols(d, k)
                            bt = sgm[:, 2 * d + 1, c]
                            pe.wait_ge(V.po, t.po + 4)
                            pe.wait_ge(V.ev, t.ev)
                            rhs = V.qp.rearrange("p h q t -> p (h q t)")
                            pe.matmul(V.b[0][:], bt, rhs, start=True, stop=True).then_inc(V.pe, 1)
                            pe.matmul(V.b[1][:], kt[d][:, c], rhs, start=True, stop=True).then_inc(V.pe, 1)
                            for h in range(2):
                                mm = pe.matmul(V.b[2][:, h * P:h * P + P], V.qp[:, h, 0, :], bt, start=True, stop=True)
                            mm.then_inc(V.pe, 1)
                            for n, src in enumerate((vst[:, c], kt[d][:, c], bt)):
                                mm = pe.transpose(V.b[3][:, n * P:n * P + P], src, K.ident)
                            mm.then_inc(V.pe, 1)
                        for lv in range(LEVELS):
                            for d in range(2):
                                V, t, c = U[d], ticks[d], cols(d, k)
                                pe.wait_ge(V.ev, t.ev + 7 + 2 * lv)
                                for h in range(2):
                                    mm = pe.matmul(V.b[2][:, h * P:h * P + P], V.bqr[:, h, 0, :], V.tx[:, 0, h, :],
                                                   start=True, stop=True)
                                mm.then_inc(V.pe, 1)
                                if lv == 0:
                                    pe.wait_ge(V.ac, t.ac + 3)
                                    out = V.b[3][:, 0:P]
                                    pe.matmul(out, sgm[:, 2 * d, c], V.s[:], start=True, stop=False)
                                    for h in range(2):
                                        mm = pe.matmul(out, V.kqr[:, h, 0, :], V.vp[:, h, :], start=False, stop=h == 1)
                                    mm.then_inc(V.pe, 1)
                            for d in range(2):
                                V, t = U[d], ticks[d]
                                pe.wait_ge(V.ev, t.ev + 8 + 2 * lv)
                                for h in range(2):
                                    if lv < LEVELS - 1:
                                        pe.matmul(V.b[0][:, h * P:h * P + P], V.tx[:, 1, h, :], V.y[:, h, :],
                                                  start=True, stop=True)
                                    mm = pe.matmul(V.b[0][:, (2 + h) * P:(3 + h) * P], V.y[:, h, :], V.tx[:, 1, h, :],
                                                   start=True, stop=True)
                                mm.then_inc(V.pe, 1)
                        for d in range(2):
                            V, t, c = U[d], ticks[d], cols(d, k)
                            pe.wait_ge(V.ev, t.ev + 7 + 2 * LEVELS)
                            pe.wait_ge(V.ac, t.ac + 5)
                            for h in range(2):
                                mm = pe.matmul(V.b[3][:, P:2 * P], V.tx[:, 1, h, :], V.rp[:, h, :], start=h == 0,
                                               stop=h == 1)
                            mm.then_inc(V.pe, 1)
                        for d in range(2):
                            V, t, c = U[d], ticks[d], cols(d, k)
                            out = V.b[3][:, 2 * P:3 * P]
                            pe.wait_ge(V.ac, t.ac + 7)
                            pe.matmul(out, V.s[:], cs[:, d, c], start=True, stop=False)
                            for h in range(2):
                                pe.matmul(out, V.vp[:, h, :], V.kqr[:, h, 1, :], start=False, stop=False)
                            for h in range(2):
                                mm = pe.matmul(out, V.sp[:, h, :], V.bqr[:, h, 1, :], start=False, stop=h == 1)
                            mm.then_inc(V.pe, 1)
                            out = V.b[1][:, 0:P]
                            pe.matmul(out, V.tok[:, 1, :], V.tok[:, 0, :], start=True, stop=False)
                            for h in range(2):
                                mm = pe.matmul(out, V.tok[:, 2, :], V.sp[:, h, :], start=False, stop=h == 1)
                            mm.then_inc(V.pe, 1)

            @block.scalar
            def _(act):
                act.wait_ge(S.zeros, 9)
                with act.Fori(0, RB) as b:
                    one = at(b, 1)
                    biases = [K.pcol("w0", 2 * RB)[:, one], K.pcol("a0", 2 * RB)[:, one],
                              K.pcol("w0", 2 * RB)[:, at(b + RB, 1)], K.pcol("a0", 2 * RB)[:, at(b + RB, 1)]]
                    for p in range(4):
                        act.wait_ge(S.pp, b * PP + p + 1)
                        for ps, sl in both(pre_banks[p]):
                            ins = act.activation(sgm[:, p, sl], ps, ACT.Sigmoid, bias=biases[p])
                        ins.then_inc(S.pa, 1)
                    act.wait_ge(S.pd, b * PD + 1)
                    act.activation(tmp, kk[:], ACT.Square).then_inc(S.pa, 1)
                    act.activation(vst[:], u[:, at(b + 2 * RB, 1), :], ACT.Copy).then_inc(S.pa, 1)
                    act.wait_ge(S.pp, b * PP + 5)
                    for ps, sl in both(pre_banks[0]):
                        ins = act.activation(tmp[:, sl], ps, ACT.Sqrt)
                    ins.then_inc(S.pa, 1)
                    for d in range(2):
                        act.wait_ge(S.pd, b * PD + 4 + 2 * (d + 1))
                        act.activation(wi[:, d, :], cs[:, d, :], ACT.Exp, scale=DECAY).then_inc(S.pa, 1)
                        act.wait_ge(S.pa, b * PA + 8 + 3 * d)
                        act.activation(cs[:, d, :], cs[:, d, :], ACT.Exp, scale=-DECAY).then_inc(S.pa, 1)
                        act.activation(sgm[:, 2 * d, :], sgm[:, 2 * d, :], ACT.Exp, scale=-DECAY).then_inc(S.pa, 1)
                    for k in range(NCH):
                        for d in range(2):
                            V = U[d]
                            act.wait_ge(V.pe, b * (NCH * PE_U) + (k * PE_U + 5))
                            act.activation(V.tok.rearrange("p n c -> p (n c)"), V.b[3][:, 0:3 * P],
                                           ACT.Copy).then_inc(V.ac, 1)
                            for h in range(2):
                                hc = slice(64 * h, 64 * h + 64)
                                act.activation(V.vp[:, h, hc], V.b[3][:, hc], ACT.Copy).then_inc(V.ac, 1)
                        for d in range(2):
                            V = U[d]
                            act.wait_ge(V.pe, b * (NCH * PE_U) + (k * PE_U + 7))
                            for h in range(2):
                                hc = slice(64 * h, 64 * h + 64)
                                act.activation(V.rp[:, h, hc], V.b[3][:, hc], ACT.Copy).then_inc(V.ac, 1)
                        for d in range(2):
                            V = U[d]
                            act.wait_ge(V.pe, b * (NCH * PE_U) + (k * PE_U + 7 + 2 * LEVELS))
                            for h in range(2):
                                act.activation(V.sp[:, h, 64 * h:64 * h + 64], V.b[3][:, P + 64 * h:P + 64 * h + 64],
                                               ACT.Copy, scale=-1.0).then_inc(V.ac, 1)

            @block.vector
            def _(dve):
                dve.tensor_scalar(omk[:], K.pcol("k_a", RB), -1.0, 1.0, ALU.mult, ALU.add).then_inc(S.omk, 1)
                dve.wait_ge(S.omk, 1)
                dve.wait_ge(S.tables, 48)
                for d in range(2):
                    dve.sem_inc(U[d].ev, 1)
                with dve.Fori(0, RB) as b:
                    steps = Steps(dve, S.pd, b * PD)
                    row = lambda n: u[:, at(b + n * RB, 1), :].rearrange("p a t -> p (a t)")
                    col = lambda name: K.pcol(name, RB)[:, at(b, 1)]
                    r, k0, v = row(0), row(1), row(2)
                    steps(dve.tensor_scalar(kk[:], k0, col("k_k"), None, ALU.mult))
                    dve.wait_ge(S.pa, b * PA + 7)
                    steps(dve.tensor_scalar(tmp, tmp, 1e-12, None, ALU.max))
                    steps(dve.reciprocal(tmp, tmp))
                    steps(dve.tensor_tensor(kk[:], kk[:], tmp, ALU.mult))
                    for d in range(2):
                        way = slice(None, None, -1) if d else slice(None)
                        steps(dve.tensor_tensor_scan(cs[:, d, way], goes[:], sgm[:, 2 * d, way], 0.0, ALU.mult, ALU.add))
                        steps(dve.tensor_tensor(sgm[:, 2 * d, :], cs[:, d, :], sgm[:, 2 * d, :], ALU.subtract))
                    for d in range(2):
                        steps(dve.memset(U[d].s[:], 0.0))
                    for d in range(2):
                        rate = sgm[:, 2 * d + 1, :]
                        steps(dve.tensor_scalar(kt[d], rate, col("k_a"), omk[:, at(b, 1)], ALU.mult, ALU.add))
                        steps(dve.tensor_tensor(kt[d], kt[d], k0, ALU.mult))
                        dve.wait_ge(S.pa, b * PA + 10 + 3 * d)
                        last = 0 if d else CH - 1
                        steps(dve.tensor_copy(wlast[:, d, :], cs[:, d, :].rearrange("p (c t) -> p c t", t=CH)[:, :, last]))
                        steps(dve.tensor_tensor(rate, rate, kk[:], ALU.mult))
                        steps(dve.tensor_tensor(rate, rate, wi[:, d, :], ALU.mult))
                        steps(dve.tensor_tensor(sgm[:, 2 * d, :], sgm[:, 2 * d, :], kk[:], ALU.mult))
                        steps(dve.tensor_tensor(cs[:, d, :], cs[:, d, :], r, ALU.mult))
                    steps(dve.tensor_tensor(ksum, kt[0], kt[1], ALU.add))
                    steps(dve.tensor_tensor(kt[0], kt[0], wi[:, 0, :], ALU.mult))
                    steps(dve.scalar_tensor_tensor(ksum, ksum, col("r_k"), r, ALU.mult, ALU.mult))
                    steps(dve.tensor_tensor(kt[1], kt[1], wi[:, 1, :], ALU.mult))
                    dve.wait_ge(S.pp, b * PP + 6)
                    for ps, sl in both(pre_banks[1]):
                        steps(dve.tensor_tensor(u[:, at(b, 1), sl], ps.rearrange("p (a t) -> p a t", a=1),
                                                u[:, at(b + 2 * RB, 1), sl], ALU.mult))
                    assert steps.n == PD - 1, steps.n
                    dve.sem_inc(S.pd, 1)
                    for k in range(NCH):
                        pe0 = b * (NCH * PE_U) + (k * PE_U + 1)
                        ev0 = b * (NCH * EV_U) + (k * EV_U + 1)
                        for d in range(2):
                            V = U[d]
                            tri = masks[:, 2 * d:2 * d + 2, :].rearrange("p q t -> p (q t)")
                            tri = tri.rearrange("p (a c) -> p a c", a=1).broadcast_to([P, 2, 2 * P])
                            pair = lambda ap: ap.rearrange("p h q t -> p h (q t)")
                            two = lambda ap: ap.rearrange("p (h t) -> p h t", h=2)
                            dve.wait_ge(V.pe, pe0 + 1)
                            dve.tensor_tensor(pair(V.bqr), two(V.b[0][:]), tri, ALU.mult).then_inc(V.ev, 1)
                            dve.wait_ge(V.pe, pe0 + 2)
                            dve.tensor_tensor(pair(V.kqr), two(V.b[1][:]), tri, ALU.mult).then_inc(V.ev, 1)
                            dve.wait_ge(V.pe, pe0 + 3)
                            dve.tensor_tensor(V.low[:], two(V.b[2][:, 0:2 * P]), heads(levels[:, 0, d, :]),
                                              ALU.mult).then_inc(V.ev, 1)
                            dve.wait_ge(V.ev, ev0 + 3)
                            dve.tensor_tensor(V.tx[:, 0], heads(K.ident), V.low[:], ALU.subtract).then_inc(V.ev, 1)
                            dve.tensor_tensor(V.y[:], V.bqr[:, :, 0, :], heads(levels[:, 0, 1 - d, :]),
                                              ALU.mult).then_inc(V.ev, 1)
                            dve.wait_ge(V.ev, ev0 + 5)
                            dve.tensor_tensor(V.tx[:, 1], heads(K.ident), V.y[:], ALU.subtract).then_inc(V.ev, 2)
                        for lv in range(LEVELS):
                            for d in range(2):
                                V = U[d]
                                dve.wait_ge(V.pe, pe0 + 5 + 2 * lv + (1 if lv else 0))
                                dve.tensor_tensor(V.y[:], two(V.b[2][:, 0:2 * P]), heads(levels[:, lv + 1, d, :]),
                                                  ALU.mult).then_inc(V.ev, 1)
                            for d in range(2):
                                V = U[d]
                                dve.wait_ge(V.pe, pe0 + 7 + 2 * lv)
                                if lv < LEVELS - 1:
                                    dve.tensor_tensor(V.tx.rearrange("p x h t -> p (x h t)"),
                                                      V.tx.rearrange("p x h t -> p (x h t)"), V.b[0][:],
                                                      ALU.subtract).then_inc(V.ev, 1)
                                else:
                                    dve.tensor_tensor(V.tx[:, 1], V.tx[:, 1], two(V.b[0][:, 2 * P:]),
                                                      ALU.subtract).then_inc(V.ev, 1)
                        for d in range(2):
                            V, c = U[d], cols(d, k)
                            dve.wait_ge(V.pe, pe0 + PE_U - 1)
                            oc = u[:, at(b, 1), c].rearrange("p a t -> p (a t)")
                            dve.tensor_tensor(oc, oc, V.b[3][:, 2 * P:3 * P], ALU.add).then_inc(V.ev, 1)
                            dve.wait_ge(V.pe, pe0 + PE_U)
                            dve.tensor_tensor(V.s[:], V.s[:], V.b[1][:, 0:P], ALU.add).then_inc(V.ev, 1)
                            dve.wait_ge(V.ev, ev0 + EV_U - 1)
                            ch = ORDER[d][k]
                            dve.scalar_tensor_tensor(V.s[:], V.s[:], wlast[:, d, ch:ch + 1], K.bd64, ALU.mult,
                                                     ALU.mult).then_inc(V.ev, 1)
                            dve.wait_ge(V.ev, ev0 + EV_U)


def even_out_phase(K, index, layer):
    nc, A, u = K.nc, K.A, K.u
    (seg,) = K.weights.phases[index]
    post_mods = [(sl, x, K.mod2_cols(layer, v, 2)) for v, (sl, x) in enumerate(((LAT, K.x), (CON, K.xc)))]
    G0, F0, Z0 = RB, 2 * RB, 2 * RB + 4
    NT, NL, NF = TOK // P, SEQ // P, 2
    with phase(K, *norm_names("post"), *SUB_SEMS, "four_in", "gates_in", "x_in", "tables", "zc_ps", "zc_ready",
               "mean_ps", "dev_ready", "dev_sq", "stat_ps", "gn_var", "gn_std", "gn_inv", "gn_scaled", "gn_out",
               "four_ps", "m_full", "m_hi", "m_ready") as S:
        K.norm_buffers(S, TOK)
        feat = S.sb("dft_feat", [P, 2 * P])
        lat = S.sb("dft_lat", [P, 2, NL, SEQ])
        con = S.sb("dft_con", [P, 2, NT - NL, CTX])
        mo = S.sb("m", [P, 2, DB, TOK], F32R)
        S.y = u
        wide = [S.psum(f"lat{i}", [P, 512]) for i in range(4)]
        narrow = [S.psum(f"con{i}", [P, 512]) for i in range(4)]
        pair = lambda i: [(wide[i][:], LAT), (narrow[i][:, 0:CTX], CON)]
        zc = u[:, Z0:Z0 + 4, :].rearrange("p b t -> p (b t)")
        var = [K.ssq, K.var]
        out_banks = lambda n: pair(n % 2)

        with nc.Block() as block:

            @block.sync
            def _(sp):
                sp.dma_start(u[:, F0:F0 + 4, :], K.late_dram[RB:RB + 4].rearrange("n p t -> p n t")).then_inc(S.four_in, 16)
                sp.dma_start(feat[:], A["dft_feat"]).then_inc(S.four_in, 16)
                sp.dma_start(u[:, G0:G0 + RB, :], K.late_dram[0:RB].rearrange("n p t -> p n t")).then_inc(S.gates_in, 16)
                for m in range(2):
                    sp.dma_start(lat[:, m], A["dft_lat"][m].rearrange("(t p) l -> p t l", p=P)).then_inc(S.tables, 16)
                    sp.dma_start(con[:, m], A["dft_ctx"][m].rearrange("(t p) l -> p t l", p=P)).then_inc(S.tables, 16)
                sp.dma_start(K.x[:], K.x_dram).then_inc(S.x_in, 16)
                weights_sp(sp, K, index)

            @block.gpsimd
            def _(pool):
                split_all(pool, K, [seg], [(DB,)])

            @block.scalar
            def _(act):
                for n in range(SPLIT):
                    split_hi(act, K, seg, n, n, 0, DB)
                for t in range(NT):
                    act.wait_ge(S.zc_ps, t + 1)
                    act.activation(zc[:, 512 * t:512 * t + 512], wide[t % 4][:], ACT.Copy).then_inc(S.zc_ready, 1)
                for i in range(RB + 3):
                    if i < RB:
                        act.wait_ge(S.dev_ready, i + 1)
                        if i >= 2:
                            act.wait_ge(S.stat_ps, i - 1)
                        act.activation(K.sq[:, i % 2, :], u[:, i, :], ACT.Square).then_inc(S.dev_sq, 1)
                    if 0 <= i - 1 < RB:
                        act.wait_ge(S.gn_var, i)
                        act.activation(var[(i - 1) % 2][:], var[(i - 1) % 2][:], ACT.Sqrt).then_inc(S.gn_std, 1)
                    j = i - 2
                    if 0 <= j < RB:
                        act.wait_ge(S.gn_scaled, j + 1)
                        act.activation(u[:, j, :], u[:, j, :], ACT.Identity, scale=K.pcol("lnx_g", RB)[:, j:j + 1],
                                       bias=K.pcol("lnx_b", RB)[:, j:j + 1]).then_inc(S.gn_out, 1)
                    j = i - 3
                    if 0 <= j < RB:
                        split_operand_act(act, S, j, u[:, j, :], mo[:, HI, j, :])
                for j in range(NF):
                    split_operand_act(act, S, RB + j, u[:, F0 + 2 + j, :], mo[:, HI, RB + j, :])
                out_act(act, K, S, seg, out_banks, TOK, SPLIT)

            @block.tensor
            def _(pe):
                pe.wait_ge(S.four_in, 32)
                for t in range(NT):
                    if t >= 4:
                        pe.wait_ge(S.zc_ready, t - 3)
                    for j in range(NF):
                        mm = pe.matmul(wide[t % 4][:, 256 * j:256 * j + 256], u[:, F0 + j, t * P:(t + 1) * P], feat[:],
                                       start=True, stop=True)
                    mm.then_inc(S.zc_ps, 1)

                def mean(i):
                    if i >= 2:
                        pe.wait_ge(S.dev_ready, i - 1)
                    for ps, sl in pair(i % 2):
                        mm = pe.matmul(ps, K.bd64, u[:, i, sl], start=True, stop=True)
                    mm.then_inc(S.mean_ps, 1)
                pe.wait_ge(S.zc_ready, NT)
                mean(0)
                mean(1)
                for i in range(RB):
                    pe.wait_ge(S.dev_sq, i + 1)
                    if i >= 2:
                        pe.wait_ge(S.gn_var, i - 1)
                    for ps, sl in pair(2 + i % 2):
                        mm = pe.matmul(ps, K.bd64, K.sq[:, i % 2, sl], start=True, stop=True)
                    mm.then_inc(S.stat_ps, 1)
                    if i + 2 < RB:
                        mean(i + 2)
                pe.wait_ge(S.tables, 64)
                for j in range(NF):
                    pe.wait_ge(S.gn_var, RB - 1 + j)
                    for (ps, _), tab, t0, n in zip(pair(2 + j), (lat, con), (0, NL), (NL, NT - NL)):
                        for t in range(n):
                            for m in range(2):
                                c0 = (t0 + t) * 512 + j * 256 + m * P
                                mm = pe.matmul(ps, zc[:, c0:c0 + P], tab[:, m, t, :], start=t == 0 and m == 0,
                                               stop=t == n - 1 and m == 1)
                    mm.then_inc(S.four_ps, 1)
                pe.wait_ge(S.dev_ready, RB)
                out_pe(pe, K, S, seg, mo, out_banks, S.m_ready)
                norm_pe(pe, S.post, K, wide[2:4], TOK)

            @block.vector
            def _(dve):
                for i in range(RB + 4):
                    if i < RB:
                        dve.wait_ge(S.mean_ps, i + 1)
                        for ps, sl in pair(i % 2):
                            ins = dve.scalar_tensor_tensor(u[:, i, sl], ps, -1.0 / 64, u[:, i, sl], ALU.mult, ALU.add)
                        ins.then_inc(S.dev_ready, 1)
                    j = i - 1
                    if 0 <= j < RB:
                        dve.wait_ge(S.stat_ps, j + 1)
                        if j >= 2:
                            dve.wait_ge(S.gn_scaled, j - 1)
                        for ps, sl in pair(2 + j % 2):
                            ins = dve.tensor_scalar(var[j % 2][:, sl], ps, 1.0 / 64, GN_EPS, ALU.mult, ALU.add)
                        ins.then_inc(S.gn_var, 1)
                    j = i - 2
                    if 0 <= j < RB:
                        dve.wait_ge(S.gn_std, j + 1)
                        dve.reciprocal(var[j % 2][:], var[j % 2][:]).then_inc(S.gn_inv, 1)
                        dve.wait_ge(S.gn_inv, j + 1)
                        dve.tensor_tensor(u[:, j, :], u[:, j, :], var[j % 2][:], ALU.mult).then_inc(S.gn_scaled, 1)
                    j = i - 3
                    if 0 <= j < RB:
                        dve.wait_ge(S.gn_out, j + 1)
                        dve.wait_ge(S.gates_in, 16)
                        dve.tensor_tensor(u[:, j, :], u[:, j, :], u[:, G0 + j, :], ALU.mult).then_inc(S.m_full, 1)
                    j = i - 4
                    if 0 <= j < RB:
                        split_operand_dve(dve, S, j, u[:, j, :], mo[:, HI, j, :], mo[:, LO, j, :])
                dve.wait_ge(S.four_in, 32)
                for j in range(NF):
                    gate = u[:, F0 + 2 + j, :]
                    dve.wait_ge(S.four_ps, j + 1)
                    for ps, sl in pair(2 + j):
                        ins = dve.tensor_tensor(gate[:, sl], ps, gate[:, sl], ALU.mult)
                    ins.then_inc(S.m_full, 1)
                for j in range(NF):
                    split_operand_dve(dve, S, RB + j, u[:, F0 + 2 + j, :], mo[:, HI, RB + j, :], mo[:, LO, RB + j, :])
                dve.wait_ge(S.x_in, 16)
                post_dve(dve, K, S, post_mods, K.pcol("norm_post_2", 2 * DB)[:, layer * DB:][:, 0:DB], None,
                         wide[2:4], after_pre=False)



HEADS = 8
RET_HEAD = D // HEADS
K_SCALE = RET_HEAD ** -0.5


def odd_in_phase(K, index, layer):
    nc, A = K.nc, K.A
    (seg,) = K.weights.phases[index]
    pre_mods = [(sl, x, K.mod2_cols(layer, v, 1), K.mod2_cols(layer, v, 0))
                for v, (sl, x) in enumerate(((LAT, K.x), (CON, K.xc)))]
    with phase(K, *norm_names("pre"), *SUB_SEMS, "tables", "q_copied", "k_copied", "v_copied", "gate_ready",
               "gate_out0", "gate_out1", "rot_ps", "turned", "steps") as S:
        K.norm_buffers(S, TOK)
        S.h = S.sb("h", [P, 2, DB, TOK], F32R)
        rope = S.sb("rope", [P, 2, SEQ])
        rot = S.sb("rot", [P, P])
        plain = S.sb("plain", [P, 2, SEQ])
        part = S.sb("part", [P, 2, SEQ])
        stage = S.sb("gate", [P, 2, SEQ])
        lat = [S.psum(f"lat{i}", [P, 512]) for i in range(4)]
        con = [S.psum(f"con{i}", [P, 512]) for i in range(2)]
        turn_ps = [S.psum(f"rot{i}", [P, 512]) for i in range(2)]
        gate_out = (S.gate_out0, S.gate_out1)
        outs = [[(lat[0][:], LAT)], [(lat[1][:], LAT), (con[0][:, 0:CTX], CON)],
                [(lat[2][:], LAT), (con[1][:, 0:CTX], CON)], [(lat[3][:], LAT)]]
        Q, KEY, V, G = range(4)

        with nc.Block() as block:

            @block.sync
            def _(sp):
                sp.dma_start(rope[:], A["rope"].rearrange("m p t -> p m t")).then_inc(S.tables, 16)
                sp.dma_start(rot[:], A["rot"]).then_inc(S.tables, 16)
                weights_sp(sp, K, index)

            @block.gpsimd
            def _(pool):
                split_all(pool, K, [seg], [(DB,) * 4])

            @block.scalar
            def _(act):
                for j in range(SPLIT):
                    split_hi(act, K, seg, 0, 0, j, DB)
                pre_act(act, K, S, pre_mods)

                def turn(i, s, last=False):
                    def ahead(j):
                        if j + SPLIT < 4:
                            split_hi(act, K, seg, i, s, j + SPLIT, DB)
                        elif not last:
                            split_hi(act, K, seg, i + 1, s + 1, j + SPLIT - 4, DB)
                    act.wait_ge(K.chunks_done, seg.base + 4 * i + Q + 1)
                    if s:
                        act.wait_ge(S.turned, 2 * i)
                    act.activation(plain[:, 0, :], lat[Q][:], ACT.Copy).then_inc(S.q_copied, 1)
                    ahead(Q)
                    act.wait_ge(K.chunks_done, seg.base + 4 * i + KEY + 1)
                    act.activation(plain[:, 1, :], lat[KEY][:], ACT.Copy, scale=K_SCALE).then_inc(S.k_copied, 1)
                    act.activation(K.k[:, at(i, 1), CON], con[0][:, 0:CTX], ACT.Copy, scale=K_SCALE).then_inc(S.k_copied, 1)
                    ahead(KEY)
                    act.wait_ge(K.chunks_done, seg.base + 4 * i + V + 1)
                    for ps, sl in outs[V]:
                        ins = act.activation(K.v[:, at(i, 1), sl], ps, ACT.Copy)
                    ins.then_inc(S.v_copied, 1)
                    ahead(V)
                    act.wait_ge(K.chunks_done, seg.base + 4 * i + G + 1)
                    if s >= 2:
                        act.wait_ge(gate_out[s % 2], (i - s % 2) * 8)
                    act.activation(stage[:, s % 2, :], lat[G][:], ACT.Silu).then_inc(S.gate_ready, 1)
                    ahead(G)
                    act.wait_ge(S.gate_ready, i + 1)
                    act.dma_start(K.gate_dram[at(i, 1)].rearrange("a p t -> p (a t)"),
                                  stage[:, s % 2, :]).then_inc(gate_out[s % 2], 16)
                turn(0, 0)
                turn(1, 1)
                loop(act, 2, HEADS - 2, 2, turn)
                turn(HEADS - 2, HEADS - 2)
                turn(HEADS - 1, HEADS - 1, last=True)
                for o in gate_out:
                    act.wait_ge(o, 16 * HEADS // 2)

            @block.tensor
            def _(pe):
                norm_pe(pe, S.pre, K, turn_ps, TOK)
                pe.wait_ge(S.tables, 32)

                def turn(i, s):
                    def project(j, read, count):
                        if s:
                            pe.wait_ge(read, count)
                        multiply(pe, K, seg, i, s, j, DB, outs[j], lambda p, k, sl: S.h[:, p, k, sl],
                                 before=(lambda k: pe.wait_ge(S.h_ready, k + 1)) if s == 0 and j == 0 else None)

                    def rotate(n, ready, count):
                        pe.wait_ge(ready, count)
                        pe.matmul(turn_ps[n][:], rot[:], plain[:, n, :], start=True, stop=True).then_inc(S.rot_ps, 1)
                    project(Q, S.q_copied, i)
                    project(KEY, S.k_copied, 2 * i)
                    rotate(0, S.q_copied, i + 1)
                    project(V, S.v_copied, i)
                    rotate(1, S.k_copied, 2 * i + 2)
                    project(G, S.gate_ready, i)
                turn(0, 0)
                turn(1, 1)
                loop(pe, 2, HEADS, 2, turn)

            @block.vector
            def _(dve):
                pre_dve(dve, K, S, pre_mods, K.pcol("norm_pre_2", 2 * DB)[:, layer * DB:][:, 0:DB], turn_ps)
                dve.wait_ge(S.tables, 32)

                def turn(i, s):
                    for n, dst in enumerate((K.q, K.k)):
                        dve.wait_ge(S.rot_ps, 2 * i + (n + 1))
                        one = dst[:, at(i, 1), LAT].rearrange("p a t -> p (a t)")
                        dve.tensor_tensor(one, plain[:, n, :], rope[:, 0, :], ALU.mult).then_inc(S.steps, 1)
                        dve.tensor_tensor(part[:, n, :], turn_ps[n][:], rope[:, 1, :], ALU.mult).then_inc(S.steps, 1)
                        dve.wait_ge(S.steps, i * 4 + (2 * n + 2))
                        dve.tensor_tensor(one, one, part[:, n, :], ALU.add).then_inc(S.turned, 1)
                loop(dve, 0, HEADS, 2, turn)


def odd_out_phase(K, index, layer):
    nc, A = K.nc, K.A
    (seg,) = K.weights.phases[index]
    post_mods = [(LAT, K.x, K.mod2_cols(layer, 0, 2))]
    NL, NT = SEQ // CH, TOK // CH
    ORDER = ((4, 5, 0, 1, 2), (5, 4, 3, 2, 1))
    with phase(K, *norm_names("post"), *SUB_SEMS, "logits", "tables", "lg", "steps", "decays", "made", "gate_in0",
               "gate_in1", "pe_a", "pe_kv", "pe_o", "pe_s", "act_a", "act_o", "act_std", "xi_ready", "sc_ready",
               "states", "var", "inv", "m_full", "m_hi", "m_ready") as S:
        K.norm_buffers(S, SEQ)
        S.y = K.q
        mo = S.sb("m", [P, 2, DB, SEQ], F32R)
        gates = S.sb("gates", [P, 2, SEQ])
        dmask = S.sb("decay_pairs", [P, HEADS, P])
        xi = S.sb("xi", [P, 2, HEADS, P])
        zeta = S.sb("zeta", [P, 2, HEADS])
        gch = S.sb("g_chunk", [P, 2, HEADS])
        lg = S.sb("log_decay", [P, 6, 2 * HEADS])
        vt = S.sb("v_tok", [P, NT, P])
        kz = S.sb("k_zeta", [P, 2, NT, P])
        qx = S.sb("q_xi", [P, 2, SEQ])
        sc = S.sb("scores", [P, SEQ])
        st = S.sb("states", [P, 2, NL, P])
        o = S.sb("o", [P, SEQ])
        tabs = K.sq.rearrange("p a t -> p (a t)")
        dist, pos, low, high = (tabs[:, a * P:b * P] for a, b in ((0, 1), (1, 3), (3, 4), (4, 5)))
        work = tabs[:, 5 * P:7 * P]
        b = [S.psum(f"b{i}", [P, 512]) for i in range(8)]
        v_ps, mix_ps, k_ps, sc_ps, o_ps, ss_ps = b[0], b[1], b[2], b[3], b[4], b[5]
        kv_ps = b[0:3]
        out_banks = lambda n: [(b[6 + n % 2][:], LAT)]
        gate_in = (S.gate_in0, S.gate_in1)

        def kv(d, n):
            c0 = (d * 5 + n) * P
            return kv_ps[c0 // 512][:, c0 % 512:c0 % 512 + P]

        with nc.Block() as block:

            @block.sync
            def _(sp):
                sp.dma_start(lg[:, 5, :], A["od_decay_logit_2"].rearrange("a d h -> a (d h)").broadcast_to(
                    [P, 2 * HEADS])).then_inc(S.logits, 16)
                for dst, src in ((dist, A["dist"]), (pos[:, 0:P], A["posrow"][0]), (pos[:, P:], A["posrow"][1]),
                                 (low, A["masks"][1]), (high, A["masks"][2])):
                    sp.dma_start(dst, src).then_inc(S.tables, 16)

                def turn(i, s):
                    if s >= 2:
                        sp.wait_ge(S.m_full, i - 1)
                    sp.dma_start(gates[:, s % 2, :], K.gate_dram[at(i, 1)].rearrange("a p t -> p (a t)")).then_inc(
                        gate_in[s % 2], 16)
                turn(0, 0)
                turn(1, 1)
                loop(sp, 2, HEADS, 2, turn)
                weights_sp(sp, K, index)

            @block.gpsimd
            def _(pool):
                def turn(i, s):
                    if s:
                        pool.wait_ge(S.pe_o, i)
                    else:
                        pool.wait_ge(S.decays, 4 * HEADS)
                    one = K.q[:, at(i, 1), :].rearrange("p a (c t) -> p (a c) t", t=CH)
                    for d in range(2):
                        pool.tensor_tensor(qx[:, d, :].rearrange("p (c t) -> p c t", t=CH), one,
                                           xi[:, d, at(i, 1), :].broadcast_to([P, NL, CH]), ALU.mult).then_inc(S.xi_ready, 1)
                turn(0, 0)
                loop(pool, 1, HEADS, 1, turn)
                split_all(pool, K, [seg], [(DB,)])

            @block.scalar
            def _(act):
                for n in range(SPLIT):
                    split_hi(act, K, seg, n, n, 0, DB)
                act.wait_ge(S.logits, 16)
                act.activation(lg[:, 0, :], lg[:, 5, :], ACT.Abs).then_inc(S.lg, 1)
                act.wait_ge(S.lg, 1)
                act.activation(lg[:, 1, :], lg[:, 0, :], ACT.Exp, scale=-1.0).then_inc(S.lg, 1)
                act.wait_ge(S.steps, LRU_SCALE_STEPS)
                act.wait_ge(S.tables, 80)
                for d in range(2):
                    rows = lg[:, 0, d * HEADS:(d + 1) * HEADS]
                    act.activation(gch[:, d, :], rows, ACT.Exp, scale=float(CH))
                    act.activation(zeta[:, d, :], rows, ACT.Exp, scale=(K.rpos, K.pos)[d])
                for h in range(HEADS):
                    for d in range(2):
                        act.activation(xi[:, d, h, :], pos[:, d * P:(d + 1) * P], ACT.Exp,
                                       scale=lg[:, 0, d * HEADS + h:d * HEADS + h + 1]).then_inc(S.decays, 1)
                    for d in range(2):
                        if h:
                            act.wait_ge(S.made, 2 * h)
                        act.activation(work[:, d * P:(d + 1) * P], dist, ACT.Exp,
                                       scale=lg[:, 0, d * HEADS + h:d * HEADS + h + 1]).then_inc(S.decays, 1)

                def first(i):
                    act.wait_ge(S.pe_a, 2 * i + 1)
                    act.activation(vt[:, 0:4, :].rearrange("p c d -> p (c d)"), v_ps[:], ACT.Copy)
                    act.activation(vt[:, 4:6, :].rearrange("p c d -> p (c d)"), mix_ps[:, 0:256], ACT.Copy)
                    for d in range(2):
                        col = zeta[:, d, at(i, 1)]
                        act.activation(kz[:, d, 0:4, :].rearrange("p c d -> p (c d)"), k_ps[:], ACT.Copy, scale=col)
                        ins = act.activation(kz[:, d, 4:6, :].rearrange("p c d -> p (c d)"), mix_ps[:, 256:512],
                                             ACT.Copy, scale=col)
                    ins.then_inc(S.act_a, 1)

                def second(i, first_head=False):
                    act.wait_ge(S.pe_o, i + 1)
                    if not first_head:
                        act.wait_ge(S.m_ready, i)
                    act.activation(o[:], o_ps[:], ACT.Copy).then_inc(S.act_o, 1)
                    act.activation(K.ssq[:], o_ps[:], ACT.Square).then_inc(S.act_o, 1)

                def third(i):
                    act.wait_ge(S.var, i + 1)
                    act.activation(K.var[:], K.var[:], ACT.Sqrt).then_inc(S.act_std, 1)
                    act.wait_ge(S.m_full, i + 1)
                    act.activation(mo[:, HI, at(i, 1), :], o[:], ACT.Copy).then_inc(S.m_hi, 1)

                first(0)
                second(0, True)

                def turn(i, s):
                    first(i)
                    third(i - 1)
                    second(i)
                loop(act, 1, HEADS, 1, turn)
                third(HEADS - 1)
                out_act(act, K, S, seg, out_banks, SEQ, SPLIT)

            @block.tensor
            def _(pe):
                def first(i):
                    if i:
                        pe.wait_ge(S.states, i)
                    one, key = K.v[:, at(i, 1), :], K.k[:, at(i, 1), :]
                    flat = lambda ap, c: ap.rearrange("p a t -> p (a t)")[:, c * CH:(c + 1) * CH]
                    for c in range(NT):
                        dv = v_ps[:, c * P:(c + 1) * P] if c < 4 else mix_ps[:, (c - 4) * P:(c - 3) * P]
                        dk = k_ps[:, c * P:(c + 1) * P] if c < 4 else mix_ps[:, (c - 2) * P:(c - 1) * P]
                        pe.transpose(dv, flat(one, c), K.ident)
                        mm = pe.transpose(dk, flat(key, c), K.ident)
                    mm.then_inc(S.pe_a, 1)
                    if i:
                        pe.wait_ge(S.sc_ready, i)
                    for c in range(NL):
                        mm = pe.matmul(sc_ps[:, c * P:(c + 1) * P], flat(key, c), flat(K.q[:, at(i, 1), :], c),
                                       start=True, stop=True)
                    mm.then_inc(S.pe_a, 1)

                def products(i):
                    pe.wait_ge(S.act_a, i + 1)
                    for d in range(2):
                        for n, c in enumerate(ORDER[d]):
                            mm = pe.matmul(kv(d, n), kz[:, d, c, :], vt[:, c, :], start=True, stop=True)
                    mm.then_inc(S.pe_kv, 1)

                def outputs(i):
                    pe.wait_ge(S.sc_ready, i + 1)
                    pe.wait_ge(S.xi_ready, 2 * i + 2)
                    pe.wait_ge(S.states, i + 1)
                    if i:
                        pe.wait_ge(S.act_o, 2 * i)
                    for c in range(NL):
                        out, cs = o_ps[:, c * P:(c + 1) * P], slice(c * CH, (c + 1) * CH)
                        pe.matmul(out, vt[:, c, :], sc[:, cs], start=True, stop=False)
                        pe.matmul(out, st[:, 0, c, :], qx[:, 0, cs], start=False, stop=False)
                        mm = pe.matmul(out, st[:, 1, c, :], qx[:, 1, cs], start=False, stop=True)
                    mm.then_inc(S.pe_o, 1)

                def sums(i):
                    pe.wait_ge(S.act_o, 2 * i + 2)
                    if i:
                        pe.wait_ge(S.var, i)
                    pe.matmul(ss_ps[:], K.ones, K.ssq[:], start=True, stop=True).then_inc(S.pe_s, 1)
                first(0)
                products(0)
                outputs(0)

                for i in range(1, HEADS):
                    first(i)
                    sums(i - 1)
                    products(i)
                    outputs(i)
                sums(HEADS - 1)
                out_pe(pe, K, S, seg, mo, out_banks, S.m_ready)
                norm_pe(pe, S.post, K, [ss_ps], SEQ)

            @block.vector
            def _(dve):
                steps = Steps(dve, S.steps)
                dve.wait_ge(S.lg, 2)
                lru_scale(dve, steps, lg[:, 5, :], [lg[:, q, :] for q in range(5)], lg[:, 0, :])
                assert steps.n == LRU_SCALE_STEPS
                dve.wait_ge(S.tables, 80)
                for h in range(HEADS):
                    for d in range(2):
                        dve.wait_ge(S.decays, 4 * h + 3 + d)
                        tri = (low, high)[d]
                        steps(dve.tensor_tensor(work[:, d * P:(d + 1) * P], work[:, d * P:(d + 1) * P], tri, ALU.mult))
                    dve.tensor_tensor(dmask[:, h, :], work[:, 0:P], work[:, P:], ALU.add).then_inc(S.made, 2)

                def first(i, first_head=False):
                    dve.wait_ge(S.pe_a, 2 * i + 2)
                    if not first_head:
                        dve.wait_ge(S.pe_o, i)
                    dve.tensor_tensor(sc.rearrange("p (c t) -> p c t", t=CH), sc_ps.rearrange("p (c t) -> p c t", t=CH),
                                      dmask[:, at(i, 1), :].broadcast_to([P, NL, CH]), ALU.mult).then_inc(S.sc_ready, 1)

                def chain(i):
                    dve.wait_ge(S.pe_kv, i + 1)
                    base = i * 8 + (LRU_SCALE_STEPS + 2 * HEADS)
                    chain_steps = Steps(dve, S.steps, base)
                    for d in range(2):
                        g = gch[:, d, at(i, 1)]
                        way = [0, 1, 2, 3] if d == 0 else [3, 2, 1, 0]
                        chain_steps(dve.tensor_copy(st[:, d, way[0], :], kv(d, 0)))
                        chain_steps(dve.scalar_tensor_tensor(st[:, d, way[0], :], st[:, d, way[0], :], g, kv(d, 1),
                                                             ALU.mult, ALU.add))
                        for n in range(1, NL):
                            ins = dve.scalar_tensor_tensor(st[:, d, way[n], :], st[:, d, way[n - 1], :], g, kv(d, n + 1),
                                                           ALU.mult, ALU.add)
                            if n < NL - 1:
                                chain_steps(ins)
                    ins.then_inc(S.states, 1)

                def norm(i):
                    dve.wait_ge(S.pe_s, i + 1)
                    dve.tensor_scalar(K.var[:], ss_ps[:], 1.0 / RET_HEAD, EPS, ALU.mult, ALU.add).then_inc(S.var, 1)

                def finish(i, s):
                    dve.wait_ge(S.act_std, i + 1)
                    dve.reciprocal(K.var[:], K.var[:]).then_inc(S.inv, 1)
                    dve.wait_ge(S.inv, 2 * i + 1)
                    dve.tensor_tensor(o[:], o[:], K.var[:], ALU.mult).then_inc(S.inv, 1)
                    dve.wait_ge(gate_in[s % 2], (i - s % 2) * 8 + 16)
                    dve.wait_ge(S.inv, 2 * i + 2)
                    dve.tensor_tensor(o[:], o[:], gates[:, s % 2, :], ALU.mult).then_inc(S.m_full, 1)
                    dve.wait_ge(S.m_hi, i + 1)
                    dve.tensor_tensor(mo[:, LO, at(i, 1), :], o[:], mo[:, HI, at(i, 1), :].bitcast(F32),
                                      ALU.subtract).then_inc(S.m_ready, 1)
                first(0, True)
                chain(0)

                def turn(i, s):
                    first(i)
                    norm(i - 1)
                    finish(i - 1, s - 1)
                    chain(i)
                loop(dve, 1, HEADS, 2, turn)
                norm(HEADS - 1)
                finish(HEADS - 1, HEADS - 1)
                post_dve(dve, K, S, post_mods, K.pcol("norm_post_2", 2 * DB)[:, layer * DB:][:, 0:DB], None,
                         [ss_ps], after_pre=False)



class AdaSource:

    def __init__(self, weights, first, use, bias, out):
        self.w = weights.rearrange("(k p) c -> p k c", p=P)
        self.first, self.use, self.vecs = first, use, len(use)
        self.bias_cols, self.out_cols = bias, out

    def __call__(self, i):
        return self.w[:, :, at((i + self.first) * ADA_W, ADA_W)]

    def bias(self, i):
        return self.bias_cols[:, at((i + self.first) * 2, 2)]

    def out(self, i):
        return lambda v: self.out_cols(v)[:, at((i + self.first) * 2, 2)]


def second_block(K, ctx, first):
    with ExitStack() as even:
        K.xc = K.sbuf(ctx, "x_context", [P, DB, CTX])
        K.u = K.sbuf(even, "u", [P, SHIFT_BLOCKS, TOK])
        run = [lambda: even_in_phase(K, first, 0), lambda: even_scan_phase(K), lambda: even_out_phase(K, first + 1, 0)]
        for f in run:
            f()
    K.q = K.sbuf(ctx, "q", [P, HEADS, SEQ])
    K.k = K.sbuf(ctx, "k", [P, HEADS, TOK])
    K.v = K.sbuf(ctx, "v", [P, HEADS, TOK])
    odd_in_phase(K, first + 2, 1)
    odd_out_phase(K, first + 3, 1)


def build(nc, A, out):
    with ExitStack() as ctx:
        K = Names(nc=nc, A=A, out=out, serial=0)

        def sbuf(c, name, shape, dt=F32):
            K.serial += 1
            return c.enter_context(nc.sbuf_tensor(f"{name}_{K.serial}", shape, dt))

        def psum(c, name, shape, dt=F32):
            K.serial += 1
            return c.enter_context(nc.psum_tensor(f"{name}_{K.serial}", shape, dt))

        K.sbuf, K.psum = sbuf, psum
        sb = lambda name, shape, dt=F32: sbuf(ctx, name, shape, dt)
        sem = lambda name: ctx.enter_context(nc.semaphore(name))

        K.pool_sem = sem

        K.x = sb("x", [P, DB, SEQ])
        K.raw = sb("w_raw", [P, RAW, DB, P])
        K.w_hi = sb("w_hi", [P, SPLIT, DB, P], F32R)
        K.w_lo = sb("w_lo", [P, SPLIT, DB, P], F32R)
        K.params = sb("params", [P, len(PARAM_PAGES) * P])
        K.const = sb("const", [P, CONST_W])
        K.mods = sb("mods", [P, 144])
        K.mods2 = sb("mods2", [P, 2, 48])
        K.cact = sb("c_act", [P, 3, DB])
        K.fac = sb("fac", [P, 2, DB])
        K.fac2 = sb("fac2", [P, 2, DB])

        def const(name):
            c0, n = CONST_COLS[name]
            return K.const[:, c0:c0 + n]
        K.ident, K.ones, K.bd64 = const("ident"), const("ones"), const("bd64")
        K.shift4, K.shift2, K.pos, K.rpos = const("shift4"), const("shift2"), const("pos"), const("rpos")

        def pcol(name, n):
            return K.params[:, PARAM_AT[name]:PARAM_AT[name] + n]
        K.pcol = pcol

        def mod_cols(layer, sub, kind):
            c0 = layer * 72 + (sub * 3 + kind) * DB
            return K.mods[:, c0:c0 + DB]
        K.mod_cols = mod_cols

        def mod2_cols(layer, v, kind):
            c0 = layer * 24 + kind * DB
            return K.mods2[:, v, c0:c0 + DB]
        K.mod2_cols = mod2_cols
        K.x_dram = nc.dram_tensor("x_wait", (P, DB, SEQ), F32, kind="Internal").ap()
        K.gate_dram = nc.dram_tensor("gate_wait", (HEADS, P, SEQ), F32, kind="Internal").ap()
        K.late_dram = nc.dram_tensor("late_wait", (EVEN_BLOCKS - SHIFT_BLOCKS, P, TOK), F32, kind="Internal").ap()

        def norm_buffers(S, width):
            K.sq = S.sb("sq", [P, 2, width])
            K.ssq = S.sb("ssq", [P, width])
            K.var = S.sb("var", [P, width])
        K.norm_buffers = norm_buffers

        K.landed = [sem(f"landed{i}") for i in range(RAW)]
        K.hi_ready, K.lo_ready, K.chunks_done = sem("hi_ready"), sem("lo_ready"), sem("chunks_done")
        K.ada_landed = [sem(f"ada_landed{i}") for i in range(ADA)]
        K.ada_used, K.ada_total = sem("ada_used"), sem("ada_total")
        K.local_n = 60
        local = [nc.alloc_semaphore(name=f"local{i}") for i in range(K.local_n)]
        K.local0 = local[0].num
        assert [h.num for h in local] == list(range(K.local0, K.local0 + K.local_n))
        for h in local:
            nc.release_semaphore(h)

        def rows(name):
            rows128 = lambda ap: ap.rearrange("(r c) -> r c", c=P)
            one = {
                "a_conv_b": "a_conv_b", "b_conv_b": "b_conv_b", "b_norm_g": "b_norm_g", "b_norm_b": "b_norm_b",
                "a_lam": "a_lam", "c_b_in": "c_b_in", "c_norm_g": "c_norm_g", "c_norm_b": "c_norm_b",
                "c": "c", "c_2": "c_2", "k_k": "ev_k_k_2", "k_a": "ev_k_a_2", "mu": "ev_mu_2",
                "lnx_g": "ev_lnx_g_2", "lnx_b": "ev_lnx_b_2",
            }
            two = {"norm_pre_2": "norm_pre_2", "norm_post_2": "norm_post_2", "ada_b_2": "ada_b_2"}
            if name in ("ada_b0", "ada_b1"):
                return [(0, 72, rows128(A["ada_b"][int(name[-1])]))]
            if name in one:
                src = rows128(A[one[name]][0])
            elif name in two:
                src = A[two[name]].rearrange("l (r c) -> (l r) c", c=P)
            elif name in ("norm_pre", "norm_post"):
                src = A[name].rearrange("l s (r c) -> (l s r) c", c=P)
            elif name == "c_ctx":
                src = rows128(A["c_ctx_2"])
            elif name in ("a_conv_w", "b_conv_w"):
                src = A[name][0].rearrange("k (r c) -> (k r) c", c=P)
            elif name in ("w0", "a0"):
                src = A[f"ev_{name}_2"][0].rearrange("d (r c) -> (d r) c", c=P)
            elif name == "r_k":
                src = A["ev_r_k_2"][0].rearrange("(r t) c -> r (t c)", t=2)
            else:
                g = {"gate_br": 0, "gate_bi": 64}[name]
                src = A["a_gate_b"][0].rearrange("(b t) e -> b t e", t=2)[:, :, g:g + 64]
            return [(0, src.shape[0], src)]
        K.rows = rows
        K.row_loads = sum(len(page) for page in PARAM_PAGES)

        def ada1(layer, first):
            return AdaSource(A["ada_w"][layer], first, (0,), pcol(f"ada_b{layer}", 72),
                             lambda v: K.mods[:, 72 * layer:72 * layer + 72])

        def ada2(layer, first):
            return AdaSource(A["ada_w_2"][layer], first, (1, 2), pcol("ada_b_2", 48)[:, 24 * layer:24 * layer + 24],
                             lambda v: K.mods2[:, v, 24 * layer:24 * layer + 24])
        K.ada_src = lambda layer, m: ada1(layer, 0)(m)

        W = K.weights = Weights()

        def columns(w):
            w = w.rearrange("(k p) c -> p k c", p=P)
            return lambda j: w[:, :, at(j * P, P)]

        def ffn_weights(layer, which, parts):
            up = columns(A["ffn_w13"][layer, which])
            down = A["ffn_w2"][layer, which].rearrange("(k p) c -> p k c", p=P)
            segs, t0 = [], 0
            for turns, ada in parts:
                segs.append((turns, [lambda i, t0=t0: up(i + t0), lambda i, t0=t0: up(i + (t0 + FB))], ada))
                t0 += turns
            segs.append((DB, [lambda n, a=a, b=b: down[:, a:b, at(n * P, P)]
                              for a, b in ((0, 8), (8, 16), (16, FB))], None))
            return segs

        def proj(w, first, n):
            w = columns(w)
            return (n, [lambda i: w(i + first)], None)

        ab = columns(A["ab_w_in"][0])
        W.add(*ffn_weights(0, 0, [(22, ada1(0, 10))]))
        W.add((4, [lambda i: ab(i + 8), lambda i: ab(i + 12)], None), proj(A["ab_w_in"][0], 4, 4),
              proj(A["ab_w_in"][0], 0, 4), proj(A["ab_w_out"][0], 0, DB))
        W.add(*ffn_weights(0, 1, [(4, ada1(0, 32)), (18, ada1(1, 0))]))
        W.add(*ffn_weights(1, 0, [(18, ada1(1, 18)), (4, ada2(0, 0))]))
        W.add(proj(A["c_w_in"][0], DB, DB), proj(A["c_w_in"][0], 0, DB), proj(A["c_w_out"][0], 0, DB))
        W.add(*ffn_weights(1, 1, [(8, ada2(0, 4)), (12, ada2(1, 0)), (2, None)]))
        first_even = len(W.phases)
        W.add(proj(A["ev_w_in_2"][0], 0, SHIFT_BLOCKS), proj(A["ev_w_in_2"][0], SHIFT_BLOCKS, EVEN_BLOCKS - SHIFT_BLOCKS))
        W.add(proj(A["ev_w_out_2"][0], 0, DB))
        odd = columns(A["od_w_in_2"][0])
        W.add((HEADS, [lambda i, j=j: odd(i + HEADS * j) for j in range(4)], None))
        W.add(proj(A["od_w_out_2"][0], 0, DB))

        K.ada_raw = None
        with ExitStack() as first:
            K.ada_raw = sbuf(first, "ada_raw", [P, ADA, DB, ADA_W])
            K.ada_acc = sbuf(first, "ada_acc", [P, 2, ADA_W])
            K.ada_dia = sbuf(first, "ada_dia", [P, 2, 2, P])
            K.ada_col = sbuf(first, "ada_col", [P, 2, 2])
            K.ada_ps = psum(first, "ada_sums", [P, 2, ADA_W])
            run = [lambda: start_phase(K), lambda: ffn_phase(K, 0, 0, 0, 0), lambda: mixer_ab_phase(K, 1, 0, 1),
                   lambda: ffn_phase(K, 2, 0, 2, 1), lambda: ffn_phase(K, 3, 1, 0, 0),
                   lambda: mixer_c_phase(K, 4, 1, 1), lambda: ffn_phase(K, 5, 1, 2, 1)]
            for f in run:
                f()
        second_block(K, ctx, first_even)
        output_phase(K)


NAMES = [
    "x", "c", "ada_w", "ada_b", "norm_pre", "norm_post", "ffn_w13", "ffn_w2", "ab_w_in", "a_conv_w", "a_conv_b",
    "a_gate_w", "a_gate_b", "a_lam", "b_conv_w", "b_conv_b", "b_norm_g", "b_norm_b", "ab_w_out", "c_w_in", "c_b_in",
    "c_norm_g", "c_norm_b", "c_w_s", "c_b_s", "c_w_out", "c_2", "ctx_2", "c_ctx_2", "ada_w_2", "ada_b_2",
    "norm_pre_2", "norm_post_2", "ev_w_in_2", "ev_mu_2", "ev_w0_2", "ev_w2_2", "ev_a0_2", "ev_a2_2", "ev_k_k_2",
    "ev_k_a_2", "ev_r_k_2", "ev_lnx_g_2", "ev_lnx_b_2", "ev_w_out_2", "od_w_in_2", "od_decay_logit_2", "od_w_out_2",
]


def kernel(**inputs):
    import concourse.bacc as bacc
    from concourse.bass_utils import run_bass_kernel_spmd

    nc = bacc.Bacc("TRN2", target_bir_lowering=False, num_devices=1)
    arrays, A = {}, {}
    for name, a in [*((n, inputs[n]) for n in NAMES), *constants().items()]:
        a = np.ascontiguousarray(a)
        arrays[f"in_{name}"] = a
        A[name] = nc.dram_tensor(f"in_{name}", a.shape, mybir.dt.from_np(a.dtype), kind="ExternalInput").ap()
    out = nc.dram_tensor("out_x", (1, SEQ, D), F32, kind="ExternalOutput").ap()
    build(nc, A, out)
    result = run_bass_kernel_spmd(nc, [arrays], core_ids=[0])
    return result.results[0]["out_x"]
```

```python
from contextlib import ExitStack, contextmanager

import numpy as np

import concourse.bass as bass
from concourse import mybir

F32 = mybir.dt.float32
F32R = mybir.dt.float32r
ALU = mybir.AluOpType
ACT = mybir.ActivationFunctionType
AX = mybir.AxisListType

P = 128
D = 1024
DB = D // P
SEQ = 512
CTX = 256
TOK = SEQ + CTX
LAT, CON = slice(0, SEQ), slice(SEQ, TOK)
D_FF = 2816
FB = D_FF // P
EPS = 1e-6
GN_EPS = 64e-5
NS = 3
GRID = 64
RW = 768
RB = RW // P
DECAY = float(np.exp(-0.5))
CH = 128
RAW = 4
SPLIT = 2
ADA = 1
ADA_W = 256
FIRST_ADA = 10
FIRST_SLOTS = 3
HI, LO = 0, 1
PASSES = ((HI, HI), (HI, LO), (LO, HI))



class Names:

    def __init__(self, **values):
        self.values = values

    def __getattr__(self, name):
        return self.values[name]


def loop(eng, lo, hi, step, body):
    turns = (hi - lo) // step
    if turns >= 2:
        with eng.Fori(0, turns) as t:
            for u in range(step):
                body(t * step + (lo + u), lo + u)
        lo += turns * step
    for i in range(lo, hi):
        body(i, i)


def at(i, n):
    return bass.ds(i, n)


class Steps:

    def __init__(self, eng, sem, base=0):
        self.eng, self.sem, self.base, self.n = eng, sem, base, 0

    def __call__(self, ins):
        self.n += 1
        ins.then_inc(self.sem, 1)
        self.eng.wait_ge(self.sem, self.base + self.n)


PARAM_PAGES = [
    [("ada_b0", 72), ("norm_pre", 48), ("c", 8)],
    [("ada_b1", 72), ("norm_post", 48), ("c_2", 8)],
    [("b_conv_w", 124), ("a_lam", 4)],
    [("a_conv_b", 4), ("a_conv_w", 16), ("b_conv_b", 4), ("b_norm_g", 4), ("b_norm_b", 4),
     ("gate_br", 4), ("gate_bi", 4), ("c_b_in", 16), ("c_norm_g", 8), ("c_norm_b", 8), ("c_ctx", 8),
     ("norm_pre_2", 16), ("norm_post_2", 16), ("k_k", 6), ("k_a", 6)],
    [("ada_b_2", 48), ("mu", 20), ("w0", 12), ("a0", 12), ("r_k", 6), ("lnx_g", 6), ("lnx_b", 6)],
]
PARAM_AT = {}
for _page, _rows in enumerate(PARAM_PAGES):
    _r = 0
    for _name, _n in _rows:
        PARAM_AT[_name] = _page * P + _r
        _r += _n
    assert _r <= P

CONST_COLS = {"ident": (0, 128), "ones": (128, 128), "bd64": (256, 128), "shift4": (384, 4),
              "shift2": (388, 2), "pos": (390, 1), "rpos": (391, 1)}
CONST_W = 392


def constants():
    i = np.arange(P)
    c = np.zeros((P, CONST_W), np.float32)
    c[:, 0:128] = np.eye(P)
    c[:, 128:256] = 1.0
    c[:, 256:384] = (i[:, None] // 64) == (i[None, :] // 64)
    c[:, 384:388] = (i[:, None] % 4) == np.arange(4)[None, :]
    c[:, 388:390] = (i[:, None] % 2) == np.arange(2)[None, :]
    c[:, 390] = i
    c[:, 391] = P - 1 - i
    su = (i[:, None] < i[None, :]).astype(np.float32)
    iu = (i[:, None] <= i[None, :]).astype(np.float32)
    masks = np.stack([su, iu, su.T, iu.T]).astype(np.float32)
    levels = []
    for n in (1, 2, 4, 8, 16, 32, 64):
        same = (i[:, None] // (2 * n)) == (i[None, :] // (2 * n))
        m = same & ((i[:, None] // n) % 2 == 1) & ((i[None, :] // n) % 2 == 0)
        levels += [m, m.T]
    levels = np.stack(levels).astype(np.float32)
    dist = np.abs(i[:, None] - i[None, :]).astype(np.float32)
    def dft(n):
        a = 2 * np.pi * np.outer(np.arange(n), np.arange(n)) / n
        return np.cos(a), np.sin(a)
    c64, s64 = dft(64)
    feat = np.zeros((P, 256))
    for g in range(2):
        feat[64 * g:64 * g + 64, 64 * g:64 * g + 64] = c64
        feat[64 * g:64 * g + 64, 128 + 64 * g:128 + 64 * g + 64] = s64
    time = []
    for n in (CTX, SEQ):
        cn, sn = dft(n)
        time.append((np.stack([cn, -sn]) / np.sqrt(n * 64.0)).astype(np.float32))
    half = 64
    tok = np.arange(SEQ)
    rc = np.stack([tok // GRID, tok % GRID], -1).astype(np.float32)
    inv = (np.float32(10000.0) ** (-np.arange(0, half, 2, dtype=np.float32) / half)).astype(np.float32)
    ang = (rc[:, :, None] * inv).astype(np.float32).reshape(SEQ, half).T
    cos, sin = np.cos(ang), np.sin(ang)
    rope = np.stack([np.concatenate([cos, cos]), np.concatenate([sin, sin])]).astype(np.float32)
    rot = np.zeros((P, P), np.float32)
    for d in range(half):
        rot[half + d, d] = -1.0
        rot[d, half + d] = 1.0
    posrow = np.stack([np.broadcast_to(i + 1.0, (P, P)), np.broadcast_to(P - i + 0.0, (P, P))])
    return {
        "const": c, "masks": masks, "levels": levels, "dist": dist,
        "dft_feat": feat.astype(np.float32), "dft_ctx": time[0], "dft_lat": time[1],
        "rope": rope, "rot": rot, "posrow": posrow.astype(np.float32),
    }



class Weights:

    def __init__(self):
        self.phases, self.total = [], 0

    def add(self, *segments):
        phase, n = [], self.total
        ada_before = sum(s.n for p in self.phases for s in p if s.ada)
        for turns, sources, ada in segments:
            phase.append(Names(n=turns, sources=sources, per=len(sources), base=n,
                                         ada=ada, ada_base=FIRST_ADA + ada_before))
            n += turns * len(sources)
            ada_before += turns if ada else 0
        self.total = n
        self.phases.append(phase)
        return phase


def load_ada(sp, K, seg, i, s):
    m, slot = seg.ada_base + i, (seg.ada_base + s) % ADA
    sp.wait_ge(K.ada_used, m - (ADA - 1))
    sp.dma_start(K.ada_raw[:, slot], seg.ada(i)).then_inc(K.ada_landed[slot], 16)


def load_turn(sp, K, seg, i, s):
    for j, source in enumerate(seg.sources):
        n, first = seg.base + seg.per * i + j, seg.base + seg.per * s + j
        if first >= RAW:
            sp.wait_ge(K.lo_ready, n - (RAW - 1))
        src = source(i)
        sp.dma_start(K.raw[:, first % RAW, 0:src.shape[1], :], src).then_inc(K.landed[first % RAW], 16)


def load_ahead(sp, K, phase):
    seg = phase[0]
    for i in range(RAW // seg.per):
        load_turn(sp, K, seg, i, i)
    if seg.ada:
        load_ada(sp, K, seg, 0, 0)


def weights_sp(sp, K, index):
    for k, seg in enumerate(K.weights.phases[index]):
        out = RAW // seg.per if k == 0 else 0
        if seg.ada:
            for i in range(1, out):
                load_ada(sp, K, seg, i, i)

        def turn(i, s, seg=seg):
            load_turn(sp, K, seg, i, s)
            if seg.ada:
                load_ada(sp, K, seg, i, s)
        loop(sp, out, seg.n, RAW // int(np.gcd(RAW, seg.per)), turn)
    if index + 1 < len(K.weights.phases):
        load_ahead(sp, K, K.weights.phases[index + 1])


def landed_value(seg, i, s, j):
    first = (seg.base + seg.per * s + j) // RAW + 1
    if isinstance(i, int):
        return 16 * first
    return (seg.base + seg.per * i + j - (seg.base + seg.per * s + j) % RAW) * (16 // RAW) + 16


def split_hi(act, K, seg, i, s, j, tiles):
    n, first = seg.base + seg.per * i + j, seg.base + seg.per * s + j
    act.wait_ge(K.landed[first % RAW], landed_value(seg, i, s, j))
    if first >= SPLIT:
        act.wait_ge(K.chunks_done, n - (SPLIT - 1))
    act.activation(K.w_hi[:, first % SPLIT, 0:tiles, :], K.raw[:, first % RAW, 0:tiles, :],
                   ACT.Copy).then_inc(K.hi_ready, 1)


def split_lo(pool, K, seg, i, s, j, tiles):
    n, first = seg.base + seg.per * i + j, seg.base + seg.per * s + j
    pool.wait_ge(K.hi_ready, n + 1)
    pool.tensor_tensor(K.w_lo[:, first % SPLIT, 0:tiles, :], K.raw[:, first % RAW, 0:tiles, :],
                       K.w_hi[:, first % SPLIT, 0:tiles, :].bitcast(F32),
                       ALU.subtract).then_inc(K.lo_ready, 1)


def split_all(pool, K, phase, tiles):
    for seg, counts in zip(phase, tiles):
        step = RAW // int(np.gcd(RAW, seg.per))

        def body(i, s, seg=seg, counts=counts):
            for j in range(seg.per):
                split_lo(pool, K, seg, i, s, j, counts[j])
        loop(pool, 0, seg.n, step, body)


def multiply(pe, K, seg, i, s, j, tiles, outs, moving, first=True, last=True, before=None):
    n, slot = seg.base + seg.per * i + j, (seg.base + seg.per * s + j) % SPLIT
    pe.wait_ge(K.lo_ready, n + 1)
    for k in range(tiles):
        if before:
            before(k)
        for p, (wp, ap) in enumerate(PASSES):
            w = (K.w_hi, K.w_lo)[wp]
            for out, tokens in outs:
                mm = pe.matmul(out, w[:, slot, k, :], moving(ap, k, tokens),
                               start=first and k == 0 and p == 0,
                               stop=last and k == tiles - 1 and p == len(PASSES) - 1)
    mm.then_inc(K.chunks_done, 1)



NORM_SEMS = ("sq_ready", "ssq_added", "ssq_done", "var_ready", "std_ready", "rstd_ready", "spread")


def squares_act(act, N, K, b, parts):
    if b >= 2:
        act.wait_ge(N.ssq_added, b - 1)
    for src, sl in parts:
        ins = act.activation(K.sq[:, b % 2, sl], src, ACT.Square)
    ins.then_inc(N.sq_ready, 1)


def squares_dve(dve, N, K, b, width):
    if b == 0:
        return
    dve.wait_ge(N.sq_ready, b + 1)
    if b == 1:
        dve.tensor_tensor(K.ssq[:, 0:width], K.sq[:, 0, 0:width], K.sq[:, 1, 0:width],
                          ALU.add).then_inc(N.ssq_added, 2)
    else:
        dve.wait_ge(N.ssq_added, b)
        dve.tensor_tensor(K.ssq[:, 0:width], K.ssq[:, 0:width], K.sq[:, b % 2, 0:width],
                          ALU.add).then_inc(N.ssq_added, 1)


def norm_pe(pe, N, K, banks, width, carried=False):
    if not carried:
        pe.wait_ge(N.ssq_added, DB)
        for c in range(width // P):
            mm = pe.matmul(banks[0][:, c:c + 1], K.ssq[:, c * P:(c + 1) * P], K.ones[:, 0:1], start=True, stop=True)
        mm.then_inc(N.ssq_done, 1)
        pe.wait_ge(N.rstd_ready, 1)
    for c in range(width // P):
        mm = pe.matmul(banks[c // 4][:, (c % 4) * P:(c % 4 + 1) * P], K.rstd[:, c:c + 1].broadcast_to([P, P]), K.ident,
                       start=True, stop=True)
    mm.then_inc(N.spread, 1)


def norm_act(act, N, K, width):
    act.wait_ge(N.var_ready, 1)
    act.activation(K.rstd[:, 0:width // P], K.rstd[:, 0:width // P], ACT.Sqrt).then_inc(N.std_ready, 1)


def norm_dve(dve, N, K, banks, width, carried=False):
    if not carried:
        factors = K.rstd[:, 0:width // P]
        dve.wait_ge(N.ssq_done, 1)
        dve.tensor_scalar(factors, banks[0][:, 0:width // P], 1.0 / D, EPS, ALU.mult, ALU.add).then_inc(N.var_ready, 1)
        dve.wait_ge(N.std_ready, 1)
        dve.reciprocal(factors, factors).then_inc(N.rstd_ready, 1)
    dve.wait_ge(N.spread, 1)


def spread_factors(banks, sl):
    return banks[sl.start // 512][:, 0:sl.stop - sl.start]



def width_of(mods):
    return sum(m[0].stop - m[0].start for m in mods)


def pre_act(act, K, S, mods, carried=False):
    if not carried:
        for b in range(DB):
            squares_act(act, S.pre, K, b, [(x[:, b, :], sl) for sl, x, _, _ in mods])
        norm_act(act, S.pre, K, width_of(mods))
    for b in range(DB):
        act.wait_ge(S.scaled, b + 1)
        for sl, _, _, shift in mods:
            ins = act.activation(S.h[:, HI, b, sl], K.sq[:, b % 2, sl], ACT.Identity,
                                 bias=shift[:, b:b + 1])
        ins.then_inc(S.h_hi, 1)


def pre_dve(dve, K, S, mods, gain, banks, carried=False):
    width = width_of(mods)
    for n, (_, _, scale, _) in enumerate(mods):
        ins = dve.scalar_tensor_tensor(K.fac[:, n], scale, 1.0, gain, ALU.add, ALU.mult)
        ins.then_inc(S.fac_ready, 1)
    if not carried:
        for b in range(DB):
            squares_dve(dve, S.pre, K, b, width)
    norm_dve(dve, S.pre, K, banks, width, carried)
    dve.wait_ge(S.fac_ready, len(mods))

    def low(b):
        dve.wait_ge(S.h_hi, b + 1)
        for sl, _, _, shift in mods:
            ins = dve.scalar_tensor_tensor(S.h[:, LO, b, sl], K.sq[:, b % 2, sl], shift[:, b:b + 1],
                                           S.h[:, HI, b, sl].bitcast(F32), ALU.add, ALU.subtract)
        ins.then_inc(S.h_ready, 1)

    for b in range(DB):
        if b >= 2:
            dve.wait_ge(S.h_ready, b - 1)
        for n, (sl, x, _, _) in enumerate(mods):
            ins = dve.scalar_tensor_tensor(K.sq[:, b % 2, sl], x[:, b, :], K.fac[:, n, b:b + 1],
                                           spread_factors(banks, sl), ALU.mult, ALU.mult)
        ins.then_inc(S.scaled, 1)
        if b >= 1:
            low(b - 1)
    low(DB - 1)



def post_act_block(act, K, S, n, s, parts, width):
    for ps, sl in parts:
        ins = act.activation(S.y[:, at(n, 1), sl], ps, ACT.Copy)
    ins.then_inc(S.y_ready, 1)
    if s >= 2:
        act.wait_ge(S.post.ssq_added, n - 1)
    for ps, sl in parts:
        ins = act.activation(K.sq[:, s % 2, sl], ps, ACT.Square)
    ins.then_inc(S.post.sq_ready, 1)


def post_dve(dve, K, S, mods, gain, res, banks, after_pre=True):
    width = width_of(mods)
    for n, (_, _, gate) in enumerate(mods):
        dve.tensor_scalar(K.fac2[:, n], gate, 1.0 if res is not None else 0.0, res or 1.0, ALU.add,
                          ALU.mult).then_inc(S.fac_ready, 1)
    first, scaled = (len(mods), DB) if after_pre else (0, 0)
    dve.wait_ge(S.fac_ready, first + len(mods))
    for n, _ in enumerate(mods):
        dve.tensor_tensor(K.fac[:, n], K.fac2[:, n], gain, ALU.mult).then_inc(S.fac_ready, 1)
    for b in range(DB):
        squares_dve(dve, S.post, K, b, width)
    norm_dve(dve, S.post, K, banks, width)
    dve.wait_ge(S.fac_ready, first + 2 * len(mods))
    dve.wait_ge(S.y_ready, DB)

    for b in range(DB):
        if b >= 2:
            dve.wait_ge((S.x_even, S.x_odd)[b % 2], b // 2)
        for n, (sl, _, _) in enumerate(mods):
            ins = dve.scalar_tensor_tensor(K.sq[:, b % 2, sl], S.y[:, b, sl], K.fac[:, n, b:b + 1],
                                           spread_factors(banks, sl), ALU.mult, ALU.mult)
        ins.then_inc(S.scaled, 1)
        if b % 2:
            dve.wait_ge(S.scaled, scaled + b)
            for sl, x, _ in mods:
                ins = dve.tensor_tensor(x[:, b - 1, :], x[:, b - 1, :], K.sq[:, 0, sl], ALU.add)
            ins.then_inc(S.x_even, 1)


def post_pool(pool, K, S, mods, after_pre=True):
    for b in range(1, DB, 2):
        pool.wait_ge(S.scaled, (DB if after_pre else 0) + b + 1)
        for sl, x, _ in mods:
            ins = pool.tensor_tensor(x[:, b, :], x[:, b, :], K.sq[:, 1, sl], ALU.add)
        ins.then_inc(S.x_odd, 1)



CARRY_SEMS = ("carry.sq", "carry.sum", "carry.var", "carry.std")


def carry_act(act, K, S, mods):
    width = width_of(mods)
    for b in range(DB):
        act.wait_ge((S.x_even, S.x_odd)[b % 2], b // 2 + 1)
        for sl, x, _ in mods:
            ins = act.activation(S.y[:, b, sl], x[:, b, :], ACT.Square)
        ins.then_inc(S.carry.sq, 1)
    act.wait_ge(S.carry.var, 1)
    act.activation(K.rstd[:, 0:width // P], K.rstd[:, 0:width // P], ACT.Sqrt).then_inc(S.carry.std, 1)


def carry_pe(pe, K, S, bank, width):
    for b in range(DB):
        pe.wait_ge(S.carry.sq, b + 1)
        for c in range(width // P):
            mm = pe.matmul(bank[:, c:c + 1], S.y[:, b, c * P:(c + 1) * P], K.ones[:, 0:1], start=b == 0 and c == 0,
                           stop=b == DB - 1 and c == width // P - 1)
    mm.then_inc(S.carry.sum, 1)


def carry_dve(dve, K, S, bank, width):
    factors = K.rstd[:, 0:width // P]
    dve.wait_ge(S.carry.sum, 1)
    dve.tensor_scalar(factors, bank[:, 0:width // P], 1.0 / D, EPS, ALU.mult, ALU.add).then_inc(S.carry.var, 1)
    dve.wait_ge(S.carry.std, 1)
    dve.reciprocal(factors, factors)


SUB_SEMS = ("scaled", "h_hi", "h_ready", "fac_ready", "y_ready", "x_even", "x_odd")


@contextmanager
def phase(K, *names):
    nc = K.nc
    with ExitStack() as ctx:
        S = Names()
        assert len(names) <= K.local_n, len(names)
        for k, name in enumerate(names):
            K.serial += 1
            h = ctx.enter_context(nc.semaphore(f"{name.replace('.', '_')}_{K.serial}", num=K.local0 + k))
            if "." in name:
                group, field = name.split(".")
                S.values.setdefault(group, Names()).values[field] = h
            else:
                S.values[name] = h
        S.sb = lambda name, shape, dt=F32: K.sbuf(ctx, name, shape, dt)
        S.psum = lambda name, shape, dt=F32: K.psum(ctx, name, shape, dt)
        yield S
    nc.all_engine_barrier(sems_to_clear=range(K.local0, K.local0 + K.local_n))


def norm_names(group):
    return tuple(f"{group}.{n}" for n in NORM_SEMS)



def ada_sum(dve, K, steps, m, vecs, raw=None, acc=None):
    if raw is None:
        dve.wait_ge(K.ada_landed[0], 16 * (m - FIRST_ADA) + 16)
        raw, acc = K.ada_raw[:, 0], K.ada_acc
    for v, vec in enumerate(vecs):
        out = acc[:, v, :]
        for k in range(DB):
            col = K.cact[:, vec, k:k + 1]
            if k == 0:
                ins = dve.tensor_scalar(out, raw[:, k, :], col, None, ALU.mult)
            else:
                ins = dve.scalar_tensor_tensor(out, raw[:, k, :], col, out, ALU.mult, ALU.add)
            if v == len(vecs) - 1 and k == DB - 1:
                ins.then_inc(K.ada_used, 1)
            else:
                steps(ins)


def ada_pe(pe, K, m, nv, acc=None, out=None):
    pe.wait_ge(K.ada_used, m + 1)
    for v in range(nv):
        mm = pe.matmul(K.ada_ps[:, v, :] if out is None else out, K.ones, K.ada_acc[:, v, :] if acc is None else acc,
                       start=True, stop=True)
    mm.then_inc(K.ada_total, 1)


def ada_columns(dve, K, steps, m, bias, out, nv, ps=None):
    dve.wait_ge(K.ada_total, m + 1)
    ident = K.ident.rearrange("p (a c) -> p a c", a=1).broadcast_to([P, 2, P])
    for v in range(nv):
        dia = K.ada_dia[:, v]
        steps(dve.tensor_tensor(dia, (K.ada_ps[:, v, :] if ps is None else ps).rearrange("p (a c) -> p a c", a=2), ident, ALU.mult))
        steps(dve.tensor_reduce(K.ada_col[:, v, :], dia, AX.X, ALU.add))
    for v in range(nv):
        ins = dve.tensor_tensor(out(v), K.ada_col[:, v, :], bias, ALU.add)
    steps(ins)


def ada_ops(nv):
    return nv * DB - 1 + 2 * nv + 1


def start_phase(K):
    nc, A = K.nc, K.A
    with phase(K, "const_in", "x_in", "turned", "copied", "silu_ready", "steps", "stored",
               *(f"first_landed{i}" for i in range(FIRST_SLOTS))) as S:
        S.rows_in = K.pool_sem("rows_in")
        xin = S.sb("x_in", [P, SEQ // P, D])
        first_raw = S.sb("first_ada", [P, FIRST_SLOTS, DB, ADA_W])
        first_landed = (S.first_landed0, S.first_landed1, S.first_landed2)
        rows = S.sb("param_rows", [P, len(PARAM_PAGES), P])
        ps = [S.psum(f"turn{i}", [P, 512]) for i in range(4)]
        pages = len(PARAM_PAGES)
        used = [sum(n for _, n in page) for page in PARAM_PAGES]
        with nc.Block() as block:

            @block.sync
            def _(sp):
                sp.dma_start(K.const[:], A["const"]).then_inc(S.const_in, 16)
                for m in range(FIRST_ADA):
                    slot = m % FIRST_SLOTS
                    if m >= FIRST_SLOTS:
                        sp.wait_ge(K.ada_used, m - FIRST_SLOTS + 1)
                    sp.dma_start(first_raw[:, slot], K.ada_src(0, m)).then_inc(first_landed[slot], 16)
                load_ahead(sp, K, K.weights.phases[0])

            @block.scalar
            def _(act):
                act.dma_start(xin[:], A["x"].rearrange("a (t p) d -> p (a t) d", p=P)).then_inc(S.x_in, 16)
                act.wait_ge(S.copied, pages)
                for v, name in enumerate(("c", "c_2", "c_ctx")):
                    act.activation(K.cact[:, v, :], K.pcol(name, DB), ACT.Silu).then_inc(S.silu_ready, 1)

            @block.gpsimd
            def _(pool):
                for page, entries in enumerate(PARAM_PAGES):
                    r = 0
                    for name, n in entries:
                        for r0, nr, src in K.rows(name):
                            dst = rows[r + r0:r + r0 + nr, page, :]
                            if len(src.shape) == 3:
                                dst = dst.rearrange("p (a c) -> p a c", a=src.shape[1])
                            pool.dma_start(dst, src).then_inc(S.rows_in, 16)
                        r += n

            @block.tensor
            def _(pe):
                pe.wait_ge(S.const_in, 16)
                pe.wait_ge(S.rows_in, 16 * K.row_loads)
                for page in range(pages):
                    if page >= 4:
                        pe.wait_ge(S.copied, page - 3)
                    pe.transpose(ps[page % 4][:, 0:used[page]], rows[0:used[page], page, :],
                                 K.ident[0:used[page], 0:used[page]]).then_inc(S.turned, 1)
                pe.wait_ge(S.x_in, 16)
                for b in range(DB):
                    n = pages + b
                    pe.wait_ge(S.copied, n - 3)
                    for t in range(SEQ // P):
                        mm = pe.transpose(ps[n % 4][:, t * P:(t + 1) * P], xin[:, t, b * P:(b + 1) * P], K.ident)
                    mm.then_inc(S.turned, 1)
                for m in range(FIRST_ADA):
                    ada_pe(pe, K, m, 1, acc=K.ada_acc[:, m % 2, :], out=ps[m % 2][:, 0:ADA_W])

            @block.vector
            def _(dve):
                for page in range(pages):
                    dve.wait_ge(S.turned, page + 1)
                    dve.tensor_copy(K.params[:, page * P:page * P + used[page]],
                                    ps[page % 4][:, 0:used[page]]).then_inc(S.copied, 1)
                for b in range(DB):
                    n = pages + b
                    dve.wait_ge(S.turned, n + 1)
                    dve.tensor_copy(K.x[:, b, :], ps[n % 4][:]).then_inc(S.copied, 1)
                dve.wait_ge(S.silu_ready, 3)
                dve.wait_ge(S.copied, pages + DB)
                steps = Steps(dve, S.steps)

                def columns(m):
                    ada_columns(dve, K, steps, m, K.pcol("ada_b0", 72)[:, 2 * m:2 * m + 2],
                                lambda v: K.mods[:, 2 * m:2 * m + 2], 1, ps[m % 2][:, 0:ADA_W])
                for m in range(FIRST_ADA):
                    dve.wait_ge(first_landed[m % FIRST_SLOTS], 16 * (m // FIRST_SLOTS) + 16)
                    ada_sum(dve, K, steps, m, (0,), first_raw[:, m % FIRST_SLOTS], K.ada_acc[:, m % 2:m % 2 + 1])
                    if m:
                        columns(m - 1)
                columns(FIRST_ADA - 1)



def ffn_phase(K, index, layer, sub, which, carried=True, carry=True):
    nc, A = K.nc, K.A
    seg = K.weights.phases[index]
    up, down = seg[:-1], seg[-1]
    u0 = up[0]
    shift, scale, gate = (K.mod_cols(layer, sub, kind) for kind in range(3))
    pre_mods = [(LAT, K.x, scale, shift)]
    post_mods = [(LAT, K.x, gate)]
    tiles = (8, 8, FB - 16)
    with phase(K, *norm_names("pre"), *norm_names("post"), *SUB_SEMS, *CARRY_SEMS, "silu_ready", "prod_ready",
               "hid_hi", "hid_ready", "steps") as S:
        hid = S.sb("hid", [P, 2, FB, SEQ], F32R)
        sil = S.sb("sil", [P, 2, SEQ])
        prod = S.sb("prod", [P, 2, SEQ])
        K.norm_buffers(S, SEQ)
        with ExitStack() as c:
            S.h = K.sbuf(c, "h", [P, 2, DB, SEQ], F32R)
        S.y = S.sb("y", [P, DB, SEQ])
        banks = [S.psum(f"acc{i}", [P, 512]) for i in range(4)]
        sums = [S.psum("sums", [P, 512])]
        with nc.Block() as block:

            @block.sync
            def _(sp):
                weights_sp(sp, K, index)

            @block.gpsimd
            def _(pool):
                split_all(pool, K, [Names(n=FB, per=2, base=u0.base), down], [(8, 8), tiles])
                post_pool(pool, K, S, post_mods)

            @block.scalar
            def _(act):
                def split_up(i, s):
                    for j in range(2):
                        split_hi(act, K, u0, i, s, j, 8)

                def hidden(i, s):
                    act.wait_ge(K.chunks_done, u0.base + 2 * i + 1)
                    if s >= 2:
                        act.wait_ge(S.prod_ready, i - 1)
                    act.activation(sil[:, s % 2, :], banks[2 * (s % 2)][:], ACT.Silu).then_inc(S.silu_ready, 1)
                    act.wait_ge(S.prod_ready, i + 1)
                    act.activation(hid[:, HI, at(i, 1), :], prod[:, s % 2, :], ACT.Copy).then_inc(S.hid_hi, 1)

                split_up(0, 0)
                pre_act(act, K, S, pre_mods, carried)

                def turn(i, s):
                    split_up(i + 1, s + 1)
                    hidden(i, s)
                turn(0, 0)
                turn(1, 1)
                loop(act, 2, FB - 1, 2, turn)
                split_hi(act, K, down, 0, 0, 0, tiles[0])
                hidden(FB - 1, FB - 1)
                for n in range(DB):
                    for j in range(3):
                        if n + j > 0:
                            split_hi(act, K, down, n, n, j, tiles[j])
                    if n:
                        act.wait_ge(K.chunks_done, down.base + 3 * n)
                        post_act_block(act, K, S, n - 1, n - 1, [(banks[(n - 1) % 4][:], LAT)], SEQ)
                act.wait_ge(K.chunks_done, down.base + 3 * DB)
                post_act_block(act, K, S, DB - 1, DB - 1, [(banks[(DB - 1) % 4][:], LAT)], SEQ)
                norm_act(act, S.post, K, SEQ)
                if carry:
                    carry_act(act, K, S, post_mods)

            @block.tensor
            def _(pe):
                norm_pe(pe, S.pre, K, sums, SEQ, carried)
                done = 0
                for part in up:
                    def turn(i, s, part=part, done=done):
                        i, s = i + done, s + done
                        if s >= 2:
                            pe.wait_ge(S.prod_ready, i - 1)
                        for j in range(2):
                            multiply(pe, K, u0, i, s, j, 8, [(banks[2 * (s % 2) + j][:], LAT)],
                                     lambda p, k, sl: S.h[:, p, k, sl],
                                     before=(lambda k: pe.wait_ge(S.h_ready, k + 1)) if s == 0 and j == 0 else None)
                        if part.ada:
                            ada_pe(pe, K, part.ada_base + i - done, part.ada.vecs)
                    lead = 2 if done == 0 else 0
                    for i in range(lead):
                        turn(i, i)
                    loop(pe, lead, part.n, 2, turn)
                    done += part.n

                pe.wait_ge(S.prod_ready, FB - 1)

                def block_turn(n, s):
                    if s >= 4:
                        pe.wait_ge(S.post.sq_ready, n - 3)
                    for j in range(3):
                        if s == 0:
                            pe.wait_ge(S.hid_ready, (8, 16, FB)[j])
                        multiply(pe, K, down, n, s, j, tiles[j], [(banks[s % 4][:], LAT)],
                                 lambda p, k, sl, j=j: hid[:, p, 8 * j + k, sl], first=j == 0, last=j == 2)
                for n in range(4):
                    block_turn(n, n)
                loop(pe, 4, DB, 4, block_turn)
                norm_pe(pe, S.post, K, sums, SEQ)
                if carry:
                    carry_pe(pe, K, S, banks[0], SEQ)

            @block.vector
            def _(dve):
                pre_dve(dve, K, S, pre_mods, K.pcol("norm_pre", 48)[:, (layer * NS + sub) * DB:][:, 0:DB], sums,
                        carried)
                done, base = 0, 0
                for part in up:
                    nv = part.ada.vecs if part.ada else 0
                    per = ada_ops(nv) if nv else 0

                    def turn(i, s, part=part, done=done, base=base, nv=nv, per=per):
                        steps = Steps(dve, S.steps, i * per + base)
                        if nv:
                            m = part.ada_base + i
                            ada_sum(dve, K, steps, m, part.ada.use)
                        i, s = i + done, s + done
                        dve.wait_ge(S.silu_ready, i + 1)
                        dve.wait_ge(K.chunks_done, u0.base + 2 * i + 2)
                        dve.tensor_tensor(prod[:, s % 2, :], sil[:, s % 2, :], banks[2 * (s % 2) + 1][:],
                                          ALU.mult).then_inc(S.prod_ready, 1)
                        dve.wait_ge(S.hid_hi, i + 1)
                        dve.tensor_tensor(hid[:, LO, at(i, 1), :], prod[:, s % 2, :],
                                          hid[:, HI, at(i, 1), :].bitcast(F32),
                                          ALU.subtract).then_inc(S.hid_ready, 1)
                        if nv:
                            ada_columns(dve, K, steps, m, part.ada.bias(i - done), part.ada.out(i - done), nv)
                            assert steps.n == per
                    loop(dve, 0, part.n, 2, turn)
                    done += part.n
                    base += part.n * per
                post_dve(dve, K, S, post_mods, K.pcol("norm_post", 48)[:, (layer * NS + sub) * DB:][:, 0:DB],
                         0.5, sums)
                if carry:
                    carry_dve(dve, K, S, banks[0], SEQ)

def split_operand_act(act, S, n, src, dst):
    act.wait_ge(S.m_full, n + 1)
    act.activation(dst, src, ACT.Copy).then_inc(S.m_hi, 1)


def split_operand_dve(dve, S, n, src, hi, lo):
    dve.wait_ge(S.m_hi, n + 1)
    dve.tensor_tensor(lo, src, hi.bitcast(F32), ALU.subtract).then_inc(S.m_ready, 1)


def out_pe(pe, K, S, seg, operand, banks_of, ready):
    for n in range(DB):
        if n >= 2:
            pe.wait_ge(S.post.sq_ready, n - 1)
        multiply(pe, K, seg, n, n, 0, DB, banks_of(n), lambda p, k, sl: operand[:, p, k, sl],
                 before=(lambda k: pe.wait_ge(ready, k + 1)) if n == 0 else None)


def out_act(act, K, S, seg, banks_of, width, first_split):
    for n in range(DB):
        if n + 1 >= first_split and n + 1 < DB:
            split_hi(act, K, seg, n + 1, n + 1, 0, DB)
        act.wait_ge(K.chunks_done, seg.base + n + 1)
        post_act_block(act, K, S, n, n, banks_of(n), width)
    norm_act(act, S.post, K, width)



CONV_A, CONV_B = 4, 31
LRU_C = 8.0


def lru_scale(dve, steps, lam, t, out):
    z, q, q2, acc = t[1], t[2], t[3], t[4]
    steps(dve.tensor_scalar(acc, z, 2.0, None, ALU.add))
    steps(dve.reciprocal(acc, acc))
    steps(dve.tensor_tensor(q, z, acc, ALU.mult))
    steps(dve.tensor_tensor(q2, q, q, ALU.mult))
    steps(dve.tensor_scalar(acc, q2, 1.0 / 19, 1.0 / 17, ALU.mult, ALU.add))
    for d in (15, 13, 11, 9, 7, 5, 3, 1):
        steps(dve.tensor_tensor(acc, acc, q2, ALU.mult))
        steps(dve.tensor_scalar(acc, acc, 1.0 / d, None, ALU.add))
    steps(dve.tensor_tensor(acc, acc, q, ALU.mult))
    steps(dve.tensor_scalar(q, lam, 0.0, None, ALU.min))
    steps(dve.scalar_tensor_tensor(out, acc, -2.0, q, ALU.mult, ALU.add))


LRU_SCALE_STEPS = 5 + 16 + 3


def mixer_ab_phase(K, index, layer, sub):
    nc, A = K.nc, K.A
    pairs, ax_seg, ag_seg, out_seg = K.weights.phases[index]
    shift, scale, gate = (K.mod_cols(layer, sub, kind) for kind in range(3))
    pre_mods, post_mods = [(LAT, K.x, scale, shift)], [(LAT, K.x, gate)]
    HB = 4
    with phase(K, *norm_names("pre"), *norm_names("post"), *SUB_SEMS, *CARRY_SEMS, "gate_ready", "v_ready", "ax_ready",
               "pads", "conv_b", "conv_a", "lam_z", "steps", "w_in", "gates_ps", "ri_ready", "exp_ready",
               "sq_in", "root_ready", "ya_in", "stat_in", "stat_ps", "dev_ready", "dsq_ready", "gn_var",
               "gn_std", "gn_out", "m_full", "m_hi", "m_ready") as S:
        K.norm_buffers(S, SEQ)
        ga = S.sb("a_gate", [P, HB, SEQ])
        axp = S.sb("a_x_padded", [P, HB, CONV_A - 1 + SEQ])
        vp = S.sb("v_padded", [P, HB, CONV_B - 1 + SEQ])
        gsig = S.sb("b_gate", [P, 2, SEQ])
        conv = S.sb("conv", [P, 2, SEQ])
        vc = S.sb("v_conv", [P, HB, SEQ])
        xc = S.sb("x_conv", [P, HB, SEQ])
        wr = S.sb("gate_w", [P, 2, HB, P])
        lam = S.sb("lam", [P, 6, HB])
        mo = S.sb("m", [P, 2, DB, SEQ], F32R)
        with ExitStack() as c:
            S.h = K.sbuf(c, "h", [P, 2, DB, SEQ], F32R)
        with ExitStack() as c:
            ri = K.sbuf(c, "r_i", [P, 2, HB, SEQ])
            th = K.sbuf(c, "tanh", [P, HB, SEQ])
            mf = K.sbuf(c, "m_full", [P, HB, SEQ])
        with ExitStack() as c:
            S.y = K.sbuf(c, "y", [P, DB, SEQ])
        banks = [S.psum(f"acc{i}", [P, 512]) for i in range(4)]
        stat = [S.psum(f"stat{i}", [P, 512]) for i in range(2)]
        sums = [S.psum("sums", [P, 512])]
        wr4 = wr.rearrange("p g b (t e) -> p g b t e", t=2)
        out_banks = lambda n: [(banks[n % 2][:], LAT)]

        with nc.Block() as block:

            @block.sync
            def _(sp):
                weights_sp(sp, K, index)

            @block.gpsimd
            def _(pool):
                pool.memset(wr[:], 0.0).then_inc(S.pads, 1)
                pool.memset(axp[:, :, 0:CONV_A - 1], 0.0).then_inc(S.pads, 1)
                pool.memset(vp[:, :, 0:CONV_B - 1], 0.0).then_inc(S.pads, 1)
                split_all(pool, K, [pairs, ax_seg, ag_seg, out_seg], [(8, 8), (8,), (8,), (8,)])
                post_pool(pool, K, S, post_mods)

            @block.scalar
            def _(act):
                chunks = [(pairs, i, j) for i in range(HB) for j in range(2)] + \
                         [(ax_seg, i, 0) for i in range(HB)] + [(ag_seg, i, 0) for i in range(HB)]
                for n in range(SPLIT):
                    split_hi(act, K, chunks[n][0], chunks[n][1], chunks[n][1], chunks[n][2], 8)
                act.wait_ge(S.pads, 1)
                for t in range(2):
                    for g in range(2):
                        src = A["a_gate_w"][0].rearrange("(b t) d e -> t d b e", t=2)[t]
                        act.dma_start(wr4[64 * t:64 * t + 64, g, :, t, :],
                                      src[:, :, 64 * g:64 * g + 64]).then_inc(S.w_in, 16)
                act.activation(lam[:, 0], K.pcol("a_lam", HB), ACT.Abs).then_inc(S.lam_z, 1)
                act.wait_ge(S.lam_z, 1)
                act.activation(lam[:, 1], lam[:, 0], ACT.Exp, scale=-1.0).then_inc(S.lam_z, 1)
                pre_act(act, K, S, pre_mods, True)
                for n, (seg, i, j) in enumerate(chunks):
                    act.wait_ge(K.chunks_done, pairs.base + n + 1)
                    bank = banks[n % 4]
                    if seg is pairs and j == 1:
                        if i >= 2:
                            act.wait_ge(S.v_ready, i - 1)
                        act.activation(gsig[:, i % 2, :], bank[:], ACT.Sigmoid).then_inc(S.gate_ready, 1)
                    elif seg is ax_seg:
                        if i == 0:
                            act.wait_ge(S.pads, 2)
                        act.activation(axp[:, i, CONV_A - 1:], bank[:], ACT.Copy).then_inc(S.ax_ready, 1)
                    elif seg is ag_seg:
                        act.activation(ga[:, i, :], bank[:], ACT.Gelu_apprx_tanh).then_inc(S.ax_ready, 1)
                    if n + SPLIT < len(chunks):
                        nxt, ni, nj = chunks[n + SPLIT]
                        split_hi(act, K, nxt, ni, ni, nj, 8)
                    else:
                        split_hi(act, K, out_seg, n + SPLIT - len(chunks), n + SPLIT - len(chunks), 0, 8)
                for b in range(HB):
                    for g, name in enumerate(("gate_br", "gate_bi")):
                        n = 2 * b + g
                        act.wait_ge(S.gates_ps, n + 1)
                        act.activation(ri[:, g, b, :], banks[n % 4][:], ACT.Sigmoid,
                                       bias=K.pcol(name, HB)[:, b:b + 1]).then_inc(S.ri_ready, 1)
                act.wait_ge(S.steps, LRU_SCALE_STEPS + 2)
                for b in range(HB):
                    act.wait_ge(S.ri_ready, 2 * b + 1)
                    act.activation(th[:, b, :], ri[:, 0, b, :], ACT.Tanh,
                                   scale=lam[:, 5, b:b + 1]).then_inc(S.exp_ready, 1)
                    act.wait_ge(S.exp_ready, 2 * b + 1)
                    act.activation(ri[:, 0, b, :], ri[:, 0, b, :], ACT.Exp,
                                   scale=lam[:, 0, b:b + 1]).then_inc(S.exp_ready, 1)
                for b in range(HB):
                    act.wait_ge(S.sq_in, b + 1)
                    act.activation(th[:, b, :], th[:, b, :], ACT.Sqrt).then_inc(S.root_ready, 1)
                for b in range(HB):
                    split_operand_act(act, S, b, mf[:, b, :], mo[:, HI, b, :])
                for b in range(HB):
                    act.wait_ge(S.dev_ready, b + 1)
                    act.activation(K.sq[:, b % 2, :], vc[:, b, :], ACT.Square).then_inc(S.dsq_ready, 1)
                    act.wait_ge(S.gn_var, b + 1)
                    act.activation(th[:, b, :], th[:, b, :], ACT.Sqrt).then_inc(S.gn_std, 1)
                for b in range(HB):
                    act.wait_ge(S.gn_out, b + 1)
                    act.activation(mf[:, b, :], vc[:, b, :], ACT.Silu, scale=K.pcol("b_norm_g", HB)[:, b:b + 1],
                                   bias=K.pcol("b_norm_b", HB)[:, b:b + 1]).then_inc(S.m_full, 1)
                    split_operand_act(act, S, HB + b, mf[:, b, :], mo[:, HI, HB + b, :])
                out_act(act, K, S, out_seg, out_banks, SEQ, SPLIT)
                carry_act(act, K, S, post_mods)

            @block.tensor
            def _(pe):
                norm_pe(pe, S.pre, K, sums, SEQ, True)
                hm = lambda p, k, sl: S.h[:, p, k, sl]
                n = 0
                for seg in (pairs, ax_seg, ag_seg):
                    for i in range(HB):
                        for j in range(seg.per):
                            if 4 <= n < 12:
                                pe.wait_ge(S.v_ready, (n - 4) // 2 + 1)
                            elif n >= 12:
                                pe.wait_ge(S.ax_ready, n - 11)
                            multiply(pe, K, seg, i, i, j, 8, [(banks[n % 4][:], LAT)], hm,
                                     before=(lambda k: pe.wait_ge(S.h_ready, k + 1)) if n == 0 else None)
                            n += 1
                pe.wait_ge(S.w_in, 16 * 4)
                for b in range(HB):
                    pe.wait_ge(S.conv_a, 3 * HB + b + 1)
                    for g in range(2):
                        n = 2 * b + g
                        pe.wait_ge(S.ax_ready, HB + n + 1) if n < 4 else pe.wait_ge(S.ri_ready, n - 3)
                        pe.matmul(banks[n % 4][:], wr[:, g, b, :], xc[:, b, :], start=True,
                                  stop=True).then_inc(S.gates_ps, 1)
                for b in range(HB):
                    pe.wait_ge(S.stat_in, b + 1)
                    pe.matmul(stat[0][:], K.bd64, vc[:, b, :], start=True, stop=True).then_inc(S.stat_ps, 1)
                    pe.wait_ge(S.dsq_ready, b + 1)
                    pe.matmul(stat[1][:], K.bd64, K.sq[:, b % 2, :], start=True, stop=True).then_inc(S.stat_ps, 1)
                pe.wait_ge(S.ri_ready, 2 * HB)
                out_pe(pe, K, S, out_seg, mo, out_banks, S.m_ready)
                norm_pe(pe, S.post, K, sums, SEQ)
                carry_pe(pe, K, S, banks[0], SEQ)

            @block.vector
            def _(dve):
                steps = Steps(dve, S.steps)
                pre_dve(dve, K, S, pre_mods, K.pcol("norm_pre", 48)[:, (layer * NS + sub) * DB:][:, 0:DB], sums,
                        True)
                dve.wait_ge(S.lam_z, 2)
                lru_scale(dve, steps, K.pcol("a_lam", HB), [lam[:, q] for q in range(5)], lam[:, 0])
                steps(dve.tensor_scalar(lam[:, 0], lam[:, 0], LRU_C, None, ALU.mult))
                steps(dve.tensor_scalar(lam[:, 5], lam[:, 0], -1.0, None, ALU.mult))
                dve.wait_ge(S.pads, 3)
                taps = K.pcol("b_conv_w", CONV_B * HB)
                done = 0
                for b in range(HB):
                    dve.wait_ge(S.gate_ready, b + 1)
                    dve.tensor_tensor(vp[:, b, CONV_B - 1:], banks[(2 * b) % 4][:], gsig[:, b % 2, :],
                                      ALU.mult).then_inc(S.v_ready, 1)
                    dve.wait_ge(S.v_ready, b + 1)
                    for k in range(CONV_B):
                        col = taps[:, HB * k + b:HB * k + b + 1]
                        src = vp[:, b, k:k + SEQ]
                        if k >= 2:
                            dve.wait_ge(S.conv_b, done - 1)
                            ins = dve.scalar_tensor_tensor(conv[:, k % 2, :], src, col, conv[:, k % 2, :],
                                                           ALU.mult, ALU.add)
                        else:
                            if b:
                                dve.wait_ge(S.conv_b, done)
                            ins = dve.tensor_scalar(conv[:, k % 2, :], src, col,
                                                    K.pcol("b_conv_b", HB)[:, b:b + 1] if k == 0 else 0.0,
                                                    ALU.mult, ALU.add)
                        ins.then_inc(S.conv_b, 1)
                        done += 1
                    dve.wait_ge(S.conv_b, done)
                    dve.tensor_tensor(vc[:, b, :], conv[:, 0, :], conv[:, 1, :], ALU.add).then_inc(S.conv_b, 1)
                    done += 1
                dve.wait_ge(S.ax_ready, HB)
                taps = K.pcol("a_conv_w", CONV_A * HB)
                for k in range(CONV_A):
                    for b in range(HB):
                        col = taps[:, HB * k + b:HB * k + b + 1]
                        src = axp[:, b, k:k + SEQ]
                        if k:
                            dve.wait_ge(S.conv_a, HB * (k - 1) + b + 1)
                            ins = dve.scalar_tensor_tensor(xc[:, b, :], src, col, xc[:, b, :], ALU.mult, ALU.add)
                        else:
                            ins = dve.tensor_scalar(xc[:, b, :], src, col, K.pcol("a_conv_b", HB)[:, b:b + 1],
                                                    ALU.mult, ALU.add)
                        ins.then_inc(S.conv_a, 1)
                for b in range(HB):
                    dve.wait_ge(S.exp_ready, 2 * b + 2)
                    steps(dve.tensor_tensor(mf[:, b, :], ri[:, 0, b, :], ri[:, 0, b, :], ALU.mult))
                    dve.scalar_tensor_tensor(th[:, b, :], mf[:, b, :], 1.0, th[:, b, :], ALU.add,
                                             ALU.mult).then_inc(S.sq_in, 1)
                    dve.wait_ge(S.ri_ready, 2 * HB)
                    steps(dve.tensor_tensor(xc[:, b, :], xc[:, b, :], ri[:, 1, b, :], ALU.mult))
                for b in range(HB):
                    dve.wait_ge(S.root_ready, b + 1)
                    steps(dve.tensor_tensor(xc[:, b, :], xc[:, b, :], th[:, b, :], ALU.mult))
                    steps(dve.tensor_tensor_scan(th[:, b, :], ri[:, 0, b, :], xc[:, b, :], 0.0, ALU.mult, ALU.add))
                    dve.wait_ge(S.ax_ready, 2 * HB)
                    dve.tensor_tensor(mf[:, b, :], th[:, b, :], ga[:, b, :], ALU.mult).then_inc(S.m_full, 1)
                for b in range(HB):
                    split_operand_dve(dve, S, b, mf[:, b, :], mo[:, HI, b, :], mo[:, LO, b, :])
                for b in range(HB):
                    if b == 0:
                        dve.wait_ge(S.conv_b, done)
                        dve.sem_inc(S.stat_in, HB)
                    dve.wait_ge(S.stat_ps, 2 * b + 1)
                    dve.scalar_tensor_tensor(vc[:, b, :], stat[0][:], -1.0 / 64, vc[:, b, :], ALU.mult,
                                             ALU.add).then_inc(S.dev_ready, 1)
                    dve.wait_ge(S.stat_ps, 2 * b + 2)
                    dve.tensor_scalar(th[:, b, :], stat[1][:], 1.0 / 64, EPS, ALU.mult, ALU.add).then_inc(S.gn_var, 1)
                    dve.wait_ge(S.gn_std, b + 1)
                    steps(dve.reciprocal(th[:, b, :], th[:, b, :]))
                    dve.tensor_tensor(vc[:, b, :], vc[:, b, :], th[:, b, :], ALU.mult).then_inc(S.gn_out, 1)
                for b in range(HB):
                    split_operand_dve(dve, S, HB + b, mf[:, b, :], mo[:, HI, HB + b, :], mo[:, LO, HB + b, :])
                post_dve(dve, K, S, post_mods, K.pcol("norm_post", 48)[:, (layer * NS + sub) * DB:][:, 0:DB],
                         1.0, sums)
                carry_dve(dve, K, S, banks[0], SEQ)

C_HEADS = 8


def mixer_c_phase(K, index, layer, sub):
    nc, A = K.nc, K.A
    values, gates, out_seg = K.weights.phases[index]
    in_seg = Names(n=2 * DB, per=1, base=values.base)
    shift, scale, gate = (K.mod_cols(layer, sub, kind) for kind in range(3))
    pre_mods, post_mods = [(LAT, K.x, scale, shift)], [(LAT, K.x, gate)]
    NC = SEQ // CH
    with phase(K, *norm_names("pre"), *norm_names("post"), *norm_names("mid"), *SUB_SEMS, *CARRY_SEMS, "z_ready", "mean_ps",
               "dev_ready", "vn_scaled", "vn_ready", "vt_ps", "vt_ready", "ws_ps", "ws_ready",
               "mix_ps", "m_full", "m_hi", "m_ready") as S:
        K.norm_buffers(S, SEQ)
        S.ws_in, S.mask_in = K.pool_sem("ws_in"), K.pool_sem("mask_in")
        z = S.sb("z", [P, 2, DB, SEQ])
        ws = S.sb("w_s", [P, C_HEADS, P])
        wst = S.sb("w_s_turned", [P, C_HEADS, P])
        mask = S.sb("mask", [P, P])
        bs = S.sb("b_s", [1, C_HEADS, P])
        vt = S.sb("v_turned", [P, 2, NC, P])
        mf = S.sb("m_full", [P, 2, SEQ])
        S.y = S.sb("y", [P, DB, SEQ])
        with ExitStack() as c:
            S.h = K.sbuf(c, "h", [P, 2, DB, SEQ], F32R)
        mo = S.sb("m", [P, 2, DB, SEQ], F32R)
        banks = [S.psum(f"acc{i}", [P, 512]) for i in range(4)]
        sums = [S.psum("sums", [P, 512])]
        tp = S.psum("turn", [P, 512])
        mixp = banks[2:4]
        out_banks = lambda n: [(banks[n % 2][:], LAT)]

        def turned_copy(act, b):
            act.wait_ge(S.vt_ps, b + 1)
            if b >= 2:
                act.wait_ge(S.mix_ps, b - 1)
            act.activation(vt[:, b % 2].rearrange("p n d -> p (n d)"), tp[:], ACT.Copy).then_inc(S.vt_ready, 1)

        def mix_pe(pe, b):
            pe.wait_ge(S.vt_ready, b + 1)
            if b >= 2:
                pe.wait_ge(S.m_full, b - 1)
            for n in range(NC):
                out = mixp[b % 2][:, n * P:(n + 1) * P]
                pe.matmul(out, vt[:, b % 2, n, :], wst[:, b, :], start=True, stop=False)
                mm = pe.matmul(out, K.ones[0:1, :], bs[:, b, :], start=False, stop=True)
            mm.then_inc(S.mix_ps, 1)

        with nc.Block() as block:

            @block.sync
            def _(sp):
                weights_sp(sp, K, index)

            @block.gpsimd
            def _(pool):
                pool.dma_start(ws[:], A["c_w_s"][0].rearrange("h t s -> t h s")).then_inc(S.ws_in, 16)
                pool.dma_start(mask[:], A["masks"][1]).then_inc(S.mask_in, 16)
                pool.dma_start(bs[:], A["c_b_s"]).then_inc(S.mask_in, 16)
                split_all(pool, K, [in_seg, out_seg], [(8,), (8,)])
                post_pool(pool, K, S, post_mods)

            @block.scalar
            def _(act):
                for n in range(SPLIT):
                    split_hi(act, K, in_seg, n, n, 0, 8)
                pre_act(act, K, S, pre_mods, True)

                for n in range(2 * DB):
                    act.wait_ge(K.chunks_done, in_seg.base + n + 1)
                    half = (1 - n // DB) * DB + n % DB
                    act.activation(z[:, n // DB, n % DB, :], banks[n % 4][:], ACT.Gelu_apprx_tanh,
                                   bias=K.pcol("c_b_in", 2 * DB)[:, half:half + 1]).then_inc(S.z_ready, 1)
                    if n + SPLIT < 2 * DB:
                        split_hi(act, K, in_seg, n + SPLIT, n + SPLIT, 0, 8)
                    else:
                        m = n + SPLIT - 2 * DB
                        split_hi(act, K, out_seg, m, m, 0, 8)
                for b in range(DB):
                    act.wait_ge(S.dev_ready, b + 1)
                    squares_act(act, S.mid, K, b, [(z[:, 0, b, :], LAT)])
                norm_act(act, S.mid, K, SEQ)
                for b in range(DB):
                    act.wait_ge(S.vn_scaled, b + 1)
                    act.activation(z[:, 0, b, :], z[:, 0, b, :], ACT.Identity,
                                   bias=K.pcol("c_norm_b", DB)[:, b:b + 1]).then_inc(S.vn_ready, 1)
                    if b >= 1:
                        turned_copy(act, b - 1)
                    if b >= 3:
                        split_operand_act(act, S, b - 3, mf[:, (b - 3) % 2, :], mo[:, HI, b - 3, :])
                turned_copy(act, DB - 1)
                for b in range(DB - 3, DB):
                    split_operand_act(act, S, b, mf[:, b % 2, :], mo[:, HI, b, :])
                out_act(act, K, S, out_seg, out_banks, SEQ, SPLIT)
                carry_act(act, K, S, post_mods)

            @block.tensor
            def _(pe):
                norm_pe(pe, S.pre, K, sums, SEQ, True)
                hm = lambda p, k, sl: S.h[:, p, k, sl]
                for n in range(2 * DB):
                    if n >= 4:
                        pe.wait_ge(S.z_ready, n - 3)
                    multiply(pe, K, in_seg, n, n, 0, 8, [(banks[n % 4][:], LAT)], hm,
                             before=(lambda k: pe.wait_ge(S.h_ready, k + 1)) if n == 0 else None)
                pe.wait_ge(S.ws_in, 16)
                pe.wait_ge(S.z_ready, 2 * DB)
                for h in range(0, C_HEADS, 4):
                    for q in range(4):
                        mm = pe.transpose(mixp[h // 4][:, q * P:(q + 1) * P], ws[:, h + q, :], K.ident)
                    mm.then_inc(S.ws_ps, 1)
                pe.wait_ge(S.z_ready, DB)
                for b in range(DB):
                    mm = pe.matmul(tp[:], K.ones, z[:, 0, b, :], start=b == 0, stop=b == DB - 1)
                mm.then_inc(S.mean_ps, 1)
                norm_pe(pe, S.mid, K, sums, SEQ)
                pe.wait_ge(S.ws_ready, 2)
                pe.wait_ge(S.mask_in, 32)
                for b in range(DB):
                    pe.wait_ge(S.vn_ready, b + 1)
                    if b >= 1:
                        pe.wait_ge(S.vt_ready, b)
                    for n in range(NC):
                        mm = pe.transpose(tp[:, n * P:(n + 1) * P], z[:, 0, b, n * CH:(n + 1) * CH], K.ident)
                    mm.then_inc(S.vt_ps, 1)
                    if b >= 1:
                        mix_pe(pe, b - 1)
                mix_pe(pe, DB - 1)
                out_pe(pe, K, S, out_seg, mo, out_banks, S.m_ready)
                norm_pe(pe, S.post, K, sums, SEQ)
                carry_pe(pe, K, S, banks[0], SEQ)

            @block.vector
            def _(dve):
                pre_dve(dve, K, S, pre_mods, K.pcol("norm_pre", 48)[:, (layer * NS + sub) * DB:][:, 0:DB], sums,
                        True)
                dve.wait_ge(S.mask_in, 32)
                low = mask.rearrange("p (a c) -> p a c", a=1).broadcast_to([P, 4, P])
                for h in range(2):
                    dve.wait_ge(S.ws_ps, h + 1)
                    dve.tensor_tensor(wst[:, 4 * h:4 * h + 4, :],
                                      mixp[h].rearrange("p (a c) -> p a c", a=4), low,
                                      ALU.mult).then_inc(S.ws_ready, 1)
                dve.wait_ge(S.mean_ps, 1)
                for b in range(DB):
                    dve.scalar_tensor_tensor(z[:, 0, b, :], tp[:], -1.0 / D, z[:, 0, b, :], ALU.mult,
                                             ALU.add).then_inc(S.dev_ready, 1)
                for b in range(DB):
                    squares_dve(dve, S.mid, K, b, SEQ)
                norm_dve(dve, S.mid, K, sums, SEQ)
                for b in range(DB):
                    dve.scalar_tensor_tensor(z[:, 0, b, :], z[:, 0, b, :], K.pcol("c_norm_g", DB)[:, b:b + 1],
                                             spread_factors(sums, LAT), ALU.mult, ALU.mult).then_inc(S.vn_scaled, 1)
                dve.wait_ge(S.z_ready, 2 * DB)
                for b in range(DB):
                    dve.wait_ge(S.mix_ps, b + 1)
                    if b >= 2:
                        dve.wait_ge(S.m_ready, b - 1)
                    dve.tensor_tensor(mf[:, b % 2, :], mixp[b % 2][:], z[:, 1, b, :], ALU.mult).then_inc(S.m_full, 1)
                    split_operand_dve(dve, S, b, mf[:, b % 2, :], mo[:, HI, b, :], mo[:, LO, b, :])
                post_dve(dve, K, S, post_mods, K.pcol("norm_post", 48)[:, (layer * NS + sub) * DB:][:, 0:DB],
                         1.0, sums)
                carry_dve(dve, K, S, banks[0], SEQ)



def output_phase(K):
    nc = K.nc
    with phase(K, "turned", "copied", "stored") as S:
        rows = S.sb("out_rows", [P, SEQ // P, D])
        ps = [S.psum(f"turn{i}", [P, 512]) for i in range(4)]
        NT = SEQ // P
        with nc.Block() as block:

            @block.tensor
            def _(pe):
                for n in range(2 * NT):
                    t, half = n // 2, n % 2
                    if n >= 4:
                        pe.wait_ge(S.copied, n - 3)
                    for q in range(4):
                        mm = pe.transpose(ps[n % 4][:, q * P:(q + 1) * P],
                                          K.x[:, 4 * half + q, t * P:(t + 1) * P], K.ident)
                    mm.then_inc(S.turned, 1)

            @block.vector
            def _(dve):
                for n in range(2 * NT):
                    dve.wait_ge(S.turned, n + 1)
                    dve.tensor_copy(rows[:, n // 2, (n % 2) * 512:(n % 2) * 512 + 512],
                                    ps[n % 4][:]).then_inc(S.copied, 1)

            @block.sync
            def _(sp):
                for t in range(NT):
                    sp.wait_ge(S.copied, 2 * t + 2)
                    sp.dma_start(K.out.rearrange("a (t p) d -> p (a t) d", p=P)[:, t, :],
                                 rows[:, t, :]).then_inc(S.stored, 16)
                sp.wait_ge(S.stored, 16 * NT)



LORA_BLOCKS = 2
SHIFT_BLOCKS = 3 * RB + LORA_BLOCKS
GATE_R, FOUR, GATE_F = SHIFT_BLOCKS, SHIFT_BLOCKS + RB, SHIFT_BLOCKS + RB + 2
EVEN_BLOCKS = GATE_F + 2
PARTS = (LAT, CON)


def even_in_phase(K, index, layer):
    nc, A, u = K.nc, K.A, K.u
    seg, late = K.weights.phases[index]
    pre_mods = [(sl, x, K.mod2_cols(layer, v, 1), K.mod2_cols(layer, v, 0))
                for v, (sl, x) in enumerate(((LAT, K.x), (CON, K.xc)))]
    with phase(K, *norm_names("pre"), *SUB_SEMS, "ctx_in", "turned", "copied", "coef", "based", "shifted",
               "late_ready", "late_out0", "late_out1", "x_saved") as S:
        K.norm_buffers(S, TOK)
        stage = S.sb("late", [P, 2, TOK])
        with ExitStack() as c:
            rows = K.sbuf(c, "ctx_rows", [P, CTX // P, D])
        S.h = S.sb("h", [P, 2, DB, TOK], F32R)
        keep = S.sb("keep", [P, SHIFT_BLOCKS])
        move4 = S.sb("move4", [P, 4, SHIFT_BLOCKS])
        move2 = S.sb("move2", [P, 2, SHIFT_BLOCKS])
        lat = [S.psum(f"lat{i}", [P, 512]) for i in range(4)]
        con = [S.psum(f"con{i}", [P, 512]) for i in range(4)]
        sums = con[2:4]
        late_out = (S.late_out0, S.late_out1)
        outs = lambda s: [(lat[s % 4][:], LAT), (con[s % 4][:, 0:CTX], CON)]
        NT = CTX // P

        with nc.Block() as block:

            @block.sync
            def _(sp):
                sp.dma_start(rows[:], A["ctx_2"].rearrange("a (t p) d -> p (a t) d", p=P)).then_inc(S.ctx_in, 16)
                sp.dma_start(K.x_dram, K.x[:]).then_inc(S.x_saved, 16)
                weights_sp(sp, K, index)
                sp.wait_ge(S.copied, DB)
                sp.dma_start(K.xc_dram, K.xc[:]).then_inc(S.x_saved, 16)
                sp.wait_ge(S.x_saved, 32)

            @block.gpsimd
            def _(pool):
                split_all(pool, K, [seg, late], [(8,), (8,)])

            @block.scalar
            def _(act):
                for n in range(SPLIT):
                    split_hi(act, K, seg, n, n, 0, DB)
                act.wait_ge(S.copied, DB)
                pre_act(act, K, S, pre_mods)

                def base_turn(i, s):
                    act.wait_ge(K.chunks_done, seg.base + i + 1)
                    for ps, sl in outs(s):
                        ins = act.activation(u[:, at(i, 1), sl], ps, ACT.Copy, scale=keep[:, at(i, 1)])
                    ins.then_inc(S.based, 1)

                def turn(i, s):
                    base_turn(i, s)
                    split_hi(act, K, seg, i + SPLIT, s + SPLIT, 0, DB)
                act.wait_ge(S.coef, 1 + 4 + 2)
                loop(act, 0, SHIFT_BLOCKS - 4, 4, turn)
                for i in range(SHIFT_BLOCKS - 4, SHIFT_BLOCKS):
                    base_turn(i, i)
                    if i + SPLIT < SHIFT_BLOCKS:
                        split_hi(act, K, seg, i + SPLIT, i + SPLIT, 0, DB)
                    else:
                        split_hi(act, K, late, i + SPLIT - SHIFT_BLOCKS, i + SPLIT - SHIFT_BLOCKS, 0, DB)
                for i in range(late.n):
                    act.wait_ge(K.chunks_done, late.base + i + 1)
                    if i >= 2:
                        act.wait_ge(late_out[i % 2], 16 * (i // 2))
                    func = ACT.Copy if i in (RB, RB + 1) else ACT.Silu
                    for ps, sl in outs(SHIFT_BLOCKS + i):
                        ins = act.activation(stage[:, i % 2, sl], ps, func)
                    ins.then_inc(S.late_ready, 1)
                    if i + SPLIT < late.n:
                        split_hi(act, K, late, i + SPLIT, i + SPLIT, 0, DB)
                    act.wait_ge(S.late_ready, i + 1)
                    act.dma_start(K.late_dram[i], stage[:, i % 2, :]).then_inc(late_out[i % 2], 16)
                for o in late_out:
                    act.wait_ge(o, 16 * (late.n // 2))
                act.wait_ge(S.shifted, 6 * SHIFT_BLOCKS)
                act.activation(u[:, 3 * RB, :], u[:, 3 * RB, :], ACT.Tanh)

            @block.tensor
            def _(pe):
                pe.wait_ge(S.ctx_in, 16)
                for b in range(DB):
                    if b >= 4:
                        pe.wait_ge(S.copied, b - 3)
                    for t in range(NT):
                        mm = pe.transpose(lat[b % 4][:, t * P:(t + 1) * P], rows[:, t, b * P:(b + 1) * P], K.ident)
                    mm.then_inc(S.turned, 1)
                norm_pe(pe, S.pre, K, sums, TOK)

                def turn(i, s):
                    if s >= 4:
                        pe.wait_ge(S.based, i - 3)
                        pe.wait_ge(S.shifted, i * 6 - 18)
                    multiply(pe, K, seg, i, s, 0, DB, outs(s), lambda p, k, sl: S.h[:, p, k, sl],
                             before=(lambda k: pe.wait_ge(S.h_ready, k + 1)) if s == 0 else None)
                for i in range(4):
                    turn(i, i)
                loop(pe, 4, SHIFT_BLOCKS, 4, turn)
                for i in range(late.n):
                    if i < 4:
                        pe.wait_ge(S.based, SHIFT_BLOCKS - 3 + i)
                        pe.wait_ge(S.shifted, 6 * (SHIFT_BLOCKS - 3 + i))
                    else:
                        pe.wait_ge(S.late_ready, i - 3)
                    multiply(pe, K, late, i, i, 0, DB, outs(SHIFT_BLOCKS + i), lambda p, k, sl: S.h[:, p, k, sl])

            @block.vector
            def _(dve):
                for b in range(DB):
                    dve.wait_ge(S.turned, b + 1)
                    dve.tensor_copy(K.xc[:, b, :], lat[b % 4][:, 0:CTX]).then_inc(S.copied, 1)
                dve.wait_ge(S.copied, DB)
                mu = K.pcol("mu", SHIFT_BLOCKS)
                dve.tensor_scalar(keep[:], mu, -1.0, 1.0, ALU.mult, ALU.add).then_inc(S.coef, 1)
                for m in range(4):
                    dve.tensor_scalar(move4[:, m, :], mu, K.shift4[:, m:m + 1], None, ALU.mult).then_inc(S.coef, 1)
                for m in range(2):
                    dve.tensor_scalar(move2[:, m, :], mu, K.shift2[:, m:m + 1], None, ALU.mult).then_inc(S.coef, 1)
                pre_dve(dve, K, S, pre_mods, K.pcol("norm_pre_2", 16)[:, layer * DB:][:, 0:DB], sums)
                dve.wait_ge(S.coef, 7)

                def add(i, dst, src, col, before):
                    if before is not None:
                        dve.wait_ge(S.shifted, i * 6 + before)
                    dve.scalar_tensor_tensor(dst, src, col, dst, ALU.mult, ALU.add).then_inc(S.shifted, 1)

                def turn(i, s):
                    dve.wait_ge(S.based, i + 1)
                    (L, _), (C, _) = outs(s)
                    one = at(i, 1)
                    grid = lambda ap: ap.rearrange("p (r c) -> p r c", c=GRID)
                    ul = u[:, one, LAT].rearrange("p a t -> p (a t)")
                    uc = u[:, one, CON].rearrange("p a t -> p (a t)")
                    c4 = [move4[:, m, one] for m in range(4)]
                    c2 = [move2[:, m, one] for m in range(2)]
                    add(i, grid(ul)[:, :, 1:], grid(L)[:, :, :-1], c4[0], None)
                    add(i, uc[:, 1:], C[:, :-1], c2[0], None)
                    add(i, grid(ul)[:, :, :-1], grid(L)[:, :, 1:], c4[1], 1)
                    add(i, uc[:, :-1], C[:, 1:], c2[1], 2)
                    add(i, ul[:, GRID:], L[:, :-GRID], c4[2], 3)
                    add(i, ul[:, :-GRID], L[:, GRID:], c4[3], 5)
                loop(dve, 0, SHIFT_BLOCKS, 4, turn)


PREP = {
    "pe": ["decay0", "rate0", "decay1", "rate1", "norm", "bonus"],
    "act": ["v", "square", "decay0", "rate0", "decay1", "rate1", "root", "wi0", "w0", "q0", "wi1", "w1", "q1"],
    "dve": ["kk", "sum0", "kt0", "sum1", "k0", "kt1", "k1", "max", "inv", "last0", "r0", "last1", "r1", "rk", "bonus"],
    "pool": ["before0", "before1", "kk", "bkk0", "b0", "ksum", "q0", "kw0", "bkk1", "b1", "q1", "kw1"],
}


def even_scan_phase(K):
    nc, A, u = K.nc, K.A, K.u
    NCH = TOK // CH
    ORDER = ((4, 5, 0, 1, 2, 3), (5, 4, 3, 2, 1, 0))
    LEVELS = 6
    PE_U, EV_U, AC_U, PO_U = 5 + 3 * LEVELS + 3, 4 + 2 * LEVELS + 3, 7 + LEVELS, 2
    with phase(K, "tables", "zeros", "pp", "pa", "pd", "pq", "omk", "lw", "reset",
               *(f"{n}{d}" for n in ("pe", "ev", "ac", "po") for d in range(2))) as S:
        masks = S.sb("masks", [P, 4, P])
        levels = S.sb("levels", [P, 7, 2, P])
        lw = S.sb("lora_w", [P, 4, P])
        omk = S.sb("one_minus_ka", [P, RB])
        wi = S.sb("w_inv", [P, 2, TOK])
        flat, flat_c = K.x.rearrange("p b t -> p (b t)"), K.xc.rearrange("p b t -> p (b t)")
        kk, tmp = flat[:, 4 * TOK:5 * TOK], flat_c[:, 0:TOK]
        vst1 = S.sb("v_block", [P, TOK])
        B = []
        for g in range(2):
            B.append(Names(kt=[flat[:, (2 * g + d) * TOK:(2 * g + d + 1) * TOK] for d in range(2)],
                           v=flat_c[:, TOK:2 * TOK] if g == 0 else vst1[:],
                           sgm=S.sb("decay_rate", [P, 4, TOK]),
                           cs=S.sb("decay_sums", [P, 2, TOK]),
                           wlast=S.sb("w_last", [P, 2, NCH])))
        U = []
        for d in range(2):
            U.append(Names(
                qp=S.sb("q_r_padded", [P, 2, 2, P]), bqr=S.sb("bqr", [P, 2, 2, P]), kqr=S.sb("kqr", [P, 2, 2, P]),
                tx=S.sb("t_x", [P, 2, 2, P]), y=S.sb("y", [P, 2, P]),
                vp=S.sb("v_padded", [P, 2, P]), tok=S.sb("tok", [P, 3, P]), rp=S.sb("rhs_padded", [P, 2, P]),
                sp=S.sb("sa_padded", [P, 2, P]), s=S.sb("state", [P, P]),
                b=[S.psum(f"u{d}_{i}", [P, 512]) for i in range(3)],
                pe=(S.pe0, S.pe1)[d], ev=(S.ev0, S.ev1)[d], ac=(S.ac0, S.ac1)[d], po=(S.po0, S.po1)[d]))
        prep_bank = [S.psum("prep_lat", [P, 512]), S.psum("prep_con", [P, 512])]
        both = [(prep_bank[0][:], LAT), (prep_bank[1][:, 0:CTX], CON)]

        def heads(ap):
            return ap.rearrange("p (a c) -> p a c", a=1).broadcast_to([P, 2, P])

        def cols(d, k):
            return slice(ORDER[d][k] * CH, (ORDER[d][k] + 1) * CH)

        def unit(b, k, signals, first=0):
            return b * (NCH * signals) + (k * signals + first)

        def prep(engine, c, name):
            return c * len(PREP[engine]) + (PREP[engine].index(name) + 1)

        def blocks(eng, prepare, units):
            for k in range(NCH):
                for step in range(LEVELS):
                    prepare(0, 0, k, step)

            def body(b, s):
                units(b, s % 2, lambda k, step: prepare(b + 1, (s + 1) % 2, k, step))
            loop(eng, 0, RB - 2, 2, body)
            body(RB - 2, RB - 2)
            units(RB - 1, (RB - 1) % 2, lambda k, step: None)

        own_head = K.bd64.rearrange("p (h x) -> p h x", h=2)[:, :, 0:1].broadcast_to([P, 2, P])

        with nc.Block() as block:

            @block.sync
            def _(sp):
                sp.dma_start(masks[:], A["masks"].rearrange("m s t -> s m t")).then_inc(S.tables, 16)
                sp.dma_start(levels[:], A["levels"].rearrange("(n d) t s -> t n d s", d=2)).then_inc(S.tables, 16)
                sp.wait_ge(S.zeros, 1)

                def load(b):
                    for d in range(2):
                        for w, name in enumerate(("ev_w2_2", "ev_a2_2")):
                            sp.dma_start(lw[64 * d:64 * d + 64, 2 * d + w, :],
                                         A[name][0, d][:, at(b * P, P)]).then_inc(S.lw, 16)
                load(0)
                with sp.Fori(0, RB - 1) as b:
                    sp.wait_ge(S.pp, prep("pe", b, "rate1"))
                    load(b + 1)

            @block.gpsimd
            def _(pool):
                pool.memset(lw[:], 0.0).then_inc(S.zeros, 1)
                for d in range(2):
                    for t in (U[d].qp, U[d].vp, U[d].rp, U[d].sp):
                        pool.memset(t[:], 0.0).then_inc(S.zeros, 1)
                pool.wait_ge(S.zeros, 9)

                def prepare(c, g, k, step):
                    if step:
                        return

                    def op(name, out, a, b, alu, *waits):
                        for engine, what in waits:
                            pool.wait_ge({"act": S.pa, "dve": S.pd, "pool": S.pq}[engine], prep(engine, c, what))
                        pool.tensor_tensor(out, a, b, alu).then_inc(S.pq, 1)
                    O = B[g]
                    q, rate = [O.sgm[:, 0, :], O.sgm[:, 2, :]], [O.sgm[:, 1, :], O.sgm[:, 3, :]]

                    def before(d):
                        op(f"before{d}", q[d], O.cs[:, d, :], q[d], ALU.subtract, ("dve", f"sum{d}"))
                    if k in (1, 2):
                        before(k - 1)
                    if k == 3:
                        op("kk", kk, kk, tmp, ALU.mult, ("dve", "inv"))
                        op("bkk0", rate[0], rate[0], kk, ALU.mult, ("dve", "kt0"), ("pool", "kk"))
                        op("b0", rate[0], rate[0], wi[:, 0, :], ALU.mult, ("act", "wi0"), ("pool", "bkk0"))
                    if k == 4:
                        op("ksum", tmp, O.kt[0], O.kt[1], ALU.add, ("dve", "k1"))
                        op("q0", q[0], q[0], kk, ALU.mult, ("act", "q0"))
                        op("kw0", O.kt[0], O.kt[0], wi[:, 0, :], ALU.mult, ("pool", "ksum"))
                        op("bkk1", rate[1], rate[1], kk, ALU.mult, ("dve", "kt1"))
                    if k == 5:
                        op("b1", rate[1], rate[1], wi[:, 1, :], ALU.mult, ("act", "wi1"), ("pool", "bkk1"))
                        op("q1", q[1], q[1], kk, ALU.mult, ("act", "q1"))
                        op("kw1", O.kt[1], O.kt[1], wi[:, 1, :], ALU.mult)

                def units(b, g, between):
                    pool.wait_ge(S.pq, prep("pool", b, "kw1"))
                    pool.wait_ge(S.pd, prep("dve", b, "bonus"))
                    for k in range(NCH):
                        for d in range(2):
                            c, V = cols(d, k), U[d]
                            pool.wait_ge(V.pe, unit(b, k, PE_U, 1))
                            for w, src in enumerate((B[g].sgm[:, 2 * d, c], B[g].cs[:, d, c])):
                                pool.tensor_tensor(V.qp[:, :, w, :], heads(src), own_head, ALU.mult).then_inc(V.po, 1)
                        between(k, 0)
                blocks(pool, prepare, units)

            @block.tensor
            def _(pe):
                pe.wait_ge(S.zeros, 9)
                for d in range(2):
                    pe.sem_inc(U[d].pe, 1)

                def prepare(c, g, k, step):
                    def product(lhs, src, *waits):
                        for sem, value in waits:
                            pe.wait_ge(sem, value)
                        for ps, sl in both:
                            mm = pe.matmul(ps, lhs, src(sl), start=True, stop=True)
                        mm.then_inc(S.pp, 1)

                    def lora(p, *waits):
                        product(lw[:, p, :], lambda sl: u[:, 3 * RB + p % 2, sl], *waits)
                    act = lambda name: (S.pa, prep("act", c, name))
                    if (k, step) == (0, 1):
                        free = [] if isinstance(c, int) and c == 0 else [(S.pd, c * len(PREP["dve"]))]
                        lora(0, (S.lw, c * 64 + 64), *free)
                    if (k, step) == (0, 4):
                        lora(1, act("decay0"))
                    if (k, step) == (1, 1):
                        lora(2, act("rate0"))
                    if (k, step) == (1, 4):
                        lora(3, act("decay1"))
                    if (k, step) == (2, 1):
                        product(K.bd64, lambda sl: tmp[:, sl], act("rate1"))
                    if (k, step) == (4, 4):
                        product(K.bd64, lambda sl: tmp[:, sl], act("root"), (S.pd, prep("dve", c, "rk")))

                def units(b, g, between):
                    O = B[g]
                    pe.wait_ge(S.pq, prep("pool", b, "kw1"))
                    pe.wait_ge(S.pd, prep("dve", b, "bonus"))
                    for k in range(NCH):
                        ev0, ac0, po0 = unit(b, k, EV_U, 1), unit(b, k, AC_U), unit(b, k, PO_U)
                        for d in range(2):
                            V, c = U[d], cols(d, k)
                            bt, kt = O.sgm[:, 2 * d + 1, c], O.kt[d][:, c]
                            pe.wait_ge(V.po, po0 + 2)
                            pe.wait_ge(V.ev, ev0)
                            rhs = V.qp.rearrange("p h q t -> p (h q t)")
                            pe.matmul(V.b[0][:], bt, rhs, start=True, stop=True).then_inc(V.pe, 1)
                            for h in range(2):
                                mm = pe.matmul(V.b[1][:, h * P:h * P + P], V.qp[:, h, 0, :], bt, start=True, stop=True)
                            mm.then_inc(V.pe, 1)
                            for n, src in enumerate((O.v[:, c], kt, bt)):
                                mm = pe.transpose(V.b[2][:, n * P:n * P + P], src, K.ident)
                            mm.then_inc(V.pe, 1)
                        for d in range(2):
                            V, c = U[d], cols(d, k)
                            pe.wait_ge(V.ev, ev0 + 1)
                            pe.matmul(V.b[0][:], O.kt[d][:, c], V.qp.rearrange("p h q t -> p (h q t)"), start=True,
                                      stop=True).then_inc(V.pe, 1)
                        for lv in range(LEVELS):
                            for d in range(2):
                                V = U[d]
                                pe.wait_ge(V.ev, ev0 + (4 + 2 * lv if lv else 3))
                                for h in range(2):
                                    mm = pe.matmul(V.b[1][:, h * P:h * P + P], V.bqr[:, h, 0, :], V.tx[:, 0, h, :],
                                                   start=True, stop=True)
                                mm.then_inc(V.pe, 1)
                                if lv == 0:
                                    pe.wait_ge(V.ev, ev0 + 4)
                                for h in range(2):
                                    mm = pe.transpose(V.b[0][:, (2 + h) * P:(3 + h) * P], V.tx[:, 0, h, :], K.ident)
                                mm.then_inc(V.pe, 1)
                            if lv == 0:
                                for d in range(2):
                                    V, c = U[d], cols(d, k)
                                    pe.wait_ge(V.ac, ac0 + 3)
                                    out = V.b[2][:, 0:P]
                                    pe.matmul(out, O.sgm[:, 2 * d, c], V.s[:], start=True, stop=False)
                                    for h in range(2):
                                        mm = pe.matmul(out, V.kqr[:, h, 0, :], V.vp[:, h, :], start=False, stop=h == 1)
                                    mm.then_inc(V.pe, 1)
                            between(k, lv)
                            for d in range(2):
                                V = U[d]
                                pe.wait_ge(V.ev, ev0 + (5 + 2 * lv))
                                pe.wait_ge(V.ac, ac0 + (6 + lv if lv else 4))
                                for h in range(2):
                                    T_or_X = (V.tx[:, 1, h, :], V.y[:, h, :])
                                    lhs, rhs = T_or_X if lv < LEVELS - 1 else T_or_X[::-1]
                                    mm = pe.matmul(V.b[0][:, h * P:h * P + P], lhs, rhs, start=True, stop=True)
                                mm.then_inc(V.pe, 1)
                        for d in range(2):
                            V = U[d]
                            pe.wait_ge(V.ev, ev0 + (EV_U - 3))
                            pe.wait_ge(V.ac, ac0 + 6)
                            for h in range(2):
                                mm = pe.matmul(V.b[2][:, P:2 * P], V.tx[:, 1, h, :], V.rp[:, h, :], start=h == 0,
                                               stop=h == 1)
                            mm.then_inc(V.pe, 1)
                        for d in range(2):
                            V, c = U[d], cols(d, k)
                            out = V.b[2][:, 2 * P:3 * P]
                            pe.wait_ge(V.ac, ac0 + AC_U)
                            pe.matmul(out, V.s[:], O.cs[:, d, c], start=True, stop=False)
                            for h in range(2):
                                pe.matmul(out, V.vp[:, h, :], V.kqr[:, h, 1, :], start=False, stop=False)
                            for h in range(2):
                                mm = pe.matmul(out, V.sp[:, h, :], V.bqr[:, h, 1, :], start=False, stop=h == 1)
                            mm.then_inc(V.pe, 1)
                            out = V.b[2][:, 3 * P:4 * P]
                            pe.matmul(out, V.tok[:, 1, :], V.tok[:, 0, :], start=True, stop=False)
                            for h in range(2):
                                mm = pe.matmul(out, V.tok[:, 2, :], V.sp[:, h, :], start=False, stop=h == 1)
                            mm.then_inc(V.pe, 1)
                blocks(pe, prepare, units)

            @block.scalar
            def _(act):
                act.wait_ge(S.zeros, 9)

                def prepare(c, g, k, step):
                    O = B[g]

                    def col(name, d):
                        return K.pcol(name, 2 * RB)[:, at(c + d * RB, 1)]

                    def op(out, src, func, *waits, **scaling):
                        for sem, value in waits:
                            act.wait_ge(sem, value)
                        if src is None:
                            for ps, sl in both:
                                ins = act.activation(out[:, sl], ps, func, **scaling)
                        else:
                            ins = act.activation(out, src, func, **scaling)
                        ins.then_inc(S.pa, 1)
                    pe = lambda name: (S.pp, prep("pe", c, name))
                    dve = lambda name: (S.pd, prep("dve", c, name))
                    pool = lambda name: (S.pq, prep("pool", c, name))

                    def decay(d):
                        op(O.sgm[:, 2 * d, :], None, ACT.Sigmoid, pe(f"decay{d}"), bias=col("w0", d))

                    def rate(d):
                        op(O.sgm[:, 2 * d + 1, :], None, ACT.Sigmoid, pe(f"rate{d}"), bias=col("a0", d))

                    def power(out, src, sign, *waits):
                        op(out, src, ACT.Exp, *waits, scale=sign * DECAY)
                    q, sums = [O.sgm[:, 0, :], O.sgm[:, 2, :]], [O.cs[:, 0, :], O.cs[:, 1, :]]
                    here = (k, step)
                    if here == (0, 0):
                        op(O.v, u[:, at(c + 2 * RB, 1), :].rearrange("p a t -> p (a t)"), ACT.Copy)
                    if here == (0, 1):
                        op(tmp, kk, ACT.Square, dve("kk"))
                    if here in ((0, 2), (1, 2)):
                        decay(k)
                    if here in ((0, 5), (1, 5)):
                        rate(k)
                    if here == (2, 2):
                        op(tmp, None, ACT.Sqrt, pe("norm"))
                    for d, turns in enumerate((((2, 3), (2, 4), (2, 5)), ((3, 0), (3, 1), (3, 2)))):
                        if here == turns[0]:
                            power(wi[:, d, :], sums[d], 1, dve(f"sum{d}"))
                        if here == turns[1]:
                            power(sums[d], sums[d], -1, pool(f"before{d}"), (S.pa, prep("act", c, f"wi{d}")))
                        if here == turns[2]:
                            power(q[d], q[d], -1)

                def units(b, g, between):
                    for k in range(NCH):
                        pe0 = unit(b, k, PE_U, 1)
                        for d in range(2):
                            V = U[d]
                            act.wait_ge(V.pe, pe0 + 3)
                            act.activation(V.tok.rearrange("p n c -> p (n c)"), V.b[2][:, 0:3 * P],
                                           ACT.Copy).then_inc(V.ac, 1)
                            for h in range(2):
                                hc = slice(64 * h, 64 * h + 64)
                                act.activation(V.vp[:, h, hc], V.b[2][:, hc], ACT.Copy).then_inc(V.ac, 1)
                        for lv in range(LEVELS):
                            for d in range(2):
                                V = U[d]
                                act.wait_ge(V.pe, pe0 + (7 + 3 * lv if lv else 6))
                                act.activation(V.tx[:, 1].rearrange("p h t -> p (h t)"), V.b[0][:, 2 * P:],
                                               ACT.Copy).then_inc(V.ac, 1)
                            if lv == 0:
                                for d in range(2):
                                    V = U[d]
                                    act.wait_ge(V.pe, pe0 + 7)
                                    for h in range(2):
                                        hc = slice(64 * h, 64 * h + 64)
                                        act.activation(V.rp[:, h, hc], V.b[2][:, hc], ACT.Copy).then_inc(V.ac, 1)
                            between(k, lv)
                        for d in range(2):
                            V = U[d]
                            act.wait_ge(V.pe, pe0 + (PE_U - 2))
                            for h in range(2):
                                act.activation(V.sp[:, h, 64 * h:64 * h + 64], V.b[2][:, P + 64 * h:P + 64 * h + 64],
                                               ACT.Copy, scale=-1.0).then_inc(V.ac, 1)
                blocks(act, prepare, units)

            @block.vector
            def _(dve):
                dve.tensor_scalar(omk[:], K.pcol("k_a", RB), -1.0, 1.0, ALU.mult, ALU.add).then_inc(S.omk, 1)
                dve.wait_ge(S.omk, 1)
                dve.wait_ge(S.tables, 32)
                for d in range(2):
                    dve.sem_inc(U[d].ev, 1)

                def prepare(c, g, k, step):
                    O = B[g]
                    row = lambda n: u[:, at(c + n * RB, 1), :].rearrange("p a t -> p (a t)")
                    col = lambda name: K.pcol(name, RB)[:, at(c, 1)]
                    act = lambda name: dve.wait_ge(S.pa, prep("act", c, name))
                    own = lambda name: dve.wait_ge(S.pd, prep("dve", c, name))

                    def done(ins):
                        ins.then_inc(S.pd, 1)

                    def sums(d, chunks):
                        act(f"decay{d}")
                        for ch in chunks:
                            way = slice(ch * CH, (ch + 1) * CH)
                            if d:
                                way = slice((ch + 1) * CH - 1, ch * CH - 1 if ch else None, -1)
                            ins = dve.tensor_tensor_scan(O.cs[:, d, way], K.ones, O.sgm[:, 2 * d, way], 0.0,
                                                         ALU.mult, ALU.add)
                        if NCH - 1 in chunks:
                            done(ins)

                    def inverse(parts):
                        own("max")
                        for n in parts:
                            sl = slice(n * CH, (n + 1) * CH)
                            ins = dve.reciprocal(tmp[:, sl], tmp[:, sl])
                        if NCH - 1 in parts:
                            done(ins)

                    def key(d):
                        act(f"rate{d}")
                        done(dve.tensor_scalar(O.kt[d], O.sgm[:, 2 * d + 1, :], col("k_a"), omk[:, at(c, 1)],
                                               ALU.mult, ALU.add))

                    def key_times(d):
                        own(f"kt{d}")
                        done(dve.tensor_tensor(O.kt[d], O.kt[d], row(1), ALU.mult))

                    def last(d):
                        act(f"w{d}")
                        t = 0 if d else CH - 1
                        done(dve.tensor_copy(O.wlast[:, d, :], O.cs[:, d, :].rearrange("p (c t) -> p c t", t=CH)[:, :, t]))

                    def read_times(d):
                        own(f"last{d}")
                        done(dve.tensor_tensor(O.cs[:, d, :], O.cs[:, d, :], row(0), ALU.mult))
                    here = (k, step)
                    if here == (0, 0):
                        done(dve.tensor_scalar(kk, row(1), col("k_k"), None, ALU.mult))
                    if here in ((1, 0), (1, 1)):
                        sums(0, range(3 * step, 3 * step + 3))
                    if here == (1, 2):
                        key(0)
                    if here in ((1, 3), (1, 4)):
                        sums(1, range(3 * (step - 3), 3 * (step - 3) + 3))
                    if here == (1, 5):
                        key_times(0)
                    if here == (2, 1):
                        key(1)
                    if here == (2, 2):
                        key_times(1)
                    if here == (2, 3):
                        act("root")
                        done(dve.tensor_scalar(tmp, tmp, 1e-12, None, ALU.max))
                    if (2, 4) <= here <= (3, 3):
                        inverse((6 * k + step - 16,))
                    if here == (3, 4):
                        last(0)
                    if here == (3, 5):
                        read_times(0)
                    if here == (4, 0):
                        last(1)
                    if here == (4, 1):
                        read_times(1)
                    if here == (4, 3):
                        dve.wait_ge(S.pq, prep("pool", c, "ksum"))
                        done(dve.scalar_tensor_tensor(tmp, tmp, col("r_k"), row(0), ALU.mult, ALU.mult))
                    if here == (5, 1):
                        dve.wait_ge(S.pp, prep("pe", c, "bonus"))
                        for ps, sl in both:
                            ins = dve.tensor_tensor(u[:, at(c, 1), sl], ps.rearrange("p (a t) -> p a t", a=1),
                                                    u[:, at(c + 2 * RB, 1), sl], ALU.mult)
                        done(ins)

                def units(b, g, between):
                    O = B[g]
                    dve.wait_ge(S.pd, prep("dve", b, "bonus"))
                    for d in range(2):
                        dve.memset(U[d].s[:], 0.0).then_inc(S.reset, 1)
                    dve.wait_ge(S.reset, b * 2 + 2)
                    pair = lambda ap: ap.rearrange("p h q t -> p h (q t)")
                    two = lambda ap: ap.rearrange("p (h t) -> p h t", h=2)
                    for k in range(NCH):
                        pe0, ev0 = unit(b, k, PE_U, 1), unit(b, k, EV_U, 1)
                        for d in range(2):
                            V = U[d]
                            tri = masks[:, 2 * d:2 * d + 2, :].rearrange("p q t -> p (q t)")
                            tri = tri.rearrange("p (a c) -> p a c", a=1).broadcast_to([P, 2, 2 * P])
                            dve.wait_ge(V.pe, pe0 + 1)
                            dve.tensor_tensor(pair(V.bqr), two(V.b[0][:]), tri, ALU.mult).then_inc(V.ev, 1)
                            dve.wait_ge(V.pe, pe0 + 2)
                            dve.tensor_tensor(V.tx[:, 0], two(V.b[1][:, 0:2 * P]), heads(levels[:, 0, d, :]),
                                              ALU.mult).then_inc(V.ev, 1)
                            dve.wait_ge(V.ev, ev0 + 2)
                            dve.tensor_tensor(V.tx[:, 0], heads(K.ident), V.tx[:, 0], ALU.subtract).then_inc(V.ev, 1)
                        for d in range(2):
                            V = U[d]
                            tri = masks[:, 2 * d:2 * d + 2, :].rearrange("p q t -> p (q t)")
                            tri = tri.rearrange("p (a c) -> p a c", a=1).broadcast_to([P, 2, 2 * P])
                            dve.wait_ge(V.pe, pe0 + 4)
                            dve.tensor_tensor(pair(V.kqr), two(V.b[0][:]), tri, ALU.mult).then_inc(V.ev, 1)
                        for lv in range(LEVELS):
                            for d in range(2):
                                V = U[d]
                                dve.wait_ge(V.pe, pe0 + (6 + 3 * lv if lv else 5))
                                dve.tensor_tensor(V.y[:], two(V.b[1][:, 0:2 * P]), heads(levels[:, lv + 1, d, :]),
                                                  ALU.mult).then_inc(V.ev, 1)
                            for d in range(2):
                                V = U[d]
                                part = V.tx[:, 0 if lv < LEVELS - 1 else 1]
                                dve.wait_ge(V.pe, pe0 + (8 + 3 * lv))
                                dve.tensor_tensor(part, part, two(V.b[0][:, 0:2 * P]), ALU.subtract).then_inc(V.ev, 1)
                            between(k, lv)
                        for d in range(2):
                            V, c = U[d], cols(d, k)
                            dve.wait_ge(V.pe, pe0 + PE_U)
                            oc = u[:, at(b, 1), c].rearrange("p a t -> p (a t)")
                            dve.tensor_tensor(V.s[:], V.s[:], V.b[2][:, 3 * P:4 * P], ALU.add).then_inc(V.ev, 1)
                            dve.tensor_tensor(oc, oc, V.b[2][:, 2 * P:3 * P], ALU.add).then_inc(V.ev, 1)
                            dve.wait_ge(V.ev, ev0 + (EV_U - 1))
                            ch = ORDER[d][k]
                            dve.scalar_tensor_tensor(V.s[:], V.s[:], O.wlast[:, d, ch:ch + 1], K.bd64, ALU.mult,
                                                     ALU.mult).then_inc(V.ev, 1)
                            dve.wait_ge(V.ev, ev0 + EV_U)
                blocks(dve, prepare, units)


def even_out_phase(K, index, layer):
    nc, A, u = K.nc, K.A, K.u
    (seg,) = K.weights.phases[index]
    post_mods = [(sl, x, K.mod2_cols(layer, v, 2)) for v, (sl, x) in enumerate(((LAT, K.x), (CON, K.xc)))]
    G0, F0, Z0 = RB, 2 * RB, 2 * RB + 4
    NT, NL, NF = TOK // P, SEQ // P, 2
    with phase(K, *norm_names("post"), *SUB_SEMS, *CARRY_SEMS, "four_in", "gates_in", "x_in", "tables", "zc_ps", "zc_ready",
               "mean_ps", "dev_ready", "dev_sq", "stat_ps", "gn_var", "gn_std", "gn_inv", "gn_scaled", "gn_out",
               "four_ps", "m_full", "m_hi", "m_ready") as S:
        K.norm_buffers(S, TOK)
        feat = S.sb("dft_feat", [P, 2 * P])
        lat = S.sb("dft_lat", [P, 2, NL, SEQ])
        con = S.sb("dft_con", [P, 2, NT - NL, CTX])
        mo = S.sb("m", [P, 2, DB, TOK], F32R)
        S.y = u
        wide = [S.psum(f"lat{i}", [P, 512]) for i in range(4)]
        narrow = [S.psum(f"con{i}", [P, 512]) for i in range(4)]
        pair = lambda i: [(wide[i][:], LAT), (narrow[i][:, 0:CTX], CON)]
        zc = u[:, Z0:Z0 + 4, :].rearrange("p b t -> p (b t)")
        var = [K.ssq, K.var]
        out_banks = lambda n: pair(n % 2)

        with nc.Block() as block:

            @block.sync
            def _(sp):
                sp.dma_start(u[:, F0:F0 + 4, :], K.late_dram[RB:RB + 4].rearrange("n p t -> p n t")).then_inc(S.four_in, 16)
                sp.dma_start(feat[:], A["dft_feat"]).then_inc(S.four_in, 16)
                sp.dma_start(u[:, G0:G0 + RB, :], K.late_dram[0:RB].rearrange("n p t -> p n t")).then_inc(S.gates_in, 16)
                for m in range(2):
                    sp.dma_start(lat[:, m], A["dft_lat"][m].rearrange("(t p) l -> p t l", p=P)).then_inc(S.tables, 16)
                    sp.dma_start(con[:, m], A["dft_ctx"][m].rearrange("(t p) l -> p t l", p=P)).then_inc(S.tables, 16)
                sp.dma_start(K.x[:], K.x_dram).then_inc(S.x_in, 16)
                sp.dma_start(K.xc[:], K.xc_dram).then_inc(S.x_in, 16)
                weights_sp(sp, K, index)

            @block.gpsimd
            def _(pool):
                split_all(pool, K, [seg], [(DB,)])
                pool.wait_ge(S.x_in, 32)
                post_pool(pool, K, S, post_mods, after_pre=False)

            @block.scalar
            def _(act):
                for n in range(SPLIT):
                    split_hi(act, K, seg, n, n, 0, DB)
                for t in range(NT):
                    act.wait_ge(S.zc_ps, t + 1)
                    act.activation(zc[:, 512 * t:512 * t + 512], wide[t % 4][:], ACT.Copy).then_inc(S.zc_ready, 1)
                for i in range(RB + 3):
                    if i < RB:
                        act.wait_ge(S.dev_ready, i + 1)
                        if i >= 2:
                            act.wait_ge(S.stat_ps, i - 1)
                        act.activation(K.sq[:, i % 2, :], u[:, i, :], ACT.Square).then_inc(S.dev_sq, 1)
                    if 0 <= i - 1 < RB:
                        act.wait_ge(S.gn_var, i)
                        act.activation(var[(i - 1) % 2][:], var[(i - 1) % 2][:], ACT.Sqrt).then_inc(S.gn_std, 1)
                    j = i - 2
                    if 0 <= j < RB:
                        act.wait_ge(S.gn_scaled, j + 1)
                        act.activation(u[:, j, :], u[:, j, :], ACT.Identity, scale=K.pcol("lnx_g", RB)[:, j:j + 1],
                                       bias=K.pcol("lnx_b", RB)[:, j:j + 1]).then_inc(S.gn_out, 1)
                    j = i - 3
                    if 0 <= j < RB:
                        split_operand_act(act, S, j, u[:, j, :], mo[:, HI, j, :])
                for j in range(NF):
                    split_operand_act(act, S, RB + j, u[:, F0 + 2 + j, :], mo[:, HI, RB + j, :])
                out_act(act, K, S, seg, out_banks, TOK, SPLIT)
                carry_act(act, K, S, post_mods)

            @block.tensor
            def _(pe):
                pe.wait_ge(S.four_in, 32)
                for t in range(NT):
                    if t >= 4:
                        pe.wait_ge(S.zc_ready, t - 3)
                    for j in range(NF):
                        mm = pe.matmul(wide[t % 4][:, 256 * j:256 * j + 256], u[:, F0 + j, t * P:(t + 1) * P], feat[:],
                                       start=True, stop=True)
                    mm.then_inc(S.zc_ps, 1)

                def mean(i):
                    if i >= 2:
                        pe.wait_ge(S.dev_ready, i - 1)
                    for ps, sl in pair(i % 2):
                        mm = pe.matmul(ps, K.bd64, u[:, i, sl], start=True, stop=True)
                    mm.then_inc(S.mean_ps, 1)
                pe.wait_ge(S.zc_ready, NT)
                mean(0)
                mean(1)
                for i in range(RB):
                    pe.wait_ge(S.dev_sq, i + 1)
                    if i >= 2:
                        pe.wait_ge(S.gn_var, i - 1)
                    for ps, sl in pair(2 + i % 2):
                        mm = pe.matmul(ps, K.bd64, K.sq[:, i % 2, sl], start=True, stop=True)
                    mm.then_inc(S.stat_ps, 1)
                    if i + 2 < RB:
                        mean(i + 2)
                pe.wait_ge(S.tables, 64)
                for j in range(NF):
                    pe.wait_ge(S.gn_var, RB - 1 + j)
                    for (ps, _), tab, t0, n in zip(pair(2 + j), (lat, con), (0, NL), (NL, NT - NL)):
                        for t in range(n):
                            for m in range(2):
                                c0 = (t0 + t) * 512 + j * 256 + m * P
                                mm = pe.matmul(ps, zc[:, c0:c0 + P], tab[:, m, t, :], start=t == 0 and m == 0,
                                               stop=t == n - 1 and m == 1)
                    mm.then_inc(S.four_ps, 1)
                pe.wait_ge(S.dev_ready, RB)
                out_pe(pe, K, S, seg, mo, out_banks, S.m_ready)
                norm_pe(pe, S.post, K, wide[2:4], TOK)
                carry_pe(pe, K, S, wide[0], TOK)

            @block.vector
            def _(dve):
                for i in range(RB + 4):
                    if i < RB:
                        dve.wait_ge(S.mean_ps, i + 1)
                        for ps, sl in pair(i % 2):
                            ins = dve.scalar_tensor_tensor(u[:, i, sl], ps, -1.0 / 64, u[:, i, sl], ALU.mult, ALU.add)
                        ins.then_inc(S.dev_ready, 1)
                    j = i - 1
                    if 0 <= j < RB:
                        dve.wait_ge(S.stat_ps, j + 1)
                        if j >= 2:
                            dve.wait_ge(S.gn_scaled, j - 1)
                        for ps, sl in pair(2 + j % 2):
                            ins = dve.tensor_scalar(var[j % 2][:, sl], ps, 1.0 / 64, GN_EPS, ALU.mult, ALU.add)
                        ins.then_inc(S.gn_var, 1)
                    j = i - 2
                    if 0 <= j < RB:
                        dve.wait_ge(S.gn_std, j + 1)
                        dve.reciprocal(var[j % 2][:], var[j % 2][:]).then_inc(S.gn_inv, 1)
                        dve.wait_ge(S.gn_inv, j + 1)
                        dve.tensor_tensor(u[:, j, :], u[:, j, :], var[j % 2][:], ALU.mult).then_inc(S.gn_scaled, 1)
                    j = i - 3
                    if 0 <= j < RB:
                        dve.wait_ge(S.gn_out, j + 1)
                        dve.wait_ge(S.gates_in, 16)
                        dve.tensor_tensor(u[:, j, :], u[:, j, :], u[:, G0 + j, :], ALU.mult).then_inc(S.m_full, 1)
                    j = i - 4
                    if 0 <= j < RB:
                        split_operand_dve(dve, S, j, u[:, j, :], mo[:, HI, j, :], mo[:, LO, j, :])
                dve.wait_ge(S.four_in, 32)
                for j in range(NF):
                    gate = u[:, F0 + 2 + j, :]
                    dve.wait_ge(S.four_ps, j + 1)
                    for ps, sl in pair(2 + j):
                        ins = dve.tensor_tensor(gate[:, sl], ps, gate[:, sl], ALU.mult)
                    ins.then_inc(S.m_full, 1)
                for j in range(NF):
                    split_operand_dve(dve, S, RB + j, u[:, F0 + 2 + j, :], mo[:, HI, RB + j, :], mo[:, LO, RB + j, :])
                dve.wait_ge(S.x_in, 32)
                post_dve(dve, K, S, post_mods, K.pcol("norm_post_2", 2 * DB)[:, layer * DB:][:, 0:DB], None,
                         wide[2:4], after_pre=False)
                carry_dve(dve, K, S, wide[0], TOK)



HEADS = 8
RET_HEAD = D // HEADS
K_SCALE = RET_HEAD ** -0.5


def odd_in_phase(K, index, layer):
    nc, A = K.nc, K.A
    (seg,) = K.weights.phases[index]
    pre_mods = [(sl, x, K.mod2_cols(layer, v, 1), K.mod2_cols(layer, v, 0))
                for v, (sl, x) in enumerate(((LAT, K.x), (CON, K.xc)))]
    with phase(K, *norm_names("pre"), *SUB_SEMS, "tables", "q_copied", "k_copied", "v_copied", "gate_ready",
               "gate_out0", "gate_out1", "rot_ps", "turned", "steps") as S:
        K.norm_buffers(S, TOK)
        S.h = S.sb("h", [P, 2, DB, TOK], F32R)
        rope = S.sb("rope", [P, 2, SEQ])
        rot = S.sb("rot", [P, P])
        plain = S.sb("plain", [P, 2, SEQ])
        part = S.sb("part", [P, 2, SEQ])
        stage = S.sb("gate", [P, 2, SEQ])
        lat = [S.psum(f"lat{i}", [P, 512]) for i in range(4)]
        con = [S.psum(f"con{i}", [P, 512]) for i in range(2)]
        turn_ps = [S.psum(f"rot{i}", [P, 512]) for i in range(2)]
        gate_out = (S.gate_out0, S.gate_out1)
        outs = [[(lat[0][:], LAT)], [(lat[1][:], LAT), (con[0][:, 0:CTX], CON)],
                [(lat[2][:], LAT), (con[1][:, 0:CTX], CON)], [(lat[3][:], LAT)]]
        Q, KEY, V, G = range(4)

        with nc.Block() as block:

            @block.sync
            def _(sp):
                sp.dma_start(rope[:], A["rope"].rearrange("m p t -> p m t")).then_inc(S.tables, 16)
                sp.dma_start(rot[:], A["rot"]).then_inc(S.tables, 16)
                weights_sp(sp, K, index)

            @block.gpsimd
            def _(pool):
                split_all(pool, K, [seg], [(DB,) * 4])

            @block.scalar
            def _(act):
                for j in range(SPLIT):
                    split_hi(act, K, seg, 0, 0, j, DB)
                pre_act(act, K, S, pre_mods, True)

                def turn(i, s, last=False):
                    def ahead(j):
                        if j + SPLIT < 4:
                            split_hi(act, K, seg, i, s, j + SPLIT, DB)
                        elif not last:
                            split_hi(act, K, seg, i + 1, s + 1, j + SPLIT - 4, DB)
                    act.wait_ge(K.chunks_done, seg.base + 4 * i + Q + 1)
                    if s:
                        act.wait_ge(S.turned, 2 * i)
                    act.activation(plain[:, 0, :], lat[Q][:], ACT.Copy).then_inc(S.q_copied, 1)
                    ahead(Q)
                    act.wait_ge(K.chunks_done, seg.base + 4 * i + KEY + 1)
                    act.activation(plain[:, 1, :], lat[KEY][:], ACT.Copy, scale=K_SCALE).then_inc(S.k_copied, 1)
                    act.activation(K.k[:, at(i, 1), CON], con[0][:, 0:CTX], ACT.Copy, scale=K_SCALE).then_inc(S.k_copied, 1)
                    ahead(KEY)
                    act.wait_ge(K.chunks_done, seg.base + 4 * i + V + 1)
                    for ps, sl in outs[V]:
                        ins = act.activation(K.v[:, at(i, 1), sl], ps, ACT.Copy)
                    ins.then_inc(S.v_copied, 1)
                    ahead(V)
                    act.wait_ge(K.chunks_done, seg.base + 4 * i + G + 1)
                    if s >= 2:
                        act.wait_ge(gate_out[s % 2], (i - s % 2) * 8)
                    act.activation(stage[:, s % 2, :], lat[G][:], ACT.Silu).then_inc(S.gate_ready, 1)
                    ahead(G)
                    act.wait_ge(S.gate_ready, i + 1)
                    act.dma_start(K.gate_dram[at(i, 1)].rearrange("a p t -> p (a t)"),
                                  stage[:, s % 2, :]).then_inc(gate_out[s % 2], 16)
                turn(0, 0)
                turn(1, 1)
                loop(act, 2, HEADS - 2, 2, turn)
                turn(HEADS - 2, HEADS - 2)
                turn(HEADS - 1, HEADS - 1, last=True)
                for o in gate_out:
                    act.wait_ge(o, 16 * HEADS // 2)

            @block.tensor
            def _(pe):
                norm_pe(pe, S.pre, K, turn_ps, TOK, True)
                pe.wait_ge(S.tables, 32)

                def turn(i, s):
                    def project(j, read, count):
                        if s:
                            pe.wait_ge(read, count)
                        multiply(pe, K, seg, i, s, j, DB, outs[j], lambda p, k, sl: S.h[:, p, k, sl],
                                 before=(lambda k: pe.wait_ge(S.h_ready, k + 1)) if s == 0 and j == 0 else None)

                    def rotate(n, ready, count):
                        pe.wait_ge(ready, count)
                        pe.matmul(turn_ps[n][:], rot[:], plain[:, n, :], start=True, stop=True).then_inc(S.rot_ps, 1)
                    project(Q, S.q_copied, i)
                    project(KEY, S.k_copied, 2 * i)
                    rotate(0, S.q_copied, i + 1)
                    project(V, S.v_copied, i)
                    rotate(1, S.k_copied, 2 * i + 2)
                    project(G, S.gate_ready, i)
                turn(0, 0)
                turn(1, 1)
                loop(pe, 2, HEADS, 2, turn)

            @block.vector
            def _(dve):
                pre_dve(dve, K, S, pre_mods, K.pcol("norm_pre_2", 2 * DB)[:, layer * DB:][:, 0:DB], turn_ps,
                        True)
                dve.wait_ge(S.tables, 32)

                def turn(i, s):
                    for n, dst in enumerate((K.q, K.k)):
                        dve.wait_ge(S.rot_ps, 2 * i + (n + 1))
                        one = dst[:, at(i, 1), LAT].rearrange("p a t -> p (a t)")
                        dve.tensor_tensor(one, plain[:, n, :], rope[:, 0, :], ALU.mult).then_inc(S.steps, 1)
                        dve.tensor_tensor(part[:, n, :], turn_ps[n][:], rope[:, 1, :], ALU.mult).then_inc(S.steps, 1)
                        dve.wait_ge(S.steps, i * 4 + (2 * n + 2))
                        dve.tensor_tensor(one, one, part[:, n, :], ALU.add).then_inc(S.turned, 1)
                loop(dve, 0, HEADS, 2, turn)


def odd_out_phase(K, index, layer):
    nc, A = K.nc, K.A
    (seg,) = K.weights.phases[index]
    post_mods = [(LAT, K.x, K.mod2_cols(layer, 0, 2))]
    NL, NT = SEQ // CH, TOK // CH
    ORDER = ((4, 5, 0, 1, 2), (5, 4, 3, 2, 1))
    with phase(K, *norm_names("post"), *SUB_SEMS, "logits", "tables", "lg", "steps", "decays", "made", "gate_in0",
               "gate_in1", "pe_a", "pe_kv", "pe_o", "pe_s", "act_a", "act_o", "act_std", "xi_ready", "sc_ready",
               "states", "var", "inv", "m_full", "m_hi", "m_ready") as S:
        K.norm_buffers(S, SEQ)
        S.y = K.q
        mo = S.sb("m", [P, 2, DB, SEQ], F32R)
        gates = S.sb("gates", [P, 2, SEQ])
        dmask = S.sb("decay_pairs", [P, HEADS, P])
        xi = S.sb("xi", [P, 2, HEADS, P])
        zeta = S.sb("zeta", [P, 2, HEADS])
        gch = S.sb("g_chunk", [P, 2, HEADS])
        lg = S.sb("log_decay", [P, 6, 2 * HEADS])
        vt = S.sb("v_tok", [P, NT, P])
        kz = S.sb("k_zeta", [P, 2, NT, P])
        qx = S.sb("q_xi", [P, 2, SEQ])
        sc = S.sb("scores", [P, SEQ])
        st = S.sb("states", [P, 2, NL, P])
        o = S.sb("o", [P, SEQ])
        tabs = K.sq.rearrange("p a t -> p (a t)")
        dist, pos, low, high = (tabs[:, a * P:b * P] for a, b in ((0, 1), (1, 3), (3, 4), (4, 5)))
        work = tabs[:, 5 * P:7 * P]
        b = [S.psum(f"b{i}", [P, 512]) for i in range(8)]
        v_ps, mix_ps, k_ps, sc_ps, o_ps, ss_ps = b[0], b[1], b[2], b[3], b[4], b[5]
        kv_ps = b[0:3]
        out_banks = lambda n: [(b[6 + n % 2][:], LAT)]
        gate_in = (S.gate_in0, S.gate_in1)

        def kv(d, n):
            c0 = (d * 5 + n) * P
            return kv_ps[c0 // 512][:, c0 % 512:c0 % 512 + P]

        with nc.Block() as block:

            @block.sync
            def _(sp):
                sp.dma_start(lg[:, 5, :], A["od_decay_logit_2"].rearrange("a d h -> a (d h)").broadcast_to(
                    [P, 2 * HEADS])).then_inc(S.logits, 16)
                for dst, src in ((dist, A["dist"]), (pos[:, 0:P], A["posrow"][0]), (pos[:, P:], A["posrow"][1]),
                                 (low, A["masks"][1]), (high, A["masks"][2])):
                    sp.dma_start(dst, src).then_inc(S.tables, 16)

                def turn(i, s):
                    if s >= 2:
                        sp.wait_ge(S.m_full, i - 1)
                    sp.dma_start(gates[:, s % 2, :], K.gate_dram[at(i, 1)].rearrange("a p t -> p (a t)")).then_inc(
                        gate_in[s % 2], 16)
                turn(0, 0)
                turn(1, 1)
                loop(sp, 2, HEADS, 2, turn)
                weights_sp(sp, K, index)

            @block.gpsimd
            def _(pool):
                def turn(i, s):
                    if s:
                        pool.wait_ge(S.pe_o, i)
                    else:
                        pool.wait_ge(S.decays, 4 * HEADS)
                    one = K.q[:, at(i, 1), :].rearrange("p a (c t) -> p (a c) t", t=CH)
                    for d in range(2):
                        pool.tensor_tensor(qx[:, d, :].rearrange("p (c t) -> p c t", t=CH), one,
                                           xi[:, d, at(i, 1), :].broadcast_to([P, NL, CH]), ALU.mult).then_inc(S.xi_ready, 1)
                turn(0, 0)
                loop(pool, 1, HEADS, 1, turn)
                split_all(pool, K, [seg], [(DB,)])
                post_pool(pool, K, S, post_mods, after_pre=False)

            @block.scalar
            def _(act):
                for n in range(SPLIT):
                    split_hi(act, K, seg, n, n, 0, DB)
                act.wait_ge(S.logits, 16)
                act.activation(lg[:, 0, :], lg[:, 5, :], ACT.Abs).then_inc(S.lg, 1)
                act.wait_ge(S.lg, 1)
                act.activation(lg[:, 1, :], lg[:, 0, :], ACT.Exp, scale=-1.0).then_inc(S.lg, 1)
                act.wait_ge(S.steps, LRU_SCALE_STEPS)
                act.wait_ge(S.tables, 80)
                for d in range(2):
                    rows = lg[:, 0, d * HEADS:(d + 1) * HEADS]
                    act.activation(gch[:, d, :], rows, ACT.Exp, scale=float(CH))
                    act.activation(zeta[:, d, :], rows, ACT.Exp, scale=(K.rpos, K.pos)[d])
                for h in range(HEADS):
                    for d in range(2):
                        act.activation(xi[:, d, h, :], pos[:, d * P:(d + 1) * P], ACT.Exp,
                                       scale=lg[:, 0, d * HEADS + h:d * HEADS + h + 1]).then_inc(S.decays, 1)
                    for d in range(2):
                        if h:
                            act.wait_ge(S.made, 2 * h)
                        act.activation(work[:, d * P:(d + 1) * P], dist, ACT.Exp,
                                       scale=lg[:, 0, d * HEADS + h:d * HEADS + h + 1]).then_inc(S.decays, 1)

                def first(i):
                    act.wait_ge(S.pe_a, 2 * i + 1)
                    act.activation(vt[:, 0:4, :].rearrange("p c d -> p (c d)"), v_ps[:], ACT.Copy)
                    act.activation(vt[:, 4:6, :].rearrange("p c d -> p (c d)"), mix_ps[:, 0:256], ACT.Copy)
                    for d in range(2):
                        col = zeta[:, d, at(i, 1)]
                        act.activation(kz[:, d, 0:4, :].rearrange("p c d -> p (c d)"), k_ps[:], ACT.Copy, scale=col)
                        ins = act.activation(kz[:, d, 4:6, :].rearrange("p c d -> p (c d)"), mix_ps[:, 256:512],
                                             ACT.Copy, scale=col)
                    ins.then_inc(S.act_a, 1)

                def second(i, first_head=False):
                    act.wait_ge(S.pe_o, i + 1)
                    if not first_head:
                        act.wait_ge(S.m_ready, i)
                    act.activation(o[:], o_ps[:], ACT.Copy).then_inc(S.act_o, 1)
                    act.activation(K.ssq[:], o_ps[:], ACT.Square).then_inc(S.act_o, 1)

                def third(i):
                    act.wait_ge(S.var, i + 1)
                    act.activation(K.var[:], K.var[:], ACT.Sqrt).then_inc(S.act_std, 1)
                    act.wait_ge(S.m_full, i + 1)
                    act.activation(mo[:, HI, at(i, 1), :], o[:], ACT.Copy).then_inc(S.m_hi, 1)

                first(0)
                second(0, True)

                def turn(i, s):
                    first(i)
                    third(i - 1)
                    second(i)
                loop(act, 1, HEADS, 1, turn)
                third(HEADS - 1)
                out_act(act, K, S, seg, out_banks, SEQ, SPLIT)

            @block.tensor
            def _(pe):
                def first(i):
                    if i:
                        pe.wait_ge(S.states, i)
                    one, key = K.v[:, at(i, 1), :], K.k[:, at(i, 1), :]
                    flat = lambda ap, c: ap.rearrange("p a t -> p (a t)")[:, c * CH:(c + 1) * CH]
                    for c in range(NT):
                        dv = v_ps[:, c * P:(c + 1) * P] if c < 4 else mix_ps[:, (c - 4) * P:(c - 3) * P]
                        dk = k_ps[:, c * P:(c + 1) * P] if c < 4 else mix_ps[:, (c - 2) * P:(c - 1) * P]
                        pe.transpose(dv, flat(one, c), K.ident)
                        mm = pe.transpose(dk, flat(key, c), K.ident)
                    mm.then_inc(S.pe_a, 1)
                    if i:
                        pe.wait_ge(S.sc_ready, i)
                    for c in range(NL):
                        mm = pe.matmul(sc_ps[:, c * P:(c + 1) * P], flat(key, c), flat(K.q[:, at(i, 1), :], c),
                                       start=True, stop=True)
                    mm.then_inc(S.pe_a, 1)

                def products(i):
                    pe.wait_ge(S.act_a, i + 1)
                    for d in range(2):
                        for n, c in enumerate(ORDER[d]):
                            mm = pe.matmul(kv(d, n), kz[:, d, c, :], vt[:, c, :], start=True, stop=True)
                    mm.then_inc(S.pe_kv, 1)

                def outputs(i):
                    pe.wait_ge(S.sc_ready, i + 1)
                    pe.wait_ge(S.xi_ready, 2 * i + 2)
                    pe.wait_ge(S.states, i + 1)
                    if i:
                        pe.wait_ge(S.act_o, 2 * i)
                    for c in range(NL):
                        out, cs = o_ps[:, c * P:(c + 1) * P], slice(c * CH, (c + 1) * CH)
                        pe.matmul(out, vt[:, c, :], sc[:, cs], start=True, stop=False)
                        pe.matmul(out, st[:, 0, c, :], qx[:, 0, cs], start=False, stop=False)
                        mm = pe.matmul(out, st[:, 1, c, :], qx[:, 1, cs], start=False, stop=True)
                    mm.then_inc(S.pe_o, 1)

                def sums(i):
                    pe.wait_ge(S.act_o, 2 * i + 2)
                    if i:
                        pe.wait_ge(S.var, i)
                    pe.matmul(ss_ps[:], K.ones, K.ssq[:], start=True, stop=True).then_inc(S.pe_s, 1)
                first(0)
                products(0)
                outputs(0)

                for i in range(1, HEADS):
                    first(i)
                    sums(i - 1)
                    products(i)
                    outputs(i)
                sums(HEADS - 1)
                out_pe(pe, K, S, seg, mo, out_banks, S.m_ready)
                norm_pe(pe, S.post, K, [ss_ps], SEQ)

            @block.vector
            def _(dve):
                steps = Steps(dve, S.steps)
                dve.wait_ge(S.lg, 2)
                lru_scale(dve, steps, lg[:, 5, :], [lg[:, q, :] for q in range(5)], lg[:, 0, :])
                assert steps.n == LRU_SCALE_STEPS
                dve.wait_ge(S.tables, 80)
                for h in range(HEADS):
                    for d in range(2):
                        dve.wait_ge(S.decays, 4 * h + 3 + d)
                        tri = (low, high)[d]
                        steps(dve.tensor_tensor(work[:, d * P:(d + 1) * P], work[:, d * P:(d + 1) * P], tri, ALU.mult))
                    dve.tensor_tensor(dmask[:, h, :], work[:, 0:P], work[:, P:], ALU.add).then_inc(S.made, 2)

                def first(i, first_head=False):
                    dve.wait_ge(S.pe_a, 2 * i + 2)
                    if not first_head:
                        dve.wait_ge(S.pe_o, i)
                    dve.tensor_tensor(sc.rearrange("p (c t) -> p c t", t=CH), sc_ps.rearrange("p (c t) -> p c t", t=CH),
                                      dmask[:, at(i, 1), :].broadcast_to([P, NL, CH]), ALU.mult).then_inc(S.sc_ready, 1)

                def chain(i):
                    dve.wait_ge(S.pe_kv, i + 1)
                    base = i * 8 + (LRU_SCALE_STEPS + 2 * HEADS)
                    chain_steps = Steps(dve, S.steps, base)
                    for d in range(2):
                        g = gch[:, d, at(i, 1)]
                        way = [0, 1, 2, 3] if d == 0 else [3, 2, 1, 0]
                        chain_steps(dve.tensor_copy(st[:, d, way[0], :], kv(d, 0)))
                        chain_steps(dve.scalar_tensor_tensor(st[:, d, way[0], :], st[:, d, way[0], :], g, kv(d, 1),
                                                             ALU.mult, ALU.add))
                        for n in range(1, NL):
                            ins = dve.scalar_tensor_tensor(st[:, d, way[n], :], st[:, d, way[n - 1], :], g, kv(d, n + 1),
                                                           ALU.mult, ALU.add)
                            if n < NL - 1:
                                chain_steps(ins)
                    ins.then_inc(S.states, 1)

                def norm(i):
                    dve.wait_ge(S.pe_s, i + 1)
                    dve.tensor_scalar(K.var[:], ss_ps[:], 1.0 / RET_HEAD, EPS, ALU.mult, ALU.add).then_inc(S.var, 1)

                def finish(i, s):
                    dve.wait_ge(S.act_std, i + 1)
                    dve.reciprocal(K.var[:], K.var[:]).then_inc(S.inv, 1)
                    dve.wait_ge(S.inv, 2 * i + 1)
                    dve.tensor_tensor(o[:], o[:], K.var[:], ALU.mult).then_inc(S.inv, 1)
                    dve.wait_ge(gate_in[s % 2], (i - s % 2) * 8 + 16)
                    dve.wait_ge(S.inv, 2 * i + 2)
                    dve.tensor_tensor(o[:], o[:], gates[:, s % 2, :], ALU.mult).then_inc(S.m_full, 1)
                    dve.wait_ge(S.m_hi, i + 1)
                    dve.tensor_tensor(mo[:, LO, at(i, 1), :], o[:], mo[:, HI, at(i, 1), :].bitcast(F32),
                                      ALU.subtract).then_inc(S.m_ready, 1)
                first(0, True)
                chain(0)

                def turn(i, s):
                    first(i)
                    norm(i - 1)
                    finish(i - 1, s - 1)
                    chain(i)
                loop(dve, 1, HEADS, 2, turn)
                norm(HEADS - 1)
                finish(HEADS - 1, HEADS - 1)
                post_dve(dve, K, S, post_mods, K.pcol("norm_post_2", 2 * DB)[:, layer * DB:][:, 0:DB], None,
                         [ss_ps], after_pre=False)



class AdaSource:

    def __init__(self, weights, first, use, bias, out):
        self.w = weights.rearrange("(k p) c -> p k c", p=P)
        self.first, self.use, self.vecs = first, use, len(use)
        self.bias_cols, self.out_cols = bias, out

    def __call__(self, i):
        return self.w[:, :, at((i + self.first) * ADA_W, ADA_W)]

    def bias(self, i):
        return self.bias_cols[:, at((i + self.first) * 2, 2)]

    def out(self, i):
        return lambda v: self.out_cols(v)[:, at((i + self.first) * 2, 2)]


def second_block(K, ctx, first):
    with ExitStack() as even:
        K.xc = K.sbuf(ctx, "x_context", [P, DB, CTX])
        K.u = K.sbuf(even, "u", [P, SHIFT_BLOCKS, TOK])
        run = [lambda: even_in_phase(K, first, 0), lambda: even_scan_phase(K), lambda: even_out_phase(K, first + 1, 0)]
        for f in run:
            f()
    K.q = K.sbuf(ctx, "q", [P, HEADS, SEQ])
    K.k = K.sbuf(ctx, "k", [P, HEADS, TOK])
    K.v = K.sbuf(ctx, "v", [P, HEADS, TOK])
    odd_in_phase(K, first + 2, 1)
    odd_out_phase(K, first + 3, 1)


def build(nc, A, out):
    with ExitStack() as ctx:
        K = Names(nc=nc, A=A, out=out, serial=0)

        def sbuf(c, name, shape, dt=F32):
            K.serial += 1
            return c.enter_context(nc.sbuf_tensor(f"{name}_{K.serial}", shape, dt))

        def psum(c, name, shape, dt=F32):
            K.serial += 1
            return c.enter_context(nc.psum_tensor(f"{name}_{K.serial}", shape, dt))

        K.sbuf, K.psum = sbuf, psum
        sb = lambda name, shape, dt=F32: sbuf(ctx, name, shape, dt)
        sem = lambda name: ctx.enter_context(nc.semaphore(name))

        K.pool_sem = sem

        K.x = sb("x", [P, DB, SEQ])
        K.raw = sb("w_raw", [P, RAW, DB, P])
        K.w_hi = sb("w_hi", [P, SPLIT, DB, P], F32R)
        K.w_lo = sb("w_lo", [P, SPLIT, DB, P], F32R)
        K.params = sb("params", [P, len(PARAM_PAGES) * P])
        K.const = sb("const", [P, CONST_W])
        K.mods = sb("mods", [P, 144])
        K.mods2 = sb("mods2", [P, 2, 48])
        K.cact = sb("c_act", [P, 3, DB])
        K.fac = sb("fac", [P, 2, DB])
        K.fac2 = sb("fac2", [P, 2, DB])
        K.rstd = sb("norm_factors", [P, TOK // P])

        def const(name):
            c0, n = CONST_COLS[name]
            return K.const[:, c0:c0 + n]
        K.ident, K.ones, K.bd64 = const("ident"), const("ones"), const("bd64")
        K.shift4, K.shift2, K.pos, K.rpos = const("shift4"), const("shift2"), const("pos"), const("rpos")

        def pcol(name, n):
            return K.params[:, PARAM_AT[name]:PARAM_AT[name] + n]
        K.pcol = pcol

        def mod_cols(layer, sub, kind):
            c0 = layer * 72 + (sub * 3 + kind) * DB
            return K.mods[:, c0:c0 + DB]
        K.mod_cols = mod_cols

        def mod2_cols(layer, v, kind):
            c0 = layer * 24 + kind * DB
            return K.mods2[:, v, c0:c0 + DB]
        K.mod2_cols = mod2_cols
        K.x_dram = nc.dram_tensor("x_wait", (P, DB, SEQ), F32, kind="Internal").ap()
        K.gate_dram = nc.dram_tensor("gate_wait", (HEADS, P, SEQ), F32, kind="Internal").ap()
        K.xc_dram = nc.dram_tensor("x_context_wait", (P, DB, CTX), F32, kind="Internal").ap()
        K.late_dram = nc.dram_tensor("late_wait", (EVEN_BLOCKS - SHIFT_BLOCKS, P, TOK), F32, kind="Internal").ap()

        def norm_buffers(S, width):
            K.sq = S.sb("sq", [P, 2, width])
            K.ssq = S.sb("ssq", [P, width])
            K.var = S.sb("var", [P, width])
        K.norm_buffers = norm_buffers

        K.landed = [sem(f"landed{i}") for i in range(RAW)]
        K.hi_ready, K.lo_ready, K.chunks_done = sem("hi_ready"), sem("lo_ready"), sem("chunks_done")
        K.ada_landed = [sem(f"ada_landed{i}") for i in range(ADA)]
        K.ada_used, K.ada_total = sem("ada_used"), sem("ada_total")
        K.local_n = 60
        local = [nc.alloc_semaphore(name=f"local{i}") for i in range(K.local_n)]
        K.local0 = local[0].num
        assert [h.num for h in local] == list(range(K.local0, K.local0 + K.local_n))
        for h in local:
            nc.release_semaphore(h)

        def rows(name):
            rows128 = lambda ap: ap.rearrange("(r c) -> r c", c=P)
            one = {
                "a_conv_b": "a_conv_b", "b_conv_b": "b_conv_b", "b_norm_g": "b_norm_g", "b_norm_b": "b_norm_b",
                "a_lam": "a_lam", "c_b_in": "c_b_in", "c_norm_g": "c_norm_g", "c_norm_b": "c_norm_b",
                "c": "c", "c_2": "c_2", "k_k": "ev_k_k_2", "k_a": "ev_k_a_2", "mu": "ev_mu_2",
                "lnx_g": "ev_lnx_g_2", "lnx_b": "ev_lnx_b_2",
            }
            two = {"norm_pre_2": "norm_pre_2", "norm_post_2": "norm_post_2", "ada_b_2": "ada_b_2"}
            if name in ("ada_b0", "ada_b1"):
                return [(0, 72, rows128(A["ada_b"][int(name[-1])]))]
            if name in one:
                src = rows128(A[one[name]][0])
            elif name in two:
                src = A[two[name]].rearrange("l (r c) -> (l r) c", c=P)
            elif name in ("norm_pre", "norm_post"):
                src = A[name].rearrange("l s (r c) -> (l s r) c", c=P)
            elif name == "c_ctx":
                src = rows128(A["c_ctx_2"])
            elif name in ("a_conv_w", "b_conv_w"):
                src = A[name][0].rearrange("k (r c) -> (k r) c", c=P)
            elif name in ("w0", "a0"):
                src = A[f"ev_{name}_2"][0].rearrange("d (r c) -> (d r) c", c=P)
            elif name == "r_k":
                src = A["ev_r_k_2"][0].rearrange("(r t) c -> r (t c)", t=2)
            else:
                g = {"gate_br": 0, "gate_bi": 64}[name]
                src = A["a_gate_b"][0].rearrange("(b t) e -> b t e", t=2)[:, :, g:g + 64]
            return [(0, src.shape[0], src)]
        K.rows = rows
        K.row_loads = sum(len(page) for page in PARAM_PAGES)

        def ada1(layer, first):
            return AdaSource(A["ada_w"][layer], first, (0,), pcol(f"ada_b{layer}", 72),
                             lambda v: K.mods[:, 72 * layer:72 * layer + 72])

        def ada2(layer, first):
            return AdaSource(A["ada_w_2"][layer], first, (1, 2), pcol("ada_b_2", 48)[:, 24 * layer:24 * layer + 24],
                             lambda v: K.mods2[:, v, 24 * layer:24 * layer + 24])
        K.ada_src = lambda layer, m: ada1(layer, 0)(m)

        W = K.weights = Weights()

        def columns(w):
            w = w.rearrange("(k p) c -> p k c", p=P)
            return lambda j: w[:, :, at(j * P, P)]

        def ffn_weights(layer, which, parts):
            up = columns(A["ffn_w13"][layer, which])
            down = A["ffn_w2"][layer, which].rearrange("(k p) c -> p k c", p=P)
            segs, t0 = [], 0
            for turns, ada in parts:
                segs.append((turns, [lambda i, t0=t0: up(i + t0), lambda i, t0=t0: up(i + (t0 + FB))], ada))
                t0 += turns
            segs.append((DB, [lambda n, a=a, b=b: down[:, a:b, at(n * P, P)]
                              for a, b in ((0, 8), (8, 16), (16, FB))], None))
            return segs

        def proj(w, first, n):
            w = columns(w)
            return (n, [lambda i: w(i + first)], None)

        ab = columns(A["ab_w_in"][0])
        W.add(*ffn_weights(0, 0, [(22, ada1(0, 10))]))
        W.add((4, [lambda i: ab(i + 8), lambda i: ab(i + 12)], None), proj(A["ab_w_in"][0], 4, 4),
              proj(A["ab_w_in"][0], 0, 4), proj(A["ab_w_out"][0], 0, DB))
        W.add(*ffn_weights(0, 1, [(4, ada1(0, 32)), (18, ada1(1, 0))]))
        W.add(*ffn_weights(1, 0, [(18, ada1(1, 18)), (4, ada2(0, 0))]))
        W.add(proj(A["c_w_in"][0], DB, DB), proj(A["c_w_in"][0], 0, DB), proj(A["c_w_out"][0], 0, DB))
        W.add(*ffn_weights(1, 1, [(8, ada2(0, 4)), (12, ada2(1, 0)), (2, None)]))
        first_even = len(W.phases)
        W.add(proj(A["ev_w_in_2"][0], 0, SHIFT_BLOCKS), proj(A["ev_w_in_2"][0], SHIFT_BLOCKS, EVEN_BLOCKS - SHIFT_BLOCKS))
        W.add(proj(A["ev_w_out_2"][0], 0, DB))
        odd = columns(A["od_w_in_2"][0])
        W.add((HEADS, [lambda i, j=j: odd(i + HEADS * j) for j in range(4)], None))
        W.add(proj(A["od_w_out_2"][0], 0, DB))

        K.ada_raw = None
        with ExitStack() as first:
            K.ada_raw = sbuf(first, "ada_raw", [P, ADA, DB, ADA_W])
            K.ada_acc = sbuf(first, "ada_acc", [P, 2, ADA_W])
            K.ada_dia = sbuf(first, "ada_dia", [P, 2, 2, P])
            K.ada_col = sbuf(first, "ada_col", [P, 2, 2])
            K.ada_ps = psum(first, "ada_sums", [P, 2, ADA_W])
            run = [lambda: start_phase(K), lambda: ffn_phase(K, 0, 0, 0, 0, carried=False), lambda: mixer_ab_phase(K, 1, 0, 1),
                   lambda: ffn_phase(K, 2, 0, 2, 1), lambda: ffn_phase(K, 3, 1, 0, 0),
                   lambda: mixer_c_phase(K, 4, 1, 1), lambda: ffn_phase(K, 5, 1, 2, 1, carry=False)]
            for f in run:
                f()
        second_block(K, ctx, first_even)
        output_phase(K)


NAMES = [
    "x", "c", "ada_w", "ada_b", "norm_pre", "norm_post", "ffn_w13", "ffn_w2", "ab_w_in", "a_conv_w", "a_conv_b",
    "a_gate_w", "a_gate_b", "a_lam", "b_conv_w", "b_conv_b", "b_norm_g", "b_norm_b", "ab_w_out", "c_w_in", "c_b_in",
    "c_norm_g", "c_norm_b", "c_w_s", "c_b_s", "c_w_out", "c_2", "ctx_2", "c_ctx_2", "ada_w_2", "ada_b_2",
    "norm_pre_2", "norm_post_2", "ev_w_in_2", "ev_mu_2", "ev_w0_2", "ev_w2_2", "ev_a0_2", "ev_a2_2", "ev_k_k_2",
    "ev_k_a_2", "ev_r_k_2", "ev_lnx_g_2", "ev_lnx_b_2", "ev_w_out_2", "od_w_in_2", "od_decay_logit_2", "od_w_out_2",
]


def kernel(**inputs):
    import concourse.bacc as bacc
    from concourse.bass_utils import run_bass_kernel_spmd

    nc = bacc.Bacc("TRN2", target_bir_lowering=False, num_devices=1)
    arrays, A = {}, {}
    for name, a in [*((n, inputs[n]) for n in NAMES), *constants().items()]:
        a = np.ascontiguousarray(a)
        arrays[f"in_{name}"] = a
        A[name] = nc.dram_tensor(f"in_{name}", a.shape, mybir.dt.from_np(a.dtype), kind="ExternalInput").ap()
    out = nc.dram_tensor("out_x", (1, SEQ, D), F32, kind="ExternalOutput").ap()
    build(nc, A, out)
    result = run_bass_kernel_spmd(nc, [arrays], core_ids=[0])
    return result.results[0]["out_x"]
```
